# Optimizing a Trainium2 kernel written in Bass

```python
import jax
import jax.numpy as jnp
from jax import lax
import numpy as np
import math
import jax, jax.numpy as jnp

D_MODEL = 1024
BATCH = 1
SEQ = 512
DEPTH = 1

N_META = 16
CHUNK = 128
PAD_FRONT = CHUNK - N_META
D_MIX = D_MODEL
RET_HEADS = 4
RET_DK = D_MIX // 2 // RET_HEADS
RET_DV = D_MIX // 2 // RET_HEADS
MLSTM_HEADS = 4
MLSTM_DH = D_MIX // 2 // MLSTM_HEADS
CONV_K = 5
N_EXPERTS = 16
EC_CAPACITY = 2
D_FF = 128 * ((8 * D_MODEL // 3 + 127) // 128)
ROPE_BASE = 10000.0
EPS = 1e-6
NEG = -1e30
RET_QK = RET_HEADS * RET_DK
RET_V = RET_HEADS * RET_DV
ML_W = MLSTM_HEADS * MLSTM_DH
N_GATES = 4 * MLSTM_HEADS
PROJ_SIZES = (RET_QK, RET_QK, RET_V, RET_V, ML_W, ML_W, ML_W, ML_W, N_GATES)
PROJ_COLS = sum(PROJ_SIZES)
SPLIT_AT = tuple(int(s) for s in np.cumsum(PROJ_SIZES)[:-1])


def _rmsnorm(x, g):
    xf = x.astype(jnp.float32)
    y = xf * lax.rsqrt(jnp.mean(xf * xf, axis=-1, keepdims=True) + EPS)
    return (y * g.astype(jnp.float32)).astype(x.dtype)

def _head_norm(y, g):
    mu = jnp.mean(y, axis=-1, keepdims=True)
    yc = y - mu
    var = jnp.mean(yc * yc, axis=-1, keepdims=True)
    out = (yc * lax.rsqrt(var + EPS)).reshape(y.shape[:2] + (-1,))
    return out * g.astype(jnp.float32)

def _rotary(x, pos):
    half = x.shape[-1] // 2
    inv = ROPE_BASE ** (-jnp.arange(half, dtype=jnp.float32) / half)
    ang = pos[:, None] * inv[None, :]
    cos = jnp.cos(ang)[None, :, None, :]
    sin = jnp.sin(ang)[None, :, None, :]
    x1, x2 = x[..., :half], x[..., half:]
    return jnp.concatenate([x1 * cos - x2 * sin, x2 * cos + x1 * sin], axis=-1)

def _pad_front(t, value=0.0):
    widths = [(0, 0)] * t.ndim
    widths[1] = (PAD_FRONT, 0)
    return jnp.pad(t, widths, constant_values=value)

def _flip(t):
    return jnp.flip(t, axis=1)

def _centred_conv(u, w, b):
    c = u.shape[-1]
    out = lax.conv_general_dilated(
        u, w.astype(u.dtype)[:, None, :], window_strides=(1,),
        padding=((CONV_K // 2, CONV_K // 2),),
        dimension_numbers=('NWC', 'WIO', 'NWC'), feature_group_count=c)
    return out + b.astype(u.dtype)

def _retention_dir(q, k, v, log_gamma):
    b_, t_, h_, dk = q.shape
    dv = v.shape[-1]
    nc = t_ // CHUNK
    q = q.reshape(b_, nc, CHUNK, h_, dk)
    k = k.reshape(b_, nc, CHUNK, h_, dk)
    v = v.reshape(b_, nc, CHUNK, h_, dv)
    idx = jnp.arange(CHUNK, dtype=jnp.float32)
    diff = idx[:, None] - idx[None, :]
    decay = jnp.where(diff >= 0, jnp.exp(log_gamma[:, None, None] * jnp.maximum(diff, 0.0)), 0.0)
    scores = jnp.einsum('bclhd,bcmhd->bchlm', q, k) * decay
    intra = jnp.einsum('bchlm,bcmhe->bclhe', scores, v)
    zeta = jnp.exp(log_gamma[:, None] * (CHUNK - 1.0 - idx)[None, :])
    upd = jnp.einsum('bclhd,bclhe,hl->bchde', k, v, zeta)
    g_chunk = jnp.exp(log_gamma * CHUNK)[:, None, None]

    def step(state, u_c):
        return g_chunk * state + u_c, state

    r0 = jnp.zeros((b_, h_, dk, dv), jnp.float32)
    _, r_prev = lax.scan(step, r0, jnp.moveaxis(upd, 1, 0))
    r_prev = jnp.moveaxis(r_prev, 0, 1)
    xi = jnp.exp(log_gamma[:, None] * (idx + 1.0)[None, :])
    cross = jnp.einsum('bclhd,bchde,hl->bclhe', q, r_prev, xi)
    return (intra + cross).reshape(b_, t_, h_, dv)

def _mlstm_dir(q, k, v, log_i, log_f):
    b_, t_, h_, d = q.shape
    nc = t_ // CHUNK
    q = q.reshape(b_, nc, CHUNK, h_, d)
    k = k.reshape(b_, nc, CHUNK, h_, d)
    v = v.reshape(b_, nc, CHUNK, h_, d)
    li = jnp.moveaxis(log_i.reshape(b_, nc, CHUNK, h_), 3, 2)
    lf = jnp.moveaxis(log_f.reshape(b_, nc, CHUNK, h_), 3, 2)
    bcum = jnp.cumsum(lf, axis=-1)
    b_last = bcum[..., -1]
    causal = jnp.tril(jnp.ones((CHUNK, CHUNK), dtype=bool))
    log_d = jnp.where(causal, bcum[..., :, None] - bcum[..., None, :] + li[..., None, :], NEG)
    log_u = b_last[..., None] - bcum + li
    a = jnp.max(log_u, axis=-1)
    w_u = jnp.exp(log_u - a[..., None])
    upd_c = jnp.einsum('bchl,bclhe,bclhd->bched', w_u, v, k)
    upd_n = jnp.einsum('bchl,bclhd->bchd', w_u, k)

    def step(carry, inp):
        c_st, n_st, m_st = carry
        uc, un, bl, ac = inp
        m_new = jnp.maximum(bl + m_st, ac)
        f = jnp.exp(bl + m_st - m_new)
        g = jnp.exp(ac - m_new)
        c_new = f[..., None, None] * c_st + g[..., None, None] * uc
        n_new = f[..., None] * n_st + g[..., None] * un
        return (c_new, n_new, m_new), (c_st, n_st, m_st)

    init = (jnp.zeros((b_, h_, d, d), jnp.float32),
            jnp.zeros((b_, h_, d), jnp.float32),
            jnp.zeros((b_, h_), jnp.float32))
    xs = (jnp.moveaxis(upd_c, 1, 0), jnp.moveaxis(upd_n, 1, 0),
          jnp.moveaxis(b_last, 1, 0), jnp.moveaxis(a, 1, 0))
    _, (c_prev, n_prev, m_prev) = lax.scan(step, init, xs)
    c_prev = jnp.moveaxis(c_prev, 0, 1)
    n_prev = jnp.moveaxis(n_prev, 0, 1)
    m_prev = jnp.moveaxis(m_prev, 0, 1)
    log_inter = bcum + m_prev[..., None]
    m_row = jnp.maximum(log_inter, jnp.max(log_d, axis=-1))
    s = jnp.einsum('bclhd,bcmhd->bchlm', q, k) * jnp.exp(log_d - m_row[..., None])
    w_inter = jnp.exp(log_inter - m_row)
    num = (jnp.einsum('bchlm,bcmhe->bclhe', s, v)
           + jnp.einsum('bclhd,bched,bchl->bclhe', q, c_prev, w_inter))
    den = jnp.sum(s, axis=-1) + jnp.einsum('bclhd,bchd,bchl->bchl', q, n_prev, w_inter)
    denom = jnp.maximum(jnp.abs(den), jnp.exp(-m_row))
    h = num / jnp.moveaxis(denom, 2, 3)[..., None]
    return h.reshape(b_, t_, h_, d)

def _token_mixer(h, norm_g, w_in, b_gates, conv_w, conv_b, ret_decay_logit,
                 ret_gn_g, mlstm_gn_g, w_out):
    b_, n_, _ = h.shape
    f32 = jnp.float32
    u = _rmsnorm(h, norm_g)
    proj = jnp.einsum('bnd,dk->bnk', u, w_in)
    rq, rk, rv, rg, mq, mk, mv, mo, gate_pre = jnp.split(proj, SPLIT_AT, axis=-1)

    pos = jnp.arange(n_, dtype=f32)
    rq = _rotary(rq.reshape(b_, n_, RET_HEADS, RET_DK).astype(f32), pos) * (RET_DK ** -0.5)
    rk = _rotary(rk.reshape(b_, n_, RET_HEADS, RET_DK).astype(f32), pos)
    rv = rv.reshape(b_, n_, RET_HEADS, RET_DV).astype(f32)
    rq, rk, rv = _pad_front(rq), _pad_front(rk), _pad_front(rv)
    log_gamma = jax.nn.log_sigmoid(ret_decay_logit.astype(f32))
    ret = (_retention_dir(rq, rk, rv, log_gamma[0])
           + _flip(_retention_dir(_flip(rq), _flip(rk), _flip(rv), log_gamma[1])))
    ret = ret[:, PAD_FRONT:]
    y_ret = _head_norm(ret, ret_gn_g) * jax.nn.silu(rg.astype(f32))

    qk = jax.nn.silu(_centred_conv(jnp.concatenate([mq, mk], axis=-1), conv_w, conv_b))
    mq, mk = jnp.split(qk, 2, axis=-1)
    mq = mq.reshape(b_, n_, MLSTM_HEADS, MLSTM_DH).astype(f32) * (MLSTM_DH ** -0.5)
    mk = mk.reshape(b_, n_, MLSTM_HEADS, MLSTM_DH).astype(f32)
    mv = mv.reshape(b_, n_, MLSTM_HEADS, MLSTM_DH).astype(f32)
    gts = gate_pre.astype(f32) + b_gates.astype(f32)
    log_i = gts[..., :2 * MLSTM_HEADS].reshape(b_, n_, 2, MLSTM_HEADS)
    log_f = jax.nn.log_sigmoid(gts[..., 2 * MLSTM_HEADS:]).reshape(b_, n_, 2, MLSTM_HEADS)
    mq, mk, mv = _pad_front(mq), _pad_front(mk), _pad_front(mv)
    log_i = _pad_front(log_i, NEG)
    log_f = _pad_front(log_f, 0.0)
    h_f = _mlstm_dir(mq, mk, mv, log_i[:, :, 0], log_f[:, :, 0])
    h_b = _flip(_mlstm_dir(_flip(mq), _flip(mk), _flip(mv),
                           _flip(log_i[:, :, 1]), _flip(log_f[:, :, 1])))
    hm = (h_f + h_b)[:, PAD_FRONT:]
    hm = jax.nn.sigmoid(mo.astype(f32)).reshape(b_, n_, MLSTM_HEADS, MLSTM_DH) * hm
    y_m = _head_norm(hm, mlstm_gn_g)

    y = jnp.concatenate([y_ret, y_m], axis=-1).astype(h.dtype)
    return jnp.einsum('bnk,kd->bnd', y, w_out)

def _expert_choice_ffn(h, norm_g, w_router, w_gate, w_up, w_down):
    b_, n_, _ = h.shape
    u = _rmsnorm(h, norm_g)
    aff = jax.nn.softmax(jnp.einsum('bnd,de->bne', u, w_router).astype(jnp.float32), axis=-1)
    cap = EC_CAPACITY * n_ // N_EXPERTS
    g, idx = lax.top_k(jnp.swapaxes(aff, 1, 2), cap)
    xs = jax.vmap(lambda ub, ib: ub[ib])(u, idx)
    hid = (jax.nn.silu(jnp.einsum('becd,edf->becf', xs, w_gate))
           * jnp.einsum('becd,edf->becf', xs, w_up))
    y = jnp.einsum('becf,efd->becd', hid, w_down) * g[..., None].astype(h.dtype)
    return jnp.zeros_like(h).at[jnp.arange(b_)[:, None, None], idx].add(y)

def first_inputs(seed: int = 0) -> dict:
    key = jax.random.key(seed)
    ks = jax.random.split(key, 17)
    f32 = jnp.float32
    nrm = jax.random.normal
    x = nrm(ks[0], (BATCH, SEQ, D_MODEL), f32)
    meta_tokens = nrm(ks[1], (N_META, D_MODEL), f32)
    mix_norm_g = 1.0 + 0.05 * nrm(ks[2], (DEPTH, D_MODEL), f32)
    w_in = nrm(ks[3], (DEPTH, D_MODEL, PROJ_COLS), f32) * (D_MODEL ** -0.5)
    f_bias = jnp.tile(jnp.linspace(3.0, 6.0, MLSTM_HEADS, dtype=f32), 2)
    base_gates = jnp.concatenate([jnp.zeros((2 * MLSTM_HEADS,), f32), f_bias])
    b_gates = base_gates[None, :] + 0.1 * nrm(ks[4], (DEPTH, N_GATES), f32)
    conv_w = nrm(ks[5], (DEPTH, CONV_K, 2 * ML_W), f32) * (CONV_K ** -0.5)
    conv_b = 0.01 * nrm(ks[6], (DEPTH, 2 * ML_W), f32)
    scales = 5.0 + jnp.arange(RET_HEADS, dtype=f32)
    gamma_logit = jnp.log(2.0 ** scales - 1.0)
    ret_decay_logit = gamma_logit[None, None, :] + 0.05 * nrm(ks[7], (DEPTH, 2, RET_HEADS), f32)
    ret_gn_g = 1.0 + 0.05 * nrm(ks[8], (DEPTH, RET_V), f32)
    mlstm_gn_g = 1.0 + 0.05 * nrm(ks[9], (DEPTH, ML_W), f32)
    w_out = nrm(ks[10], (DEPTH, D_MIX, D_MODEL), f32) * (D_MIX ** -0.5)
    ffn_norm_g = 1.0 + 0.05 * nrm(ks[11], (DEPTH, D_MODEL), f32)
    w_router = nrm(ks[12], (DEPTH, D_MODEL, N_EXPERTS), f32) * (D_MODEL ** -0.5)
    w_gate = nrm(ks[13], (DEPTH, N_EXPERTS, D_MODEL, D_FF), f32) * (D_MODEL ** -0.5)
    w_up = nrm(ks[14], (DEPTH, N_EXPERTS, D_MODEL, D_FF), f32) * (D_MODEL ** -0.5)
    w_down = nrm(ks[15], (DEPTH, N_EXPERTS, D_FF, D_MODEL), f32) * (D_FF ** -0.5)
    final_norm_g = 1.0 + 0.05 * nrm(ks[16], (D_MODEL,), f32)
    return {'x': x, 'meta_tokens': meta_tokens, 'mix_norm_g': mix_norm_g, 'w_in': w_in,
            'b_gates': b_gates, 'conv_w': conv_w, 'conv_b': conv_b,
            'ret_decay_logit': ret_decay_logit, 'ret_gn_g': ret_gn_g, 'mlstm_gn_g': mlstm_gn_g,
            'w_out': w_out, 'ffn_norm_g': ffn_norm_g, 'w_router': w_router, 'w_gate': w_gate,
            'w_up': w_up, 'w_down': w_down, 'final_norm_g': final_norm_g}

def first_block(x, meta_tokens, mix_norm_g, w_in, b_gates, conv_w, conv_b, ret_decay_logit,
              ret_gn_g, mlstm_gn_g, w_out, ffn_norm_g, w_router, w_gate, w_up, w_down,
              final_norm_g):
    b_ = x.shape[0]
    meta = jnp.broadcast_to(meta_tokens.astype(x.dtype)[None], (b_, N_META, x.shape[-1]))
    h = jnp.concatenate([meta, x], axis=1)
    for l in range(DEPTH):
        h = h + _token_mixer(h, mix_norm_g[l], w_in[l], b_gates[l], conv_w[l], conv_b[l],
                             ret_decay_logit[l], ret_gn_g[l], mlstm_gn_g[l], w_out[l])
        h = h + _expert_choice_ffn(h, ffn_norm_g[l], w_router[l], w_gate[l], w_up[l], w_down[l])
    h = _rmsnorm(h, final_norm_g)
    return h[:, N_META:]


N_MEM = 256

SSD_D_INNER = D_MODEL
SSD_HEAD_DIM = 64
SSD_HEADS = SSD_D_INNER // SSD_HEAD_DIM
SSD_GROUPS = 4
SSD_HEADS_PER_GROUP = SSD_HEADS // SSD_GROUPS
SSD_STATE = 128
SSD_CONV = 4
SSD_CHUNK = 128
SSD_CONV_DIM = SSD_D_INNER + 2 * SSD_GROUPS * SSD_STATE

DIL_PAIRS = ((128, 1), (512, 4), (2048, 16))
DIL_HEADS_PER_GROUP = 4
DIL_HEAD_DIM = 64
DIL_HEADS = len(DIL_PAIRS) * DIL_HEADS_PER_GROUP
DIL_WIDTH = DIL_HEADS * DIL_HEAD_DIM
DIL_OUT_WIDTH = DIL_HEADS_PER_GROUP * DIL_HEAD_DIM

MEM_HEADS = 4
MEM_HEAD_DIM = 192
MEM_WIDTH = MEM_HEADS * MEM_HEAD_DIM

ROPE_THETA = 500000.0
ROPE_FRACTION = 4

PEER_HEADS = 8
PEER_N_KEYS = 128
PEER_EXPERTS = PEER_N_KEYS * PEER_N_KEYS
PEER_QUERY_DIM = 256
PEER_TOPK = 16
PEER_BLOCK = 64

N_BRANCHES = 3

OFF_Z = 0
OFF_XBC = OFF_Z + SSD_D_INNER
OFF_DT = OFF_XBC + SSD_CONV_DIM
OFF_DQ = OFF_DT + SSD_HEADS
OFF_DK = OFF_DQ + DIL_WIDTH
OFF_DV = OFF_DK + DIL_WIDTH
OFF_MQ = OFF_DV + DIL_WIDTH
OFF_GATE = OFF_MQ + MEM_WIDTH
IN_PROJ_WIDTH = OFF_GATE + N_BRANCHES * D_MODEL


F32 = jnp.float32

def _rms_norm(t, w):
    tf = t.astype(F32)
    tf = tf * lax.rsqrt(jnp.mean(tf * tf, axis=-1, keepdims=True) + EPS)
    return (tf * w.astype(F32)).astype(t.dtype)

def _partial_rope(t, positions):
    hd = t.shape[-1]
    rot = hd // ROPE_FRACTION
    half = rot // 2
    inv = jnp.exp(-math.log(ROPE_THETA) * (2.0 / rot) * jnp.arange(half, dtype=F32))
    ang = positions.astype(F32)[..., None] * inv
    cos = jnp.cos(ang)[:, :, None, :]
    sin = jnp.sin(ang)[:, :, None, :]
    tf = t.astype(F32)
    t1 = tf[..., :half]
    t2 = tf[..., half:rot]
    out = jnp.concatenate([t1 * cos - t2 * sin, t2 * cos + t1 * sin, tf[..., rot:]], axis=-1)
    return out.astype(t.dtype)

def _causal_depthwise_conv(t, w, bias):
    c = t.shape[-1]
    y = lax.conv_general_dilated(
        t, w[:, None, :].astype(t.dtype), window_strides=(1,),
        padding=[(w.shape[0] - 1, 0)],
        dimension_numbers=('NWC', 'WIO', 'NWC'),
        feature_group_count=c)
    return y + bias.astype(t.dtype)

def _ssd_chunked(xh, dt, a, bmat, cmat):
    b, s, g, r, p = xh.shape
    n = bmat.shape[-1]
    nc = s // SSD_CHUNK
    x_dt = xh.astype(F32) * dt[..., None]
    da = dt * a

    def chunks(t):
        return jnp.moveaxis(t.reshape(b, nc, SSD_CHUNK, *t.shape[2:]), 1, 0)

    tril = jnp.tril(jnp.ones((SSD_CHUNK, SSD_CHUNK), dtype=bool))
    strict = jnp.tril(jnp.ones((SSD_CHUNK, SSD_CHUNK), dtype=bool), k=-1)

    def step(state, inp):
        xc, dac, bc, cc = inp
        dat = jnp.moveaxis(dac, 1, -1)
        acum = jnp.cumsum(dat, axis=-1)
        seg = jnp.cumsum(jnp.where(strict, dat[..., :, None], 0.0), axis=-2)
        lmat = jnp.exp(jnp.where(tril, seg, -jnp.inf))
        cb = jnp.einsum('bsgn,btgn->bgst', cc, bc)
        y_diag = jnp.einsum('bgst,bgrst,btgrp->bsgrp', cb, lmat, xc)
        y_off = jnp.einsum('bsgn,bgrpn,bgrs->bsgrp', cc, state, jnp.exp(acum))
        decay = jnp.exp(acum[..., -1:] - acum)
        new_state = (state * jnp.exp(acum[..., -1])[..., None, None]
                     + jnp.einsum('btgn,bgrt,btgrp->bgrpn', bc, decay, xc))
        return new_state, y_diag + y_off

    state0 = jnp.zeros((b, g, r, p, n), F32)
    _, ys = lax.scan(step, state0, (chunks(x_dt), chunks(da),
                                    chunks(bmat.astype(F32)), chunks(cmat.astype(F32))))
    return jnp.moveaxis(ys, 0, 1).reshape(b, s, g, r, p)

def _dilated_group_attention(q, k, v, dilation, n_back):
    b, s, h, hd = q.shape
    m = s // dilation
    blk = n_back
    nb = -(-m // blk)
    mp = nb * blk

    def to_sub(t):
        t = t.reshape(b, m, dilation, h, hd)
        t = jnp.pad(t, ((0, 0), (0, mp - m), (0, 0), (0, 0), (0, 0)))
        return t.reshape(b, nb, blk, dilation, h, hd)

    def with_prev(t):
        prev = jnp.pad(t[:, :-1], ((0, 0), (1, 0), (0, 0), (0, 0), (0, 0), (0, 0)))
        return jnp.concatenate([prev, t], axis=2)

    qs = to_sub(q)
    kk = with_prev(to_sub(k))
    vv = with_prev(to_sub(v))
    scores = jnp.einsum('bnqrhd,bnkrhd->bnrhqk', qs, kk).astype(F32) * (hd ** -0.5)
    qi = jnp.arange(blk)[:, None]
    ki = jnp.arange(2 * blk)[None, :]
    dist = qi + blk - ki
    band = (dist >= 0) & (dist <= n_back)
    valid = band[None] & ((jnp.arange(nb)[:, None, None] > 0) | (ki >= blk)[None])
    scores = jnp.where(valid[None, :, None, None], scores, -jnp.inf)
    lse = jax.nn.logsumexp(scores, axis=-1)
    probs = jnp.exp(scores - lse[..., None]).astype(v.dtype)
    out = jnp.einsum('bnrhqk,bnkrhd->bnqrhd', probs, vv)
    out = out.reshape(b, mp, dilation, h, hd)[:, :m].reshape(b, s, h, hd)
    lse = lse.transpose(0, 1, 4, 2, 3).reshape(b, mp, dilation, h)[:, :m].reshape(b, s, h)
    return out, lse

def _peer(hn, w_query, sub_keys, expert_down, expert_up):
    b, s, d = hn.shape
    q = (hn @ w_query).reshape(b, s, PEER_HEADS, 2, PEER_QUERY_DIM // 2)
    sc = jnp.einsum('bshcd,hckd->bshck', q, sub_keys).astype(F32)
    v1, i1 = lax.top_k(sc[..., 0, :], PEER_TOPK)
    v2, i2 = lax.top_k(sc[..., 1, :], PEER_TOPK)
    cand = (v1[..., :, None] + v2[..., None, :]).reshape(b, s, PEER_HEADS, PEER_TOPK * PEER_TOPK)
    cidx = (i1[..., :, None] * PEER_N_KEYS + i2[..., None, :]).reshape(b, s, PEER_HEADS, PEER_TOPK * PEER_TOPK)
    top, pos = lax.top_k(cand, PEER_TOPK)
    idx = jnp.take_along_axis(cidx, pos, axis=-1)
    gate = jax.nn.softmax(top, axis=-1)
    nblk = s // PEER_BLOCK

    def blockify(t):
        return jnp.moveaxis(t.reshape(b, nblk, PEER_BLOCK, *t.shape[2:]), 1, 0)

    def one_block(args):
        hb, ib, gb = args
        u = expert_down[ib]
        act = jax.nn.gelu(jnp.einsum('bld,blhkd->blhk', hb, u), approximate=False)
        coef = (gb * act.astype(F32)).astype(hb.dtype)
        vv = expert_up[ib]
        return jnp.einsum('blhk,blhkd->bld', coef, vv)

    out = lax.map(one_block, (blockify(hn), blockify(idx), blockify(gate)))
    return jnp.moveaxis(out, 0, 1).reshape(b, s, d)

def second_inputs(seed: int = 0) -> dict:
    key = jax.random.key(seed)
    ks = jax.random.split(key, 32)
    L = DEPTH

    def nrm(k, shape, scale):
        return jax.random.normal(k, shape, F32) * scale

    def gain(k, shape):
        return 1.0 + 0.05 * jax.random.normal(k, shape, F32)

    x = nrm(ks[0], (BATCH, SEQ, D_MODEL), 1.0)
    mem = nrm(ks[1], (BATCH, N_MEM, D_MODEL), 1.0)
    offset = jax.random.randint(ks[2], (BATCH, 1), 0, 4096, dtype=jnp.int32)
    positions = jnp.arange(SEQ, dtype=jnp.int32)[None, :] + offset
    norm_mix_w = gain(ks[3], (L, D_MODEL))
    w_in = nrm(ks[4], (L, D_MODEL, IN_PROJ_WIDTH), D_MODEL ** -0.5)
    ssd_conv_w = nrm(ks[5], (L, SSD_CONV, SSD_CONV_DIM), SSD_CONV ** -0.5)
    ssd_conv_b = nrm(ks[6], (L, SSD_CONV_DIM), 0.02)
    dt0 = jnp.exp(jax.random.uniform(ks[7], (L, SSD_HEADS), F32, math.log(1e-3), math.log(1e-1)))
    ssd_dt_bias = dt0 + jnp.log(-jnp.expm1(-dt0))
    ssd_a_log = jnp.log(jax.random.uniform(ks[8], (L, SSD_HEADS), F32, 1.0, 16.0))
    ssd_d = gain(ks[9], (L, SSD_HEADS))
    ssd_norm_w = gain(ks[10], (L, SSD_D_INNER))
    dil_q_norm_w = gain(ks[11], (L, DIL_HEAD_DIM))
    dil_k_norm_w = gain(ks[12], (L, DIL_HEAD_DIM))
    mem_norm_w = gain(ks[13], (L, D_MODEL))
    w_mem_kv = nrm(ks[14], (L, D_MODEL, 2 * MEM_WIDTH), D_MODEL ** -0.5)
    mem_q_norm_w = gain(ks[15], (L, MEM_HEAD_DIM))
    mem_k_norm_w = gain(ks[16], (L, MEM_HEAD_DIM))
    w_ssd_br = nrm(ks[17], (L, SSD_D_INNER, D_MODEL), SSD_D_INNER ** -0.5)
    w_dil_br = nrm(ks[18], (L, DIL_OUT_WIDTH, D_MODEL), DIL_OUT_WIDTH ** -0.5)
    w_mem_br = nrm(ks[19], (L, MEM_WIDTH, D_MODEL), MEM_WIDTH ** -0.5)
    w_out = nrm(ks[20], (L, D_MODEL, D_MODEL), D_MODEL ** -0.5)
    norm_ffn_w = gain(ks[21], (L, D_MODEL))
    peer_w_query = nrm(ks[22], (L, D_MODEL, PEER_HEADS * PEER_QUERY_DIM), D_MODEL ** -0.5)
    peer_sub_keys = nrm(ks[23], (L, PEER_HEADS, 2, PEER_N_KEYS, PEER_QUERY_DIM // 2),
                        (PEER_QUERY_DIM // 2) ** -0.5)
    peer_down = nrm(ks[24], (L, PEER_EXPERTS, D_MODEL), D_MODEL ** -0.5)
    peer_up = nrm(ks[25], (L, PEER_EXPERTS, D_MODEL), PEER_HEADS ** -0.5)
    return {
        'x': x, 'mem': mem, 'positions': positions,
        'norm_mix_w': norm_mix_w, 'w_in': w_in,
        'ssd_conv_w': ssd_conv_w, 'ssd_conv_b': ssd_conv_b, 'ssd_dt_bias': ssd_dt_bias,
        'ssd_a_log': ssd_a_log, 'ssd_d': ssd_d, 'ssd_norm_w': ssd_norm_w,
        'dil_q_norm_w': dil_q_norm_w, 'dil_k_norm_w': dil_k_norm_w,
        'mem_norm_w': mem_norm_w, 'w_mem_kv': w_mem_kv,
        'mem_q_norm_w': mem_q_norm_w, 'mem_k_norm_w': mem_k_norm_w,
        'w_ssd_br': w_ssd_br, 'w_dil_br': w_dil_br, 'w_mem_br': w_mem_br, 'w_out': w_out,
        'norm_ffn_w': norm_ffn_w, 'peer_w_query': peer_w_query, 'peer_sub_keys': peer_sub_keys,
        'peer_down': peer_down, 'peer_up': peer_up,
    }

def second_block(x, mem, positions, norm_mix_w, w_in, ssd_conv_w, ssd_conv_b, ssd_dt_bias,
              ssd_a_log, ssd_d, ssd_norm_w, dil_q_norm_w, dil_k_norm_w, mem_norm_w, w_mem_kv,
              mem_q_norm_w, mem_k_norm_w, w_ssd_br, w_dil_br, w_mem_br, w_out, norm_ffn_w,
              peer_w_query, peer_sub_keys, peer_down, peer_up):
    b, s, _ = x.shape
    n_mem = mem.shape[1]
    h = x
    for layer in range(DEPTH):
        u = _rms_norm(h, norm_mix_w[layer])
        proj = u @ w_in[layer]
        z = proj[..., OFF_Z:OFF_XBC]
        xbc = proj[..., OFF_XBC:OFF_DT]
        dt_raw = proj[..., OFF_DT:OFF_DQ]
        dq = proj[..., OFF_DQ:OFF_DK].reshape(b, s, DIL_HEADS, DIL_HEAD_DIM)
        dk = proj[..., OFF_DK:OFF_DV].reshape(b, s, DIL_HEADS, DIL_HEAD_DIM)
        dv = proj[..., OFF_DV:OFF_MQ].reshape(b, s, DIL_HEADS, DIL_HEAD_DIM)
        mq = proj[..., OFF_MQ:OFF_GATE].reshape(b, s, MEM_HEADS, MEM_HEAD_DIM)
        gates = jax.nn.sigmoid(proj[..., OFF_GATE:].astype(F32)).reshape(b, s, N_BRANCHES, D_MODEL)

        xbc = jax.nn.silu(_causal_depthwise_conv(xbc, ssd_conv_w[layer], ssd_conv_b[layer]))
        gn = SSD_GROUPS * SSD_STATE
        xs = xbc[..., :SSD_D_INNER].reshape(b, s, SSD_GROUPS, SSD_HEADS_PER_GROUP, SSD_HEAD_DIM)
        bm = xbc[..., SSD_D_INNER:SSD_D_INNER + gn].reshape(b, s, SSD_GROUPS, SSD_STATE)
        cm = xbc[..., SSD_D_INNER + gn:].reshape(b, s, SSD_GROUPS, SSD_STATE)
        dt = jax.nn.softplus(dt_raw.astype(F32) + ssd_dt_bias[layer].astype(F32))
        dt = dt.reshape(b, s, SSD_GROUPS, SSD_HEADS_PER_GROUP)
        a = -jnp.exp(ssd_a_log[layer].astype(F32)).reshape(SSD_GROUPS, SSD_HEADS_PER_GROUP)
        y = _ssd_chunked(xs, dt, a, bm, cm)
        y = y + ssd_d[layer].astype(F32).reshape(SSD_GROUPS, SSD_HEADS_PER_GROUP)[..., None] * xs.astype(F32)
        y = y.reshape(b, s, SSD_D_INNER) * jax.nn.silu(z.astype(F32))
        yg = y.reshape(b, s, SSD_GROUPS, SSD_D_INNER // SSD_GROUPS)
        yg = yg * lax.rsqrt(jnp.mean(yg * yg, axis=-1, keepdims=True) + EPS)
        y_ssd = (yg.reshape(b, s, SSD_D_INNER) * ssd_norm_w[layer].astype(F32)).astype(h.dtype)

        dq = _partial_rope(_rms_norm(dq, dil_q_norm_w[layer]), positions)
        dk = _partial_rope(_rms_norm(dk, dil_k_norm_w[layer]), positions)
        outs = []
        lses = []
        for gi, (window, dilation) in enumerate(DIL_PAIRS):
            sl = slice(gi * DIL_HEADS_PER_GROUP, (gi + 1) * DIL_HEADS_PER_GROUP)
            o, l = _dilated_group_attention(dq[:, :, sl], dk[:, :, sl], dv[:, :, sl],
                                            dilation, window // dilation)
            outs.append(o.astype(F32))
            lses.append(l)
        wts = jax.nn.softmax(jnp.stack(lses, axis=0), axis=0)
        y_dil = jnp.sum(wts[..., None] * jnp.stack(outs, axis=0), axis=0)
        y_dil = y_dil.reshape(b, s, DIL_OUT_WIDTH).astype(h.dtype)

        mkv = _rms_norm(mem, mem_norm_w[layer]) @ w_mem_kv[layer]
        mk = mkv[..., :MEM_WIDTH].reshape(b, n_mem, MEM_HEADS, MEM_HEAD_DIM)
        mv = mkv[..., MEM_WIDTH:].reshape(b, n_mem, MEM_HEADS, MEM_HEAD_DIM)
        mqn = _rms_norm(mq, mem_q_norm_w[layer])
        mk = _rms_norm(mk, mem_k_norm_w[layer])
        msc = jnp.einsum('bshd,bmhd->bhsm', mqn, mk).astype(F32) * (MEM_HEAD_DIM ** -0.5)
        mp = jax.nn.softmax(msc, axis=-1).astype(mv.dtype)
        y_mem = jnp.einsum('bhsm,bmhd->bshd', mp, mv).reshape(b, s, MEM_WIDTH)

        merged = (gates[:, :, 0] * (y_ssd @ w_ssd_br[layer]).astype(F32)
                  + gates[:, :, 1] * (y_dil @ w_dil_br[layer]).astype(F32)
                  + gates[:, :, 2] * (y_mem @ w_mem_br[layer]).astype(F32))
        h = h + merged.astype(h.dtype) @ w_out[layer]

        hn = _rms_norm(h, norm_ffn_w[layer])
        h = h + _peer(hn, peer_w_query[layer], peer_sub_keys[layer], peer_down[layer], peer_up[layer])
    return h


def setup_inputs(seed=0):
    out = dict(first_inputs(seed))
    for name, value in second_inputs(seed + 1).items():
        if name != "x":
            out[name + "_2"] = value
    return out


def reference(
    x, meta_tokens, mix_norm_g, w_in, b_gates, conv_w, conv_b, ret_decay_logit, ret_gn_g,
    mlstm_gn_g, w_out, ffn_norm_g, w_router, w_gate, w_up, w_down, final_norm_g, mem_2,
    positions_2, norm_mix_w_2, w_in_2, ssd_conv_w_2, ssd_conv_b_2, ssd_dt_bias_2, ssd_a_log_2,
    ssd_d_2, ssd_norm_w_2, dil_q_norm_w_2, dil_k_norm_w_2, mem_norm_w_2, w_mem_kv_2,
    mem_q_norm_w_2, mem_k_norm_w_2, w_ssd_br_2, w_dil_br_2, w_mem_br_2, w_out_2, norm_ffn_w_2,
    peer_w_query_2, peer_sub_keys_2, peer_down_2, peer_up_2,
):
    x = first_block(
        x, meta_tokens, mix_norm_g, w_in, b_gates, conv_w, conv_b, ret_decay_logit, ret_gn_g,
        mlstm_gn_g, w_out, ffn_norm_g, w_router, w_gate, w_up, w_down, final_norm_g,
    )
    return second_block(
        x, mem_2, positions_2, norm_mix_w_2, w_in_2, ssd_conv_w_2, ssd_conv_b_2, ssd_dt_bias_2,
        ssd_a_log_2, ssd_d_2, ssd_norm_w_2, dil_q_norm_w_2, dil_k_norm_w_2, mem_norm_w_2,
        w_mem_kv_2, mem_q_norm_w_2, mem_k_norm_w_2, w_ssd_br_2, w_dil_br_2, w_mem_br_2, w_out_2,
        norm_ffn_w_2, peer_w_query_2, peer_sub_keys_2, peer_down_2, peer_up_2,
    )


_drawn_inputs = setup_inputs


def setup_inputs(seed=0):
    import zlib

    import numpy as np

    out = dict(_drawn_inputs(seed))
    spreads = {}
    factors = {'conv_b': 3.337,
     'dil_q_norm_w_2': 6.268,
     'dil_k_norm_w_2': 6.015,
     'mem_norm_w_2': 5.351,
     'mem_q_norm_w_2': 7.268,
     'mem_k_norm_w_2': 5.875,
     'ssd_conv_b_2': 8.0,
     'ssd_d_2': 8.0,
     'ssd_norm_w_2': 5.457,
     'norm_ffn_w_2': 3.942}
    for name, (base, spread) in spreads.items():
        noise = np.random.default_rng([zlib.crc32(name.encode()), seed]).standard_normal(out[name].shape)
        drawn = base * np.exp(spread * noise) if base else spread * noise
        out[name] = jnp.asarray(drawn.astype(out[name].dtype))
    for name, factor in factors.items():
        out[name] = (out[name] * factor).astype(out[name].dtype)
    return out
```

```python
from contextlib import ExitStack, contextmanager

import concourse.bass as bass
from concourse import mybir

ALU = mybir.AluOpType
ACT = mybir.ActivationFunctionType
F32 = mybir.dt.float32
I32 = mybir.dt.int32
U32 = mybir.dt.uint32
AX_X = mybir.AxisListType.X

P = 128
D = 1024
KD = D // P
SEQ = 512
META = 16
TOK = SEQ + META
HALF = TOK // 2
EPS = 1e-6
NEG = -1e30
NT = SEQ // P

X_TILES = [(i, P, META + P * i) for i in range(NT)]
META_TILE = (NT, META, 0)
ALL_TILES = X_TILES + [META_TILE]
BY_POSITION = [META_TILE] + X_TILES

HEADS = 4
MIX = D // 2
N_GATES = 4 * HEADS
CONV_K = 5
REL_BASE = 400
REL_W = REL_BASE + TOK

EXPERTS = 16
CAP = 2 * TOK // EXPERTS
D_FF = 128 * ((8 * D // 3 + 127) // 128)
SLOTS = EXPERTS * CAP
TOP_ROUNDS = (CAP + 7) // 8

COLS_1 = {}
for _name, _count in (("mix_g", KD), ("ffn_g", KD), ("conv_w", KD * CONV_K), ("conv_b", KD), ("gate_b", 4)):
    COLS_1[_name] = (sum(c for _, c in COLS_1.values()), _count)
COLS_1_N = sum(c for _, c in COLS_1.values())


class Stage:

    def __init__(self, nc, name):
        self.nc, self.name, self.stack = nc, name, ExitStack()

    def __enter__(self):
        return self

    def __exit__(self, kind, *_):
        if kind is None:
            self.stack.close()

    def sb(self, name, shape, dt=F32, side="left"):
        return self.stack.enter_context(self.nc.sbuf_tensor(f"{self.name}_{name}", shape, dt, side=side))

    def ps(self, name, shape, dt=F32):
        return self.stack.enter_context(self.nc.psum_tensor(f"{self.name}_{name}", shape, dt))

    def sem(self, name):
        return self.nc.alloc_semaphore(f"{self.name}_{name}")


@contextmanager
def own_semaphores(nc):
    before = nc.snapshot_sems()
    yield
    nc.clear_and_free_semaphores(nc.allocated_since(before))
    nc.all_engine_barrier()


class InOrder:

    def __init__(self, eng, sem):
        self.eng, self.sem, self.n = eng, sem, 0

    def __call__(self, ins):
        self.n += 1
        ins.then_inc(self.sem, 1)
        self.eng.wait_ge(self.sem, self.n)


def load(nc, name, pairs):
    with Stage(nc, name) as st:
        landed = st.sem("landed")
        with nc.Block() as block:

            @block.sync
            def _(sp):
                for dst, src in pairs:
                    sp.dma_start(dst, src).then_inc(landed, 16)
                sp.wait_ge(landed, 16 * len(pairs))


def normalise(nc, name, x, tiles, gain_col, ident, xT, gain_row=None, kept=None):
    n_tiles = len(tiles)
    with Stage(nc, name) as st:
        ssq = st.sb("ssq", [P, n_tiles])
        inv = st.sb("inv", [P, n_tiles])
        rstd = st.sb("rstd", [P, n_tiles])
        squares = st.sb("squares", [P, 2, D])
        scaled = st.sb("scaled", [P, 2, D])
        turned = st.ps("turned", [P, 2, D])
        cleared, squared, inverted, rooted = (st.sem(s) for s in ("cleared", "squared", "inverted", "rooted"))
        scale_done, turn_done, evac_done = st.sem("scale_done"), st.sem("turn_done"), st.sem("evac_done")
        dve_order = st.sem("dve_order")

        def row(n):
            i, rows, _ = tiles[n]
            return kept[:rows, i, :] if kept is not None else scaled[:rows, n % 2, :]

        with nc.Block() as block:

            @block.scalar
            def _(act):
                act.wait_ge(cleared, 1)
                for n, (i, rows, _) in enumerate(tiles):
                    if n >= 2:
                        act.wait_ge(squared, n - 1)
                    act.activation(squares[:rows, n % 2, :], x[:rows, i, :], ACT.Square,
                                   accum_out=ssq[:rows, n:n + 1]).then_inc(squared, 1)
                act.wait_ge(inverted, 1)
                act.activation(rstd[:, :], inv[:, :], ACT.Sqrt).then_inc(rooted, 1)

            @block.vector
            def _(dve):
                order = InOrder(dve, dve_order)
                dve.memset(ssq[:, :], 1.0).then_inc(cleared, 1)
                dve.wait_ge(squared, n_tiles)
                order(dve.tensor_scalar(ssq[:, :], ssq[:, :], 1.0 / D, EPS, ALU.mult, ALU.add))
                dve.reciprocal(inv[:, :], ssq[:, :]).then_inc(inverted, 1)
                dve.wait_ge(rooted, 1)

                def scale(n):
                    i, rows, _ = tiles[n]
                    if n >= 2 and kept is None:
                        dve.wait_ge(turn_done, n - 1)
                    if kept is None:
                        dve.tensor_scalar(row(n), x[:rows, i, :], rstd[:rows, n:n + 1], None,
                                          ALU.mult).then_inc(scale_done, 1)
                    else:
                        dve.scalar_tensor_tensor(row(n), x[:rows, i, :], rstd[:rows, n:n + 1],
                                                 gain_row[:rows, :], ALU.mult, ALU.mult).then_inc(scale_done, 1)

                def evacuate(n):
                    _, rows, col = tiles[n]
                    dve.wait_ge(turn_done, n + 1)
                    src = turned[:, n % 2, :].rearrange("p (k c) -> p k c", k=KD)[:, :, 0:rows]
                    if kept is None:
                        gain = gain_col.unsqueeze(2).broadcast_to([P, KD, rows])
                        dve.tensor_tensor(xT[:, :, col:col + rows], src, gain, ALU.mult).then_inc(evac_done, 1)
                    else:
                        dve.tensor_copy(xT[:, :, col:col + rows], src).then_inc(evac_done, 1)

                scale(0)
                for n in range(n_tiles):
                    if n + 1 < n_tiles:
                        scale(n + 1)
                    if xT is not None:
                        evacuate(n)
                dve.wait_ge(scale_done, n_tiles)

            @block.tensor
            def _(pe):
                for n, (_, rows, _) in enumerate(tiles if xT is not None else []):
                    pe.wait_ge(scale_done, n + 1)
                    if n >= 2:
                        pe.wait_ge(evac_done, n - 1)
                    for k in range(KD):
                        last = pe.transpose(turned[:, n % 2, k * P:k * P + rows],
                                            row(n)[:, k * P:(k + 1) * P], ident[:rows, :rows])
                    last.then_inc(turn_done, 1)


class Job:

    def __init__(self, kind, offset, width, emit, eng, col=0, rows=P, parts=1, tokens=SEQ, after=None):
        self.kind, self.offset, self.width, self.emit, self.eng = kind, offset, width, emit, eng
        self.col, self.rows, self.parts, self.tokens, self.after = col, rows, parts, tokens, after


def token_jobs(tiles, width, emit, eng="act"):
    return [Job("token", 0, width, (lambda nc, ps, i=i, rows=rows: emit(nc, i, rows, ps)), eng, col=col, rows=rows)
            for i, rows, col in tiles]


def halves(ap):
    return ap.rearrange("p (a b) -> p a b", a=2)


def project(nc, name, chunks, wide=512, k_max=KD):
    slots = 4
    jobs = [(c, job) for c, (_, _, js) in enumerate(chunks) for job in js]
    place = []
    taken = {"act": 0, "dve": 0}
    for _, job in jobs:
        taken[job.eng] += 1
        place.append((job.eng, taken[job.eng]))
    with Stage(nc, name) as st:
        weights = st.sb("weights", [P, 2, k_max, wide])
        out = st.ps("out", [P, slots, 2 * 512])
        w_landed = [st.sem("w_landed0"), st.sem("w_landed1")]
        w_used, product_done = st.sem("w_used"), st.sem("product_done")
        taken_by = {"act": st.sem("taken_by_act"), "dve": st.sem("taken_by_dve")}

        def view(n, job):
            if job.kind == "token":
                return out[:job.rows, n % slots, 0:job.width]
            each = job.tokens // job.parts
            v = out[:job.width, n % slots, :].rearrange("p (a b) -> p a b", a=2)
            return v[:, 0:job.parts, 0:each] if job.parts > 1 else v[:, 0, 0:each]

        with nc.Block() as block:

            @block.sync
            def _(sp):
                for c, (w, _, _) in enumerate(chunks):
                    if c >= 2:
                        sp.wait_ge(w_used, c - 1)
                    kp, nk, cols = w.shape
                    sp.dma_start(weights[:kp, c % 2, 0:nk, 0:cols], w).then_inc(w_landed[c % 2], 16)

            @block.tensor
            def _(pe):
                last_of_chunk = {c: max(n for n, (cc, _) in enumerate(jobs) if cc == c) for c in range(len(chunks))}
                for n, (c, job) in enumerate(jobs):
                    w, source, _ = chunks[c]
                    kp, nk, _ = w.shape
                    pe.wait_ge(w_landed[c % 2], 16 * (c // 2 + 1))
                    if n >= slots:
                        eng, count = place[n - slots]
                        pe.wait_ge(taken_by[eng], count)
                    for a in range(job.parts):
                        each = job.tokens // job.parts
                        for k in range(nk):
                            if job.kind == "token":
                                last = pe.matmul(out[:job.rows, n % slots, 0:job.width],
                                                 source(k)[:, job.col:job.col + job.rows],
                                                 weights[:kp, c % 2, k, job.offset:job.offset + job.width],
                                                 start=(k == 0), stop=(k == nk - 1))
                            else:
                                last = pe.matmul(out[:job.width, n % slots, a * 512:a * 512 + each],
                                                 weights[:kp, c % 2, k, job.offset:job.offset + job.width],
                                                 source(k)[:, job.col + a * each:job.col + (a + 1) * each],
                                                 start=(k == 0), stop=(k == nk - 1))
                    last.then_inc(product_done, 1)
                    if n == last_of_chunk[c]:
                        pe.wait_ge(product_done, n + 1)
                        pe.sem_inc(w_used, 1)

            def take_out(engine, which):
                for n, (_, job) in enumerate(jobs):
                    if job.eng != which:
                        continue
                    engine.wait_ge(product_done, n + 1)
                    if job.after is not None:
                        eng, count = place[job.after]
                        engine.wait_ge(taken_by[eng], count)
                    job.emit(nc, view(n, job)).then_inc(taken_by[which], 1)

            @block.scalar
            def _(act):
                take_out(act, "act")

            @block.vector
            def _(dve):
                take_out(dve, "dve")


def head_norm(dve, order, act_sem, dve_sem, y, tiles, stats, moments, inv):
    for n, (i, rows, _) in enumerate(tiles):
        for h in range(HEADS):
            c = n * HEADS + h
            order(dve.bn_stats(stats[:rows, c, :], y[:rows, i, h * P:(h + 1) * P]))
            order(dve.bn_aggr(moments[:rows, c, :], stats[:rows, c, :]))
    order(dve.tensor_scalar(inv[:, :], moments[:, :, 1], EPS, None, ALU.add))
    dve.reciprocal(inv[:, :], inv[:, :]).then_inc(dve_sem, 1)
    dve.wait_ge(act_sem, 1)
    for n, (i, rows, _) in enumerate(tiles):
        for h in range(HEADS):
            c = n * HEADS + h
            last = dve.tensor_scalar(y[:rows, i, h * P:(h + 1) * P], y[:rows, i, h * P:(h + 1) * P],
                                     moments[:rows, c, 0:1], inv[:rows, c:c + 1], ALU.subtract, ALU.mult)
            order(last)


def retention(nc, io, rqk, rv, rg, y):
    scale = float(P) ** -0.5
    n_t = len(ALL_TILES)
    with Stage(nc, "ret") as st:
        cos = st.sb("cos", [P, TOK])
        sin = st.sb("sin", [P, TOK])
        swapped = st.sb("swapped", [P, HEADS, TOK])
        ahead = st.sb("ahead", [P, REL_W])
        behind = st.sb("behind", [P, REL_W])
        diag = st.sb("diag", [P, REL_W])
        arg = st.sb("arg", [P, REL_W])
        decay = st.sb("decay", [P, 2, REL_W])
        logit = st.sb("logit", [P, 8])
        lg = st.sb("lg", [P, 8])
        tmp8 = st.sb("tmp8", [P, 8])
        gn = st.sb("gn", [P, MIX])
        weighted = st.sb("weighted", [P, 2, n_t, TOK])
        stats = st.sb("stats", [P, n_t * HEADS, 6])
        moments = st.sb("moments", [P, n_t * HEADS, 2])
        inv = st.sb("inv", [P, n_t * HEADS])
        scores = st.ps("scores", [P, 2, 1024])
        mixed = st.ps("mixed", [P, 4, 512])
        landed, rot_half, rotated, abs_done, soft_done, arg_done = (
            st.sem(s) for s in ("landed", "rot_half", "rotated", "abs_done", "soft_done", "arg_done"))
        exp_done, decay_ready, scored, weighted_ready, mix_done, mix_out = (
            st.sem(s) for s in ("exp_done", "decay_ready", "scored", "weighted_ready", "mix_done", "mix_out"))
        var_ready, root_ready, dve_order, act_order = (
            st.sem(s) for s in ("var_ready", "root_ready", "dve_order", "act_order"))

        with nc.Block() as block:

            @block.sync
            def _(sp):
                for dst, src in ((cos[:, :], io["c_cos"]), (sin[:, :], io["c_sin"]), (ahead[:, :], io["c_ahead"]),
                                 (behind[:, :], io["c_behind"]), (diag[:, :], io["c_diag"]),
                                 (logit[:, :], io["decay_logit"].partition_broadcast(P)),
                                 (gn[:, :], io["ret_gn_row"].partition_broadcast(P))):
                    sp.dma_start(dst, src).then_inc(landed, 16)
                sp.wait_ge(landed, 7 * 16)

            @block.scalar
            def _(act):
                order = InOrder(act, act_order)
                for g in range(2):
                    if g:
                        act.wait_ge(rotated, 1)
                    order(act.copy(swapped[0:64, :, :], rqk[64:P, g * HEADS:(g + 1) * HEADS, :]))
                    act.copy(swapped[64:P, :, :], rqk[0:64, g * HEADS:(g + 1) * HEADS, :]).then_inc(rot_half, 1)
                act.wait_ge(abs_done, 1)
                order(act.activation(tmp8[:, :], tmp8[:, :], ACT.Exp, scale=-1.0))
                act.activation(tmp8[:, :], tmp8[:, :], ACT.Ln, bias=1.0).then_inc(soft_done, 1)
                for h in range(HEADS):
                    act.wait_ge(arg_done, h + 1)
                    act.activation(arg[:, :], arg[:, :], ACT.Exp).then_inc(exp_done, 1)
                    for n, (i, rows, _) in enumerate(ALL_TILES):
                        m = h * n_t + n
                        act.wait_ge(mix_done, m + 1)
                        act.copy(y[:rows, i, h * P:(h + 1) * P], mixed[:rows, m % 4, 0:P]).then_inc(mix_out, 1)
                act.wait_ge(var_ready, 1)
                act.activation(inv[:, :], inv[:, :], ACT.Sqrt).then_inc(root_ready, 1)

            @block.vector
            def _(dve):
                order = InOrder(dve, dve_order)
                order(dve.memset(moments[:, :, :], 1.0))
                dve.wait_ge(landed, 7 * 16)
                for g in range(2):
                    x = rqk[:, g * HEADS:(g + 1) * HEADS, :]
                    dve.wait_ge(rot_half, g + 1)
                    order(dve.tensor_tensor(x, x, cos[:, :].unsqueeze(1).broadcast_to([P, HEADS, TOK]), ALU.mult))
                    order(dve.tensor_tensor(swapped[:, :, :], swapped[:, :, :],
                                            sin[:, :].unsqueeze(1).broadcast_to([P, HEADS, TOK]), ALU.mult))
                    dve.tensor_tensor(x, x, swapped[:, :, :], ALU.add).then_inc(rotated, 1)
                dve.scalar_tensor_tensor(tmp8[:, :], logit[:, :], -1.0, logit[:, :], ALU.mult,
                                         ALU.max).then_inc(abs_done, 1)
                dve.wait_ge(soft_done, 1)
                order(dve.scalar_tensor_tensor(lg[:, :], logit[:, :], 0.0, tmp8[:, :], ALU.min, ALU.subtract))
                for h in range(HEADS):
                    order(dve.tensor_scalar(arg[:, :], ahead[:, :], lg[:, h:h + 1], None, ALU.mult))
                    dve.scalar_tensor_tensor(arg[:, :], behind[:, :], lg[:, HEADS + h:HEADS + h + 1], arg[:, :],
                                             ALU.mult, ALU.add).then_inc(arg_done, 1)
                    dve.wait_ge(exp_done, h + 1)
                    if h >= 1:
                        dve.wait_ge(weighted_ready, n_t * h)
                    dve.tensor_tensor(decay[:, h % 2, :], arg[:, :], diag[:, :], ALU.mult).then_inc(decay_ready, 1)
                    dve.wait_ge(decay_ready, h + 1)
                    for n, (_, rows, col) in enumerate(ALL_TILES):
                        m = h * n_t + n
                        dve.wait_ge(scored, m + 1)
                        if h >= 2:
                            dve.wait_ge(mix_done, n_t * (h - 1))
                        first = REL_BASE - col
                        dve.scalar_tensor_tensor(
                            halves(weighted[:rows, h % 2, n, :]),
                            scores[:rows, m % 2, :].rearrange("p (a b) -> p a b", a=2)[:, :, 0:HALF], scale,
                            halves(decay[:rows, h % 2, first:first + TOK]), ALU.mult, ALU.mult,
                        ).then_inc(weighted_ready, 1)
                dve.wait_ge(mix_out, n_t * HEADS)
                head_norm(dve, order, root_ready, var_ready, y, ALL_TILES, stats, moments, inv)
                for i, rows, _ in ALL_TILES:
                    order(dve.tensor_tensor(y[:rows, i, 0:MIX], y[:rows, i, 0:MIX], gn[:rows, :], ALU.mult))
                    order(dve.tensor_tensor(y[:rows, i, 0:MIX], y[:rows, i, 0:MIX], rg[:rows, i, :], ALU.mult))

            @block.tensor
            def _(pe):
                pe.wait_ge(rotated, 2)
                for h in range(HEADS):
                    for n, (_, rows, col) in enumerate(ALL_TILES):
                        m = h * n_t + n
                        if m >= 2:
                            pe.wait_ge(weighted_ready, m - 1)
                        for a in range(2):
                            last = pe.matmul(scores[:rows, m % 2, a * 512:a * 512 + HALF],
                                             rqk[:, HEADS + h, col:col + rows],
                                             rqk[:, h, a * HALF:(a + 1) * HALF], start=True, stop=True)
                        last.then_inc(scored, 1)
                    pe.wait_ge(weighted_ready, n_t * (h + 1))
                    for n, (_, rows, col) in enumerate(ALL_TILES):
                        m = h * n_t + n
                        if m >= 4:
                            pe.wait_ge(mix_out, m - 3)
                        for s, (si, srows, _) in enumerate(ALL_TILES):
                            last = pe.matmul(mixed[:rows, m % 4, 0:P], weighted[:srows, h % 2, s, col:col + rows],
                                             rv[:srows, si, h * P:(h + 1) * P],
                                             start=(s == 0), stop=(s == n_t - 1))
                        last.then_inc(mix_done, 1)


def mlstm_gates(nc, io, cols, gates, ident, g_col, exp_col, max_rows, scratch):
    with Stage(nc, "mlg") as st:
        ones = st.sb("ones", [HEADS, TOK])
        soft = st.sb("soft", [HEADS, 2, TOK])
        lf = st.sb("lf", [HEADS, 2, TOK])
        run = st.sb("run", [HEADS, 2, TOK])
        rows4 = st.sb("rows4", [HEADS, 4, TOK])
        top = st.sb("top", [HEADS, 2, TOK])
        turned = st.ps("turned", [P, len(ALL_TILES), 16])
        abs_done, soft_done, top_done, rows_done, turn_done, copied, stored, landed, dve_order, act_order = (
            st.sem(s) for s in ("abs_done", "soft_done", "top_done", "rows_done", "turn_done", "copied", "stored",
                                "landed", "dve_order", "act_order"))
        first = COLS_1["gate_b"][0]

        with nc.Block() as block:

            @block.vector
            def _(dve):
                order = InOrder(dve, dve_order)
                order(dve.memset(ones[:, :], 1.0))
                for g in range(4):
                    order(dve.tensor_scalar(gates[:, g, :], gates[:, g, :], cols[:HEADS, first + g:first + g + 1],
                                            None, ALU.add))
                forget = gates[:, 2:4, :]
                dve.scalar_tensor_tensor(soft[:, :, :], forget, -1.0, forget, ALU.mult,
                                         ALU.max).then_inc(abs_done, 1)
                dve.wait_ge(soft_done, 1)
                order(dve.scalar_tensor_tensor(lf[:, :, :], forget, 0.0, soft[:, :, :], ALU.min, ALU.subtract))
                for d in range(2):
                    def way(ap):
                        return ap if d == 0 else ap[:, ::-1]
                    order(dve.tensor_tensor_scan(way(run[:, d, :]), ones[:, :], way(lf[:, d, :]), 0.0,
                                                 ALU.mult, ALU.add))
                    order(dve.tensor_tensor(rows4[:, d, :], gates[:, d, :], run[:, d, :], ALU.subtract))
                    order(dve.tensor_tensor_scan(way(top[:, d, :]), ones[:, :], way(rows4[:, d, :]), 0.0,
                                                 ALU.mult, ALU.max))
                    order(dve.tensor_tensor(rows4[:, 2 + d, :], run[:, d, :], top[:, d, :], ALU.add))
                dve.sem_inc(rows_done, 1)
                dve.wait_ge(turn_done, 1)
                for i, rows, _ in ALL_TILES:
                    order(dve.tensor_copy(g_col[:rows, i, :], turned[:rows, i, 0:8]))
                dve.sem_inc(copied, 1)

            @block.scalar
            def _(act):
                order = InOrder(act, act_order)
                act.wait_ge(abs_done, 1)
                order(act.activation(soft[:, :, :], soft[:, :, :], ACT.Exp, scale=-1.0))
                act.activation(soft[:, :, :], soft[:, :, :], ACT.Ln, bias=1.0).then_inc(soft_done, 1)
                act.wait_ge(copied, 1)
                for i, rows, _ in ALL_TILES:
                    order(act.activation(exp_col[:rows, i, :], turned[:rows, i, 8:16], ACT.Exp, scale=-1.0))

            @block.tensor
            def _(pe):
                pe.wait_ge(rows_done, 1)
                for i, rows, col in ALL_TILES:
                    for g in range(4):
                        last = pe.transpose(turned[:rows, i, g * HEADS:(g + 1) * HEADS],
                                            rows4[:, g, col:col + rows], ident[:HEADS, :HEADS])
                last.then_inc(turn_done, 1)

            @block.sync
            def _(sp):
                sp.wait_ge(rows_done, 1)
                sp.dma_start(scratch, top[:, :, :]).then_inc(stored, 16)
                sp.wait_ge(stored, 16)
                for h in range(HEADS):
                    for d in range(2):
                        sp.dma_start(max_rows[:, 2 * h + d, :], scratch[h, d:d + 1, :].partition_broadcast(P)
                                     ).then_inc(landed, 16)
                sp.wait_ge(landed, 16 * 8)


def conv_silu(nc, name, padded, n_tiles, taps, tokens, weight, bias, out):
    with Stage(nc, name) as st:
        acc = st.sb("acc", [P, 2, tokens])
        conv_done, silu_done, dve_order = st.sem("conv_done"), st.sem("silu_done"), st.sem("dve_order")

        with nc.Block() as block:

            @block.vector
            def _(dve):
                order = InOrder(dve, dve_order)
                for c in range(n_tiles):
                    if c >= 2:
                        dve.wait_ge(silu_done, c - 1)
                    a = acc[:, c % 2, :]
                    order(dve.tensor_scalar(a, padded[:, c, 0:tokens], weight(c, 0), bias(c), ALU.mult, ALU.add))
                    for j in range(1, taps):
                        ins = dve.scalar_tensor_tensor(a, padded[:, c, j:j + tokens], weight(c, j), a,
                                                       ALU.mult, ALU.add)
                        if j < taps - 1:
                            order(ins)
                    ins.then_inc(conv_done, 1)

            @block.scalar
            def _(act):
                for c in range(n_tiles):
                    act.wait_ge(conv_done, c + 1)
                    act.activation(out[:, c, 0:tokens], acc[:, c % 2, :], ACT.Silu).then_inc(silu_done, 1)
                act.wait_ge(silu_done, n_tiles)


def clear(nc, name, aps, value=0.0):
    with Stage(nc, name) as st:
        done = st.sem("done")
        with nc.Block() as block:

            @block.vector
            def _(dve):
                for ap in aps:
                    dve.memset(ap, value).then_inc(done, 1)
                dve.wait_ge(done, len(aps))


def mlstm(nc, io, qk, v1, mo, y, g_col, exp_col, max_rows):
    scale = float(P) ** -0.5
    order_of = BY_POSITION
    n_t = len(order_of)
    passes = [(h, d) for h in range(HEADS) for d in range(2)]
    with Stage(nc, "mls") as st:
        raw = st.sb("raw", [P, n_t, TOK])
        arg = st.sb("arg", [P, 3, TOK])
        weight = st.sb("weight", [P, 2, n_t, TOK])
        keep = st.sb("keep", [P, 2, P])
        gn = st.sb("gn", [P, MIX])
        den = st.sb("den", [P, 4])
        stats = st.sb("stats", [P, n_t * HEADS, 6])
        moments = st.sb("moments", [P, n_t * HEADS, 2])
        inv = st.sb("inv", [P, n_t * HEADS])
        scores = st.ps("scores", [P, 2, 1024])
        mixed = st.ps("mixed", [P, 4, 512])
        landed, scored, raw_ready, arg_ready, exp_ready, weight_ready, mix_done, mix_out = (
            st.sem(s) for s in ("landed", "scored", "raw_ready", "arg_ready", "exp_ready", "weight_ready",
                                "mix_done", "mix_out"))
        var_ready, root_ready, dve_order, act_order = (
            st.sem(s) for s in ("var_ready", "root_ready", "dve_order", "act_order"))

        def span(d, col, rows):
            return (col, TOK) if d == 0 else (0, col + rows)

        with nc.Block() as block:

            @block.sync
            def _(sp):
                sp.dma_start(keep[:, :, :], io["c_keep"]).then_inc(landed, 16)
                sp.dma_start(gn[:, :], io["mlstm_gn_row"].partition_broadcast(P)).then_inc(landed, 16)
                sp.wait_ge(landed, 32)

            @block.scalar
            def _(act):
                for p, (h, d) in enumerate(passes):
                    if d == 0:
                        if h >= 1:
                            act.wait_ge(weight_ready, n_t * p)
                        for n, (_, rows, _) in enumerate(order_of):
                            act.wait_ge(scored, h * n_t + n + 1)
                            act.activation(halves(raw[:rows, n, :]),
                                           scores[:rows, (h * n_t + n) % 2, :].rearrange(
                                               "p (a b) -> p a b", a=2)[:, :, 0:HALF],
                                           ACT.Copy, scale=scale).then_inc(raw_ready, 1)
                    for n, (_, rows, col) in enumerate(order_of):
                        m = p * n_t + n
                        lo, hi = span(d, col, rows)
                        act.wait_ge(arg_ready, m + 1)
                        act.activation(arg[:rows, m % 3, lo:hi], arg[:rows, m % 3, lo:hi], ACT.Exp,
                                       scale=-1.0).then_inc(exp_ready, 1)
                act.wait_ge(var_ready, 1)
                act.activation(inv[:, :], inv[:, :], ACT.Sqrt).then_inc(root_ready, 1)

            @block.vector
            def _(dve):
                order = InOrder(dve, dve_order)
                order(dve.memset(moments[:, :, :], 1.0))
                dve.wait_ge(landed, 32)

                def exponents(p, n):
                    h, d = passes[p]
                    i, rows, col = order_of[n]
                    m = p * n_t + n
                    lo, hi = span(d, col, rows)
                    if m >= 3:
                        dve.wait_ge(weight_ready, m - 2)
                    dve.tensor_scalar(arg[:rows, m % 3, lo:hi], max_rows[:rows, 2 * h + d, lo:hi],
                                      g_col[:rows, i, d * HEADS + h:d * HEADS + h + 1], 0.0,
                                      ALU.subtract, ALU.max).then_inc(arg_ready, 1)

                def weigh(p, n):
                    h, d = passes[p]
                    _, rows, col = order_of[n]
                    m = p * n_t + n
                    lo, hi = span(d, col, rows)
                    dve.wait_ge(exp_ready, m + 1)
                    if p >= 2:
                        dve.wait_ge(mix_done, n_t * (p - 1))
                    if n == 0:
                        dve.wait_ge(raw_ready, n_t * (h + 1))
                    order(dve.tensor_tensor(weight[:rows, p % 2, n, lo:hi], arg[:rows, m % 3, lo:hi],
                                            raw[:rows, n, lo:hi], ALU.mult))
                    dve.tensor_tensor(weight[:rows, p % 2, n, col:col + rows],
                                      weight[:rows, p % 2, n, col:col + rows], keep[:rows, d, 0:rows],
                                      ALU.mult).then_inc(weight_ready, 1)

                def take_out(p):
                    h, d = passes[p]
                    for n, (i, rows, _) in enumerate(order_of):
                        m = p * n_t + n
                        dve.wait_ge(mix_done, m + 1)
                        ps = mixed[:rows, m % 4, :]
                        c = den[:rows, 0:1]
                        out = y[:rows, i, h * P:(h + 1) * P]
                        order(dve.tensor_scalar(den[:rows, 1:2], ps[:, P:P + 1], -1.0, None, ALU.mult))
                        order(dve.tensor_tensor(c, ps[:, P:P + 1], den[:rows, 1:2], ALU.max))
                        order(dve.tensor_tensor(c, c, exp_col[:rows, i, d * HEADS + h:d * HEADS + h + 1], ALU.max))
                        order(dve.reciprocal(c, c))
                        if d == 0:
                            ins = dve.tensor_scalar(out, ps[:, 0:P], c, None, ALU.mult)
                        else:
                            ins = dve.scalar_tensor_tensor(out, ps[:, 0:P], c, out, ALU.mult, ALU.add)
                        ins.then_inc(mix_out, 1)
                        dve.wait_ge(mix_out, m + 1)

                for p in range(len(passes)):
                    exponents(p, 0)
                    exponents(p, 1)
                    for n in range(n_t):
                        if n + 2 < n_t:
                            exponents(p, n + 2)
                        weigh(p, n)
                    if p >= 1:
                        take_out(p - 1)
                take_out(len(passes) - 1)
                for i, rows, _ in ALL_TILES:
                    order(dve.tensor_tensor(y[:rows, i, :], y[:rows, i, :], mo[:rows, i, :], ALU.mult))
                head_norm(dve, order, root_ready, var_ready, y, ALL_TILES, stats, moments, inv)
                for i, rows, _ in ALL_TILES:
                    order(dve.tensor_tensor(y[:rows, i, :], y[:rows, i, :], gn[:rows, :], ALU.mult))

            @block.tensor
            def _(pe):
                def score(h):
                    for n, (_, rows, col) in enumerate(order_of):
                        m = h * n_t + n
                        if m >= 2:
                            pe.wait_ge(raw_ready, m - 1)
                        for a in range(2):
                            last = pe.matmul(scores[:rows, m % 2, a * 512:a * 512 + HALF],
                                             qk[:, HEADS + h, col:col + rows],
                                             qk[:, h, a * HALF:(a + 1) * HALF], start=True, stop=True)
                        last.then_inc(scored, 1)

                def mix(p):
                    h, d = passes[p]
                    pe.wait_ge(weight_ready, n_t * (p + 1))
                    for n, (_, rows, col) in enumerate(order_of):
                        m = p * n_t + n
                        if m >= 4:
                            pe.wait_ge(mix_out, m - 3)
                        keys = range(0, n + 1) if d == 0 else range(n, n_t)
                        for s in keys:
                            si, srows, _ = order_of[s]
                            last = pe.matmul(mixed[:rows, m % 4, 0:P + 1],
                                             weight[:srows, p % 2, s, col:col + rows], v1[:srows, si, h, :],
                                             start=(s == keys[0]), stop=(s == keys[-1]))
                        last.then_inc(mix_done, 1)

                score(0)
                for h in range(HEADS):
                    mix(2 * h)
                    if h + 1 < HEADS:
                        score(h + 1)
                    mix(2 * h + 1)


def turn_rows(nc, name, x, tiles, ident, xT, k_tiles=KD):
    with Stage(nc, name) as st:
        turned = st.ps("turned", [P, 2, D])
        turn_done, taken = st.sem("turn_done"), st.sem("taken")
        with nc.Block() as block:

            @block.tensor
            def _(pe):
                for n, (i, rows, _) in enumerate(tiles):
                    if n >= 2:
                        pe.wait_ge(taken, n - 1)
                    for k in range(k_tiles):
                        last = pe.transpose(turned[:, n % 2, k * P:k * P + rows], x[:rows, i, k * P:(k + 1) * P],
                                            ident[:rows, :rows])
                    last.then_inc(turn_done, 1)

            @block.vector
            def _(dve):
                for n, (_, rows, col) in enumerate(tiles):
                    dve.wait_ge(turn_done, n + 1)
                    dve.tensor_copy(xT[:, :, col:col + rows],
                                    turned[:, n % 2, 0:k_tiles * P].rearrange("p (k c) -> p k c", k=k_tiles)[:, :, 0:rows]
                                    ).then_inc(taken, 1)


def route(nc, io, u, uT, ident, xsT, slot_tok, slot_gate, scratch):
    n_t = len(ALL_TILES)
    third = SLOTS // 3
    with Stage(nc, "route") as st:
        w = st.sb("w", [P, KD, EXPERTS])
        logits = st.sb("logits", [P, n_t, EXPERTS])
        top1 = st.sb("top1", [P, n_t])
        total = st.sb("total", [P, n_t])
        affT = st.sb("affT", [EXPERTS, TOK])
        vals = st.sb("vals", [EXPERTS, TOP_ROUNDS * 8])
        idx = st.sb("idx", [EXPERTS, TOP_ROUNDS * 8], U32)
        idx_f = st.sb("idx_f", [EXPERTS, TOP_ROUNDS * 8])
        idx_all = st.sb("idx_all", [P, SLOTS])
        token_id = st.sb("token_id", [P, n_t])
        onehot = st.sb("onehot", [P, n_t, SLOTS])
        small = st.ps("small", [P, 512])
        turned = st.ps("turned", [P, 1024])
        gathered = st.ps("gathered", [P, 4, 512])
        landed, logits_done, shifted, exp_done, aff_done, turn_done, idx_done, stored, spread = (
            st.sem(s) for s in ("landed", "logits_done", "shifted", "exp_done", "aff_done", "turn_done", "idx_done",
                                "stored", "spread"))
        slot_turned, onehot_done, gather_done, act_taken, dve_taken, dve_order, act_order = (
            st.sem(s) for s in ("slot_turned", "onehot_done", "gather_done", "act_taken", "dve_taken", "dve_order",
                                "act_order"))
        pieces = [(k, c) for k in range(KD) for c in range(3)]

        with nc.Block() as block:

            @block.sync
            def _(sp):
                sp.dma_start(w[:, :, :], io["w_router"][0].rearrange("(k p) e -> p k e", p=P)).then_inc(landed, 16)
                sp.dma_start(token_id[:, :], io["c_token_id"]).then_inc(landed, 16)
                sp.wait_ge(idx_done, 1)
                sp.dma_start(scratch, idx_f[:, 0:CAP]).then_inc(stored, 16)
                sp.wait_ge(stored, 16)
                sp.dma_start(idx_all[:, :], scratch.rearrange("e c -> (e c)").unsqueeze(0).partition_broadcast(P)
                             ).then_inc(spread, 16)
                sp.wait_ge(spread, 16)
                sp.wait_ge(landed, 32)

            @block.tensor
            def _(pe):
                pe.wait_ge(landed, 32)
                for n, (i, rows, col) in enumerate(ALL_TILES):
                    for k in range(KD):
                        last = pe.matmul(small[:rows, i * EXPERTS:(i + 1) * EXPERTS], uT[:, k, col:col + rows],
                                         w[:, k, :], start=(k == 0), stop=(k == KD - 1))
                last.then_inc(logits_done, 1)
                pe.wait_ge(aff_done, 1)
                for i, rows, col in ALL_TILES:
                    at = 512 if i == NT else i * P
                    last = pe.transpose(turned[:EXPERTS, at:at + rows], logits[:rows, i, :], ident[:rows, :rows])
                last.then_inc(turn_done, 1)
                pe.wait_ge(idx_done, 1)
                pe.transpose(small[:CAP, 128:128 + EXPERTS], idx_f[:, 0:CAP], ident[:EXPERTS, :EXPERTS])
                pe.transpose(small[:CAP, 160:160 + EXPERTS], vals[:, 0:CAP],
                             ident[:EXPERTS, :EXPERTS]).then_inc(slot_turned, 1)
                pe.wait_ge(onehot_done, 1)
                for m, (k, c) in enumerate(pieces):
                    if m >= 4:
                        pe.wait_ge(act_taken if m % 2 == 0 else dve_taken, m // 2 - 1)
                    for i, rows, _ in ALL_TILES:
                        last = pe.matmul(gathered[:, m % 4, 0:third], u[:rows, i, k * P:(k + 1) * P],
                                         onehot[:rows, i, c * third:(c + 1) * third],
                                         start=(i == 0), stop=(i == NT))
                    last.then_inc(gather_done, 1)

            @block.vector
            def _(dve):
                order = InOrder(dve, dve_order)
                order(dve.memset(logits[:, :, :], 0.0))
                dve.wait_ge(logits_done, 1)
                for i, rows, _ in ALL_TILES:
                    order(dve.tensor_copy(logits[:rows, i, :], small[:rows, i * EXPERTS:(i + 1) * EXPERTS]))
                order(dve.tensor_reduce(top1[:, :], logits[:, :, :], AX_X, ALU.max))
                dve.tensor_tensor(logits[:, :, :], logits[:, :, :],
                                  top1[:, :].unsqueeze(2).broadcast_to([P, n_t, EXPERTS]),
                                  ALU.subtract).then_inc(shifted, 1)
                dve.wait_ge(exp_done, 1)
                order(dve.tensor_reduce(total[:, :], logits[:, :, :], AX_X, ALU.add))
                order(dve.reciprocal(total[:, :], total[:, :]))
                dve.tensor_tensor(logits[:, :, :], logits[:, :, :],
                                  total[:, :].unsqueeze(2).broadcast_to([P, n_t, EXPERTS]),
                                  ALU.mult).then_inc(aff_done, 1)
                dve.wait_ge(turn_done, 1)
                order(dve.tensor_copy(affT[:, META:TOK], turned[:EXPERTS, 0:SEQ]))
                order(dve.tensor_copy(affT[:, 0:META], turned[:EXPERTS, 512:512 + META]))
                for r in range(TOP_ROUNDS):
                    eight = slice(8 * r, 8 * r + 8)
                    order(dve.max(vals[:, eight], affT[:, :]))
                    order(dve.max_index(idx[:, eight], vals[:, eight], affT[:, :]))
                    if r + 1 < TOP_ROUNDS:
                        order(dve.match_replace(affT[:, :], vals[:, eight], affT[:, :], -1.0))
                dve.tensor_copy(idx_f[:, :], idx[:, :]).then_inc(idx_done, 1)
                dve.wait_ge(slot_turned, 1)
                order(dve.tensor_copy(slot_tok[:, :], small[:CAP, 128:128 + EXPERTS]))
                order(dve.tensor_copy(slot_gate[:, :], small[:CAP, 160:160 + EXPERTS]))
                dve.wait_ge(spread, 16)
                for i, rows, _ in ALL_TILES:
                    order(dve.tensor_scalar(onehot[:rows, i, :], idx_all[:rows, :], token_id[:rows, i:i + 1], None,
                                            ALU.is_equal))
                dve.sem_inc(onehot_done, 1)
                for m, (k, c) in enumerate(pieces):
                    if m % 2:
                        dve.wait_ge(gather_done, m + 1)
                        dve.tensor_copy(xsT[:, k, c * third:(c + 1) * third],
                                        gathered[:, m % 4, 0:third]).then_inc(dve_taken, 1)

            @block.scalar
            def _(act):
                order = InOrder(act, act_order)
                act.wait_ge(shifted, 1)
                act.activation(logits[:, :, :], logits[:, :, :], ACT.Exp).then_inc(exp_done, 1)
                for m, (k, c) in enumerate(pieces):
                    if m % 2 == 0:
                        act.wait_ge(gather_done, m + 1)
                        act.copy(xsT[:, k, c * third:(c + 1) * third], gathered[:, m % 4, 0:third]
                                 ).then_inc(act_taken, 1)


FF_CHUNK = 512
FF_TILES = D_FF // P
FF_PER = FF_CHUNK // P
FF_CHUNKS = [(c, min(FF_CHUNK, D_FF - c)) for c in range(0, D_FF, FF_CHUNK)]


def expert_ffn(nc, io, xsT, ident, y_dram):
    nch = len(FF_CHUNKS)
    assert nch % 2 == 0
    w_gate = io["w_gate"][0].rearrange("e (k p) f -> e p k f", p=P)
    w_up = io["w_up"][0].rearrange("e (k p) f -> e p k f", p=P)
    w_down = io["w_down"][0].rearrange("e (t p) d -> e p t d", p=P)
    with Stage(nc, "ffn") as st:
        gate_w = st.sb("gate_w", [P, 2, KD, FF_CHUNK])
        up_w = st.sb("up_w", [P, 2, KD, FF_CHUNK])
        down_w = st.sb("down_w", [P, 2, FF_PER, D])
        xe = st.sb("xe", [P, KD, CAP])
        silu = st.sb("silu", [CAP, 2, FF_CHUNK])
        hidden = st.sb("hidden", [CAP, 2, FF_CHUNK])
        hiddenT = st.sb("hiddenT", [P, 2, FF_PER, CAP])
        result = st.sb("result", [CAP, D])
        gate_p = st.ps("gate_p", [P, 2, 512])
        up_p = st.ps("up_p", [P, 2, 512])
        turn_p = st.ps("turn_p", [P, 2, 512])
        down_p = st.ps("down_p", [P, D])
        gate_in = [st.sem("gate_in0"), st.sem("gate_in1")]
        up_in = [st.sem("up_in0"), st.sem("up_in1")]
        down_in = [st.sem("down_in0"), st.sem("down_in1")]
        gu_w_free, down_w_free, xe_free, x_in = (st.sem(s) for s in ("gu_w_free", "down_w_free", "xe_free", "x_in"))
        gu_done, silu_done, hidden_done, turn_done, turn_out, down_done, result_out, y_stored, result_free = (
            st.sem(s) for s in ("gu_done", "silu_done", "hidden_done", "turn_done", "turn_out", "down_done",
                                "result_out", "y_stored", "result_free"))

        with nc.Block() as block:

            @block.sync
            def _(sp):
                with sp.Fori(0, EXPERTS) as e:
                    for c, (first, width) in enumerate(FF_CHUNKS):
                        s = c % 2
                        sp.wait_ge(gu_w_free, e * nch + c + 1)
                        sp.dma_start(gate_w[:, s, :, 0:width],
                                     w_gate[bass.ds(e, 1), :, :, first:first + width].squeeze(0)
                                     ).then_inc(gate_in[s], 16)
                        sp.dma_start(up_w[:, s, :, 0:width],
                                     w_up[bass.ds(e, 1), :, :, first:first + width].squeeze(0)
                                     ).then_inc(up_in[s], 16)

            @block.gpsimd
            def _(pool):
                pool.sem_inc(result_free, 1)

                def columns_of(e):
                    pool.wait_ge(xe_free, e + 1)
                    pool.tensor_copy(xe[:, :, :], xsT[:, :, bass.ds(e * CAP, CAP)]).then_inc(x_in, 1)

                def down_weights(e, c):
                    first, width = FF_CHUNKS[c]
                    pool.wait_ge(down_w_free, e * nch + c + 1)
                    pool.dma_start(down_w[:, c % 2, 0:width // P, :],
                                   w_down[bass.ds(e, 1), :, first // P:(first + width) // P, :].squeeze(0)
                                   ).then_inc(down_in[c % 2], 16)

                def store(e):
                    pool.wait_ge(result_out, 2 * e + 4)
                    pool.dma_start(y_dram[bass.ds(e, 1), :, :].squeeze(0), result[:, :]).then_inc(y_stored, 16)

                def stored(e):
                    pool.wait_ge(y_stored, e * 16 + 16)
                    pool.sem_inc(result_free, 1)

                columns_of(0)
                for c in range(nch):
                    down_weights(0, c)
                with pool.Fori(1, EXPERTS) as e:
                    columns_of(e)
                    down_weights(e, 0)
                    store(e - 1)
                    down_weights(e, 1)
                    stored(e - 1)
                    for c in range(2, nch):
                        down_weights(e, c)
                store(EXPERTS - 1)
                stored(EXPERTS - 1)

            @block.tensor
            def _(pe):
                pe.sem_inc(gu_w_free, 2)
                pe.sem_inc(down_w_free, 2)
                pe.sem_inc(xe_free, 1)
                pe.sem_inc(turn_done, 2)
                pe.sem_inc(result_out, 2)
                with pe.Fori(0, EXPERTS) as e:
                    def gate_up(c):
                        _, width = FF_CHUNKS[c]
                        s = c % 2
                        turns = e * (nch // 2) + c // 2 + 1
                        pe.wait_ge(gate_in[s], turns * 16)
                        pe.wait_ge(hidden_done, e * nch + c + 1)
                        for k in range(KD):
                            pe.matmul(gate_p[:CAP, s, 0:width], xe[:, k, :], gate_w[:, s, k, 0:width],
                                      start=(k == 0), stop=(k == KD - 1))
                        pe.wait_ge(up_in[s], turns * 16)
                        for k in range(KD):
                            last = pe.matmul(up_p[:CAP, s, 0:width], xe[:, k, :], up_w[:, s, k, 0:width],
                                             start=(k == 0), stop=(k == KD - 1))
                        last.then_inc(gu_done, 1)

                    def turn(c):
                        _, width = FF_CHUNKS[c]
                        s = c % 2
                        pe.wait_ge(hidden_done, e * nch + c + 3)
                        pe.wait_ge(turn_out, e * nch + c + 1)
                        for t in range(width // P):
                            last = pe.transpose(turn_p[:, s, t * CAP:(t + 1) * CAP],
                                                hidden[:, s, t * P:(t + 1) * P], ident[:CAP, :CAP])
                        last.then_inc(turn_done, 1)

                    def down(c):
                        first, width = FF_CHUNKS[c]
                        s = c % 2
                        if c == 0:
                            pe.wait_ge(result_out, 2 * e + 2)
                        pe.wait_ge(down_in[s], (e * (nch // 2) + c // 2 + 1) * 16)
                        pe.wait_ge(turn_out, e * nch + c + 3)
                        for t in range(width // P):
                            for half in range(2):
                                last = pe.matmul(down_p[:CAP, half * 512:(half + 1) * 512], hiddenT[:, s, t, :],
                                                 down_w[:, s, t, half * 512:(half + 1) * 512],
                                                 start=(c == 0 and t == 0),
                                                 stop=(c == nch - 1 and t == width // P - 1))
                        last.then_inc(down_done, 1)
                        pe.wait_ge(down_done, e * nch + c + 1)
                        pe.sem_inc(down_w_free, 1)

                    def gate_up_over(c):
                        pe.wait_ge(gu_done, e * nch + c + 1)
                        pe.sem_inc(gu_w_free, 1)

                    pe.wait_ge(x_in, e + 1)
                    for c in range(nch):
                        gate_up(c)
                        gate_up_over(c)
                        if c >= 1:
                            turn(c - 1)
                        if c >= 2:
                            down(c - 2)
                    pe.sem_inc(xe_free, 1)
                    turn(nch - 1)
                    down(nch - 2)
                    down(nch - 1)

            @block.scalar
            def _(act):
                act.sem_inc(turn_out, 2)
                with act.Fori(0, EXPERTS) as e:
                    def out_of_turn(c):
                        _, width = FF_CHUNKS[c]
                        s, tiles = c % 2, width // P
                        act.wait_ge(turn_done, e * nch + c + 3)
                        act.wait_ge(down_w_free, e * nch + c + 1)
                        act.copy(hiddenT[:, s, 0:tiles, :],
                                 turn_p[:, s, 0:tiles * CAP].rearrange("p (t c) -> p t c", c=CAP)
                                 ).then_inc(turn_out, 1)

                    for c, (_, width) in enumerate(FF_CHUNKS):
                        s = c % 2
                        act.wait_ge(gu_done, e * nch + c + 1)
                        act.wait_ge(hidden_done, e * nch + c + 1)
                        act.activation(silu[:, s, 0:width], gate_p[:CAP, s, 0:width], ACT.Silu
                                       ).then_inc(silu_done, 1)
                        if c >= 1:
                            out_of_turn(c - 1)
                    out_of_turn(nch - 1)
                    act.wait_ge(down_done, e * nch + nch)
                    act.wait_ge(result_free, e + 1)
                    act.copy(result[:, 0:512], down_p[:CAP, 0:512]).then_inc(result_out, 1)

            @block.vector
            def _(dve):
                dve.sem_inc(hidden_done, 2)
                with dve.Fori(0, EXPERTS) as e:
                    for c, (_, width) in enumerate(FF_CHUNKS):
                        s = c % 2
                        dve.wait_ge(silu_done, e * nch + c + 1)
                        dve.wait_ge(turn_done, e * nch + c + 1)
                        dve.tensor_tensor(hidden[:, s, 0:width], silu[:, s, 0:width], up_p[:CAP, s, 0:width],
                                          ALU.mult).then_inc(hidden_done, 1)
                    dve.wait_ge(down_done, e * nch + nch)
                    dve.wait_ge(result_free, e + 1)
                    dve.tensor_copy(result[:, 512:D], down_p[:CAP, 512:D]).then_inc(result_out, 1)


def combine(nc, io, h, slot_tok, slot_gate, y_dram):
    with Stage(nc, "comb") as st:
        y = st.sb("y", [CAP, EXPERTS, D])
        scatter = st.sb("scatter", [CAP, EXPERTS, SEQ])
        ids = st.sb("ids", [CAP, SEQ])
        out = st.ps("out", [P, 2, D])
        landed, ids_in, scatter_done, sum_done, added, dve_order = (
            st.sem(s) for s in ("landed", "ids_in", "scatter_done", "sum_done", "added", "dve_order"))
        with nc.Block() as block:

            @block.sync
            def _(sp):
                sp.dma_start(ids[:, :], io["c_ids"].partition_broadcast(CAP)).then_inc(ids_in, 16)
                sp.dma_start(y[:, :, :], y_dram.rearrange("e c d -> c e d")).then_inc(landed, 16)

            @block.vector
            def _(dve):
                order = InOrder(dve, dve_order)
                dve.wait_ge(ids_in, 16)
                for e in range(EXPERTS):
                    dve.tensor_scalar(scatter[:, e, :], ids[:, :], slot_tok[:, e:e + 1], slot_gate[:, e:e + 1],
                                      ALU.is_equal, ALU.mult).then_inc(scatter_done, 1)
                for i in range(NT):
                    dve.wait_ge(sum_done, i + 1)
                    dve.tensor_tensor(h[:, i, :], h[:, i, :], out[:, i % 2, :], ALU.add).then_inc(added, 1)

            @block.tensor
            def _(pe):
                pe.wait_ge(landed, 16)
                pe.wait_ge(scatter_done, EXPERTS)
                for i in range(NT):
                    if i >= 2:
                        pe.wait_ge(added, i - 1)
                    for half in range(2):
                        for e in range(EXPERTS):
                            last = pe.matmul(out[:, i % 2, half * 512:(half + 1) * 512],
                                             scatter[:, e, i * P:(i + 1) * P],
                                             y[:, e, half * 512:(half + 1) * 512],
                                             start=(e == 0), stop=(e == EXPERTS - 1))
                    last.then_inc(sum_done, 1)


def first_block(nc, io, h, ident, dbg=None):
    w_in = io["w_in"][0].rearrange("(k p) c -> p k c", p=P)
    w_out = io["w_out"][0].rearrange("(k p) c -> p k c", p=P)
    max_dram = nc.dram_tensor("scratch_max", [HEADS, 2, TOK], F32).ap()
    idx_dram = nc.dram_tensor("scratch_idx", [EXPERTS, CAP], F32).ap()
    y_dram = nc.dram_tensor("scratch_y", [EXPERTS, CAP, D], F32).ap()

    with Stage(nc, "b1") as st:
        cols = st.sb("cols", [P, COLS_1_N])
        load(nc, "load1", [(cols[:, :], io["p_cols_1"]), (ident[:, :], io["c_ident"]),
                           (h[:, 0:NT, :], io["x"][0].rearrange("(i p) d -> p i d", p=P)),
                           (h[0:META, NT, :], io["meta_tokens"])])

        def gain(name):
            a, n = COLS_1[name]
            return cols[:, a:a + n]

        with Stage(nc, "mix") as mx:
            y = mx.sb("y", [P, NT + 1, D])
            with Stage(nc, "mixin") as s1:
                uT = s1.sb("uT", [P, KD, TOK], side="right")
                normalise(nc, "norm1", h, ALL_TILES, gain("mix_g"), ident, uT)

                def source(k):
                    return uT[:, k, :]

                def chunk(index, jobs):
                    return (w_in[:, :, index * 512:(index + 1) * 512], source, jobs)

                def channel_jobs(dst, base, pad=0):
                    return [Job("channel", c * P, P,
                                (lambda nc, ps, c=c, eng=eng: (nc.scalar.copy if eng == "act" else nc.vector.tensor_copy)(
                                    halves(dst[:, base + c, pad:pad + TOK]), ps)),
                                eng, parts=2, tokens=TOK) for c, eng in enumerate(("act", "dve") * 2)]

                with Stage(nc, "retbuf") as s2:
                    rqk = s2.sb("rqk", [P, 2 * HEADS, TOK])
                    rv = s2.sb("rv", [P, NT + 1, MIX])
                    rg = s2.sb("rg", [P, NT + 1, MIX])
                    project(nc, "proj_ret", [
                        chunk(0, channel_jobs(rqk, 0)), chunk(1, channel_jobs(rqk, HEADS)),
                        chunk(2, token_jobs(ALL_TILES, MIX, lambda nc, i, r, ps: nc.vector.tensor_copy(
                            rv[:r, i, :], ps), "dve")),
                        chunk(3, token_jobs(ALL_TILES, MIX, lambda nc, i, r, ps: nc.scalar.activation(
                            rg[:r, i, :], ps, ACT.Silu))),
                    ])
                    retention(nc, io, rqk, rv, rg, y)
                    if dbg: dbg("yret", y[:, :, 0:MIX])

                qk = mx.sb("qk", [P, 2 * HEADS, TOK])
                v1 = mx.sb("v1", [P, NT + 1, HEADS, P + 1])
                mo = mx.sb("mo", [P, NT + 1, MIX])
                gates = mx.sb("gates", [HEADS, 4, TOK])
                with Stage(nc, "convbuf") as s2:
                    padded = s2.sb("padded", [P, KD, TOK + CONV_K - 1])
                    gate_jobs = [Job("channel", g * HEADS, HEADS,
                                     (lambda nc, ps, g=g: nc.vector.tensor_copy(halves(gates[:, g, :]), ps)),
                                     "dve", parts=2, tokens=TOK) for g in range(4)]
                    project(nc, "proj_ml", [
                        chunk(4, channel_jobs(padded, 0, 2)), chunk(5, channel_jobs(padded, HEADS, 2)),
                        chunk(6, token_jobs(ALL_TILES, MIX, lambda nc, i, r, ps: nc.vector.tensor_copy(
                            v1[:r, i, :, 0:P], ps.rearrange("p (h e) -> p h e", h=HEADS)), "dve")),
                        chunk(7, token_jobs(ALL_TILES, MIX, lambda nc, i, r, ps: nc.scalar.activation(
                            mo[:r, i, :], ps, ACT.Sigmoid))),
                        (w_in[:, :, 8 * 512:8 * 512 + N_GATES], source, gate_jobs),
                    ])
                    clear(nc, "clear_ml", [padded[:, :, 0:2], padded[:, :, TOK + 2:TOK + 4]])
                    w0, b0 = COLS_1["conv_w"][0], COLS_1["conv_b"][0]
                    conv_silu(nc, "mlc", padded, KD, CONV_K, TOK,
                              lambda c, j: cols[:, w0 + c * CONV_K + j:w0 + c * CONV_K + j + 1],
                              lambda c: cols[:, b0 + c:b0 + c + 1], qk)
            with Stage(nc, "mlbuf") as s2:
                g_col = s2.sb("g_col", [P, NT + 1, 2 * HEADS])
                exp_col = s2.sb("exp_col", [P, NT + 1, 2 * HEADS])
                max_rows = s2.sb("max_rows", [P, 2 * HEADS, TOK])
                mlstm_gates(nc, io, cols, gates, ident, g_col, exp_col, max_rows, max_dram)
                clear(nc, "ones_ml", [v1[:, :, :, P:P + 1]], 1.0)
                mlstm(nc, io, qk, v1, mo, y[:, :, MIX:D], g_col, exp_col, max_rows)
            if dbg: dbg("y", y[:, :, :])
            with Stage(nc, "mixout") as s2:
                yT = s2.sb("yT", [P, KD, TOK])
                turn_rows(nc, "turn_y", y, ALL_TILES, ident, yT)
                project(nc, "proj_out", [
                    (w_out[:, :, n * 512:(n + 1) * 512], lambda k: yT[:, k, :],
                     token_jobs(ALL_TILES, 512, lambda nc, i, r, ps, n=n: nc.vector.tensor_tensor(
                         h[:r, i, n * 512:(n + 1) * 512], h[:r, i, n * 512:(n + 1) * 512], ps, ALU.add), "dve"))
                    for n in range(2)])
        if dbg: dbg("hmix", h[:, :, :])

        slot_tok = st.sb("slot_tok", [CAP, EXPERTS])
        slot_gate = st.sb("slot_gate", [CAP, EXPERTS])
        with Stage(nc, "moe") as s1:
            xsT = s1.sb("xsT", [P, KD, SLOTS])
            with Stage(nc, "routebuf") as s2:
                u = s2.sb("u", [P, NT + 1, D])
                uT = s2.sb("uT", [P, KD, TOK])
                gain_row = s2.sb("gain_row", [P, D])
                load(nc, "load_g", [(gain_row[:, :], io["ffn_g_row"].partition_broadcast(P))])
                normalise(nc, "norm2", h, ALL_TILES, None, ident, uT, gain_row=gain_row, kept=u)
                route(nc, io, u, uT, ident, xsT, slot_tok, slot_gate, idx_dram)
            expert_ffn(nc, io, xsT, ident, y_dram)
        combine(nc, io, h, slot_tok, slot_gate, y_dram)


N_MEM = 256
SSD_HEADS = 16
SSD_HD = D // SSD_HEADS
SSD_GROUPS = 4
SSD_RATIO = SSD_HEADS // SSD_GROUPS
SSD_CONV = 4
XBC = D + 2 * SSD_GROUPS * P
XBC_TILES = XBC // P
DIL = ((128, 1), (512, 4), (2048, 16))
DIL_J = 4
DIL_HD = 64
DIL_HEADS = len(DIL) * DIL_J
DIL_W = DIL_HEADS * DIL_HD
MEM_HD = 192
MEM_W = HEADS * MEM_HD
ROT = DIL_HD // 4
ROT_HALF = ROT // 2
OFF_XBC = D
OFF_DT = OFF_XBC + XBC
OFF_DQ = OFF_DT + SSD_HEADS
OFF_MQ = OFF_DQ + 3 * DIL_W
OFF_GATE = OFF_MQ + MEM_W
BRANCHES = 3

PEER_HEADS = 8
PEER_KEYS = 128
PEER_TOP = 16
PEER_SLOTS = PEER_HEADS * PEER_TOP

SEQ_TILES = [(i, P, P * i) for i in range(NT)]

COLS_2 = {}
for _name, _count in (("mix_g", KD), ("mem_g", KD), ("conv_w", XBC_TILES * SSD_CONV), ("conv_b", XBC_TILES),
                      ("dt_bias", 1), ("a_log", 1)):
    COLS_2[_name] = (sum(c for _, c in COLS_2.values()), _count)
COLS_2_N = sum(c for _, c in COLS_2.values())


def rms_groups(nc, name, xs, groups, width, gain):
    n = len(xs)
    with Stage(nc, name) as st:
        squares = st.sb("squares", [P, 2, groups * width])
        ssq = st.sb("ssq", [P, n, groups])
        squared, summed, inverted, rooted, dve_order = (
            st.sem(s) for s in ("squared", "summed", "inverted", "rooted", "dve_order"))

        def grouped(ap):
            return ap.rearrange("p (g w) -> p g w", g=groups)

        with nc.Block() as block:

            @block.scalar
            def _(act):
                for i in range(n):
                    if i >= 2:
                        act.wait_ge(summed, i - 1)
                    act.activation(squares[:, i % 2, :], xs[i], ACT.Square).then_inc(squared, 1)
                act.wait_ge(inverted, 1)
                act.activation(ssq[:, :, :], ssq[:, :, :], ACT.Sqrt).then_inc(rooted, 1)

            @block.vector
            def _(dve):
                order = InOrder(dve, dve_order)
                for i in range(n):
                    dve.wait_ge(squared, i + 1)
                    dve.tensor_reduce(ssq[:, i, :], grouped(squares[:, i % 2, :]), AX_X, ALU.add
                                      ).then_inc(summed, 1)
                dve.wait_ge(summed, n)
                order(dve.tensor_scalar(ssq[:, :, :], ssq[:, :, :], 1.0 / width, EPS, ALU.mult, ALU.add))
                dve.reciprocal(ssq[:, :, :], ssq[:, :, :]).then_inc(inverted, 1)
                dve.wait_ge(rooted, 1)
                for i in range(n):
                    x = grouped(xs[i])
                    order(dve.tensor_tensor(x, x, ssq[:, i, :].unsqueeze(2).broadcast_to([P, groups, width]),
                                            ALU.mult))
                    g = (gain.unsqueeze(1).broadcast_to([P, groups, width]) if gain.shape[1] == width
                         else grouped(gain))
                    order(dve.tensor_tensor(x, x, g, ALU.mult))


def ssd_prepare(nc, io, cols, dt_raw, xbc, ident, acum_rows, acum_col, xs, x_dt, scratch):
    with Stage(nc, "ssp") as st:
        dt = st.sb("dt", [SSD_HEADS, SEQ])
        soft = st.sb("soft", [SSD_HEADS, SEQ])
        acum = st.sb("acum", [SSD_HEADS, SEQ])
        ones = st.sb("ones", [SSD_HEADS, SEQ])
        a = st.sb("a", [SSD_HEADS, 1])
        dt_col = st.sb("dt_col", [P, NT, SSD_HEADS])
        small = st.ps("small", [P, NT, 2, SSD_HEADS])
        turned = st.ps("turned", [P, 2, D])
        abs_done, soft_done, a_done, rows_done, cols_turned, x_turned, x_out, stored, landed, dve_order, act_order = (
            st.sem(s) for s in ("abs_done", "soft_done", "a_done", "rows_done", "cols_turned", "x_turned", "x_out",
                                "stored", "landed", "dve_order", "act_order"))
        bias, a_log = COLS_2["dt_bias"][0], COLS_2["a_log"][0]

        with nc.Block() as block:

            @block.vector
            def _(dve):
                order = InOrder(dve, dve_order)
                order(dve.memset(ones[:, :], 1.0))
                order(dve.tensor_scalar(dt_raw[:, :], dt_raw[:, :], cols[:SSD_HEADS, bias:bias + 1], None, ALU.add))
                dve.scalar_tensor_tensor(soft[:, :], dt_raw[:, :], -1.0, dt_raw[:, :], ALU.mult,
                                         ALU.max).then_inc(abs_done, 1)
                dve.wait_ge(soft_done, 1)
                order(dve.scalar_tensor_tensor(dt[:, :], dt_raw[:, :], 0.0, soft[:, :], ALU.max, ALU.add))
                dve.wait_ge(a_done, 1)
                order(dve.tensor_scalar(soft[:, :], dt[:, :], a[:, :], -1.0, ALU.mult, ALU.mult))
                dve.tensor_tensor_scan(acum[:, :], ones[:, :], soft[:, :], 0.0, ALU.mult, ALU.add
                                       ).then_inc(rows_done, 1)
                dve.wait_ge(cols_turned, 1)
                order(dve.tensor_copy(acum_col[:, :, :], small[:, :, 0, :]))
                order(dve.tensor_copy(dt_col[:, :, :], small[:, :, 1, :]))
                for i in range(NT):
                    dve.wait_ge(x_turned, i + 1)
                    order(dve.tensor_copy(xs[:, i, :], turned[:, i % 2, :]))
                    dve.sem_inc(x_out, 1)
                    order(dve.tensor_tensor(
                        x_dt[:, i, :].rearrange("p (h e) -> p h e", h=SSD_HEADS),
                        xs[:, i, :].rearrange("p (h e) -> p h e", h=SSD_HEADS),
                        dt_col[:, i, :].unsqueeze(2).broadcast_to([P, SSD_HEADS, SSD_HD]), ALU.mult))

            @block.scalar
            def _(act):
                order = InOrder(act, act_order)
                act.activation(a[:, :], cols[:SSD_HEADS, a_log:a_log + 1], ACT.Exp).then_inc(a_done, 1)
                act.wait_ge(abs_done, 1)
                order(act.activation(soft[:, :], soft[:, :], ACT.Exp, scale=-1.0))
                act.activation(soft[:, :], soft[:, :], ACT.Ln, bias=1.0).then_inc(soft_done, 1)

            @block.tensor
            def _(pe):
                def turn_x(i):
                    if i >= 2:
                        pe.wait_ge(x_out, i - 1)
                    for k in range(KD):
                        last = pe.transpose(turned[:, i % 2, k * P:(k + 1) * P], xbc[:, k, i * P:(i + 1) * P],
                                            ident[:, :])
                    last.then_inc(x_turned, 1)

                turn_x(0)
                turn_x(1)
                pe.wait_ge(rows_done, 1)
                for i in range(NT):
                    pe.transpose(small[:, i, 0, :], acum[:, i * P:(i + 1) * P], ident[:SSD_HEADS, :SSD_HEADS])
                    last = pe.transpose(small[:, i, 1, :], dt[:, i * P:(i + 1) * P], ident[:SSD_HEADS, :SSD_HEADS])
                last.then_inc(cols_turned, 1)
                turn_x(2)
                turn_x(3)

            @block.sync
            def _(sp):
                sp.wait_ge(rows_done, 1)
                sp.dma_start(scratch, acum[:, :]).then_inc(stored, 16)
                sp.wait_ge(stored, 16)
                for hd in range(SSD_HEADS):
                    sp.dma_start(acum_rows[:, hd, :], scratch[hd:hd + 1, :].partition_broadcast(P)
                                 ).then_inc(landed, 16)
                sp.wait_ge(landed, 16 * SSD_HEADS)


def ssd(nc, io, xbc, acum_rows, acum_col, x_dt, z, y):
    with Stage(nc, "ssd") as st:
        raw = st.sb("raw", [P, NT, SEQ])
        arg = st.sb("arg", [P, 3, SEQ])
        weight = st.sb("weight", [P, 2, NT, SEQ])
        keep = st.sb("keep", [P, 2, P])
        skip = st.sb("skip", [P, SSD_HEADS])
        scores = st.ps("scores", [P, 2, 512])
        mixed = st.ps("mixed", [P, 4, 512])
        landed, scored, raw_ready, arg_ready, exp_ready, weight_ready, mix_done, mix_out, dve_order = (
            st.sem(s) for s in ("landed", "scored", "raw_ready", "arg_ready", "exp_ready", "weight_ready",
                                "mix_done", "mix_out", "dve_order"))

        with nc.Block() as block:

            @block.sync
            def _(sp):
                sp.dma_start(keep[:, :, :], io["c_keep"]).then_inc(landed, 16)
                sp.dma_start(skip[:, :], io["ssd_d_row"].partition_broadcast(P)).then_inc(landed, 16)
                sp.wait_ge(landed, 32)

            @block.scalar
            def _(act):
                for p in range(SSD_HEADS):
                    g = p // SSD_RATIO
                    if p % SSD_RATIO == 0:
                        if p:
                            act.wait_ge(weight_ready, NT * p)
                        for n in range(NT):
                            act.wait_ge(scored, g * NT + n + 1)
                            act.copy(raw[:, n, n * P:], scores[:, (g * NT + n) % 2, n * P:]).then_inc(raw_ready, 1)
                    for n in range(NT):
                        m = p * NT + n
                        act.wait_ge(arg_ready, m + 1)
                        act.activation(arg[:, m % 3, n * P:], arg[:, m % 3, n * P:], ACT.Exp
                                       ).then_inc(exp_ready, 1)

            @block.vector
            def _(dve):
                order = InOrder(dve, dve_order)
                dve.wait_ge(landed, 32)

                def exponents(p, n):
                    m = p * NT + n
                    if m >= 3:
                        dve.wait_ge(weight_ready, m - 2)
                    dve.tensor_scalar(arg[:, m % 3, n * P:], acum_rows[:, p, n * P:], acum_col[:, n, p:p + 1], 0.0,
                                      ALU.subtract, ALU.min).then_inc(arg_ready, 1)

                def weigh(p, n):
                    m = p * NT + n
                    dve.wait_ge(exp_ready, m + 1)
                    if p >= 2:
                        dve.wait_ge(mix_done, NT * (p - 1))
                    dve.tensor_tensor(weight[:, p % 2, n, n * P:], arg[:, m % 3, n * P:], raw[:, n, n * P:],
                                      ALU.mult).then_inc(weight_ready, 1)

                def take_out(p):
                    part = slice(p * SSD_HD, (p + 1) * SSD_HD)
                    for i in range(NT):
                        m = p * NT + i
                        dve.wait_ge(mix_done, m + 1)
                        dve.scalar_tensor_tensor(y[:, i, part], y[:, i, part], skip[:, p:p + 1],
                                                 mixed[:, m % 4, 0:SSD_HD], ALU.mult, ALU.add).then_inc(mix_out, 1)

                for p in range(SSD_HEADS):
                    exponents(p, 0)
                    exponents(p, 1)
                    if p % SSD_RATIO == 0:
                        dve.wait_ge(raw_ready, NT * (p // SSD_RATIO + 1))
                        for n in range(NT):
                            order(dve.tensor_tensor(raw[:, n, n * P:(n + 1) * P], raw[:, n, n * P:(n + 1) * P],
                                                    keep[:, 0, :], ALU.mult))
                    for n in range(NT):
                        if n + 2 < NT:
                            exponents(p, n + 2)
                        weigh(p, n)
                    if p:
                        take_out(p - 1)
                take_out(SSD_HEADS - 1)
                dve.wait_ge(mix_out, NT * SSD_HEADS)
                for i in range(NT):
                    order(dve.tensor_tensor(y[:, i, :], y[:, i, :], z[:, i, :], ALU.mult))

            @block.tensor
            def _(pe):
                def score(g):
                    for n in range(NT):
                        m = g * NT + n
                        if m >= 2:
                            pe.wait_ge(raw_ready, m - 1)
                        pe.matmul(scores[:, m % 2, n * P:], xbc[:, KD + g, n * P:(n + 1) * P],
                                  xbc[:, KD + SSD_GROUPS + g, n * P:SEQ], start=True, stop=True
                                  ).then_inc(scored, 1)

                def mix(p):
                    pe.wait_ge(weight_ready, NT * (p + 1))
                    for i in range(NT):
                        m = p * NT + i
                        if m >= 4:
                            pe.wait_ge(mix_out, m - 3)
                        for n in range(i + 1):
                            last = pe.matmul(mixed[:, m % 4, 0:SSD_HD], weight[:, p % 2, n, i * P:(i + 1) * P],
                                             x_dt[:, n, p * SSD_HD:(p + 1) * SSD_HD], start=(n == 0), stop=(n == i))
                        last.then_inc(mix_done, 1)

                score(0)
                for p in range(SSD_HEADS):
                    if p % SSD_RATIO == SSD_RATIO - 1 and p + 1 < SSD_HEADS:
                        score(p // SSD_RATIO + 1)
                    mix(p)


def rope(nc, io, qk):
    heads = 2 * DIL_HEADS
    two_pi = (6.28125, 0.00193500518798828125, 3.0199159819567e-07)
    magic = 1.5 * 2.0 ** 23
    pi = 3.1415925
    with Stage(nc, "rope") as st:
        pos_i = st.sb("pos_i", [P, NT], I32)
        pos = st.sb("pos", [P, NT])
        inv = st.sb("inv", [P, ROT_HALF])
        ang = st.sb("ang", [P, NT, ROT_HALF])
        turns = st.sb("turns", [P, 2, NT, ROT_HALF])
        rest = st.sb("rest", [P, 2, NT, ROT_HALF])
        a, b, c, d = (st.sb(s, [P, heads, ROT_HALF]) for s in "abcd")
        landed, reduced, sines, dve_order = (st.sem(s) for s in ("landed", "reduced", "sines", "dve_order"))
        with nc.Block() as block:

            @block.sync
            def _(sp):
                sp.dma_start(pos_i[:, :], io["positions"]).then_inc(landed, 16)
                sp.dma_start(inv[:, :], io["c_inv"].partition_broadcast(P)).then_inc(landed, 16)
                sp.wait_ge(landed, 32)

            @block.vector
            def _(dve):
                order = InOrder(dve, dve_order)
                dve.wait_ge(landed, 32)
                order(dve.tensor_copy(pos[:, :], pos_i[:, :]))
                order(dve.tensor_tensor(ang[:, :, :], pos[:, :].unsqueeze(2).broadcast_to([P, NT, ROT_HALF]),
                                        inv[:, :].unsqueeze(1).broadcast_to([P, NT, ROT_HALF]), ALU.mult))
                for w in range(2):
                    t, r = turns[:, w, :, :], rest[:, w, :, :]
                    order(dve.tensor_scalar(t, ang[:, :, :], 0.15915494309189535, 0.25 * w, ALU.mult, ALU.add))
                    order(dve.tensor_scalar(t, t, magic, None, ALU.add))
                    order(dve.tensor_scalar(t, t, magic, None, ALU.subtract))
                    order(dve.scalar_tensor_tensor(r, t, -two_pi[0], ang[:, :, :], ALU.mult, ALU.add))
                    order(dve.scalar_tensor_tensor(r, t, -two_pi[1], r, ALU.mult, ALU.add))
                    order(dve.scalar_tensor_tensor(r, t, -two_pi[2], r, ALU.mult, ALU.add))
                    if w:
                        order(dve.tensor_scalar(r, r, 1.5707963267948966, None, ALU.add))
                    order(dve.tensor_scalar(r, r, pi, -pi, ALU.min, ALU.max))
                dve.sem_inc(reduced, 1)
                dve.wait_ge(sines, 1)
                for i in range(NT):
                    x1, x2 = qk[:, i, :, 0:ROT_HALF], qk[:, i, :, ROT_HALF:ROT]
                    sin = rest[:, 0, i, :].unsqueeze(1).broadcast_to([P, heads, ROT_HALF])
                    cos = rest[:, 1, i, :].unsqueeze(1).broadcast_to([P, heads, ROT_HALF])
                    order(dve.tensor_tensor(a[:, :, :], x1, cos, ALU.mult))
                    order(dve.tensor_tensor(b[:, :, :], x2, sin, ALU.mult))
                    order(dve.tensor_tensor(c[:, :, :], x2, cos, ALU.mult))
                    order(dve.tensor_tensor(d[:, :, :], x1, sin, ALU.mult))
                    order(dve.tensor_tensor(x1, a[:, :, :], b[:, :, :], ALU.subtract))
                    order(dve.tensor_tensor(x2, c[:, :, :], d[:, :, :], ALU.add))

            @block.scalar
            def _(act):
                act.wait_ge(reduced, 1)
                act.activation(rest[:, :, :, :], rest[:, :, :, :], ACT.Sin).then_inc(sines, 1)


def attend(nc, name, units, ident, groups, wide, scale):
    n_u = len(units)
    with Stage(nc, name) as st:
        s = st.sb("s", [P, 2, groups, wide])
        pT = st.sb("pT", [P, 2, groups, wide])
        peak = st.sb("peak", [P, 2])
        total = st.sb("total", [P, 2])
        scores = st.ps("scores", [P, groups, 512])
        turned = st.ps("turned", [P, groups, 512])
        mixed = st.ps("mixed", [P, 2, 512])
        scored, masked, peaked, exped, turn_done, turn_out, mix_done, mix_out, dve_order = (
            st.sem(x) for x in ("scored", "masked", "peaked", "exped", "turn_done", "turn_out", "mix_done",
                                "mix_out", "dve_order"))
        with nc.Block() as block:

            @block.tensor
            def _(pe):
                def score(u):
                    pieces, w, _, _, _ = units[u]
                    if u:
                        pe.wait_ge(masked, u)
                    for g in range(groups):
                        for n, (q, k) in enumerate(pieces[g]):
                            last = pe.matmul(scores[:, g, 0:w], q, k, start=(n == 0), stop=(n == len(pieces[g]) - 1))
                    last.then_inc(scored, 1)

                def turn(u):
                    _, w, _, _, _ = units[u]
                    pe.wait_ge(exped, u + 1)
                    if u:
                        pe.wait_ge(turn_out, u)
                    for g in range(groups):
                        for n in range(w // P):
                            last = pe.transpose(turned[:, g, n * P:(n + 1) * P], s[:, u % 2, g, n * P:(n + 1) * P],
                                                ident[:, :])
                    last.then_inc(turn_done, 1)

                def mix(u):
                    _, w, _, values, out = units[u]
                    pe.wait_ge(turn_out, u + 1)
                    if u >= 2:
                        pe.wait_ge(mix_out, u - 1)
                    blocks = [(g, n) for g in range(groups) for n in range(w // P)]
                    for g, n in blocks:
                        last = pe.matmul(mixed[:, u % 2, 0:out.shape[1]], pT[:, u % 2, g, n * P:(n + 1) * P],
                                         values(g, n), start=((g, n) == blocks[0]), stop=((g, n) == blocks[-1]))
                    last.then_inc(mix_done, 1)

                for u in range(n_u + 2):
                    if u < n_u:
                        score(u)
                    if u >= 2:
                        mix(u - 2)
                    if 1 <= u <= n_u:
                        turn(u - 1)

            @block.vector
            def _(dve):
                order = InOrder(dve, dve_order)
                for u in range(n_u + 2):
                    if u < n_u:
                        _, w, mask, _, _ = units[u]
                        dve.wait_ge(scored, u + 1)
                        if u >= 2:
                            dve.wait_ge(turn_done, u - 1)
                        now = s[:, u % 2, :, 0:w]
                        if mask is None:
                            order(dve.tensor_scalar(now, scores[:, :, 0:w], scale, None, ALU.mult))
                        else:
                            order(dve.scalar_tensor_tensor(now, scores[:, :, 0:w], scale, mask, ALU.mult, ALU.add))
                        dve.sem_inc(masked, 1)
                        order(dve.tensor_reduce(peak[:, u % 2:u % 2 + 1], now, mybir.AxisListType.XY, ALU.max))
                        dve.tensor_scalar(peak[:, u % 2:u % 2 + 1], peak[:, u % 2:u % 2 + 1], -1.0, None,
                                          ALU.mult).then_inc(peaked, 1)
                    if u >= 2:
                        v, out = u - 2, units[u - 2][4]
                        dve.wait_ge(mix_done, v + 1)
                        order(dve.reciprocal(total[:, v % 2:v % 2 + 1], total[:, v % 2:v % 2 + 1]))
                        order(dve.tensor_scalar(out, mixed[:, v % 2, 0:out.shape[1]], total[:, v % 2:v % 2 + 1],
                                                None, ALU.mult))
                        dve.sem_inc(mix_out, 1)

            @block.scalar
            def _(act):
                for u in range(n_u + 1):
                    if u < n_u:
                        w = units[u][1]
                        act.wait_ge(peaked, u + 1)
                        if u >= 2:
                            act.wait_ge(mix_out, u - 1)
                        now = s[:, u % 2, :, 0:w]
                        act.activation(now, now, ACT.Exp, bias=peak[:, u % 2:u % 2 + 1],
                                       accum_out=total[:, u % 2:u % 2 + 1]).then_inc(exped, 1)
                    if u >= 1:
                        v, w = u - 1, units[u - 1][1]
                        act.wait_ge(turn_done, v + 1)
                        if v >= 2:
                            act.wait_ge(mix_done, v - 1)
                        act.copy(pT[:, v % 2, :, 0:w], turned[:, :, 0:w]).then_inc(turn_out, 1)


def peer_select(nc, io, qT, chosen, gates):
    hc = 2 * PEER_HEADS
    H, T = PEER_HEADS, PEER_TOP
    with Stage(nc, "sel") as st:
        keys = st.sb("keys", [P, hc, PEER_KEYS])
        sc = st.sb("sc", [P, 2, hc, PEER_KEYS])
        v = st.sb("v", [P, hc, T])
        ix = st.sb("ix", [P, hc, T], U32)
        ixf = st.sb("ixf", [P, hc, T])
        cand = st.sb("cand", [P, H, T, T])
        match = st.sb("match", [P, H, T, T])
        top = st.sb("top", [P, 2, H, T])
        pos = st.sb("pos", [P, H, T], U32)
        part = st.sb("part", [P, 2, H, T], U32)
        partf = st.sb("partf", [P, 2, H, T])
        picked = st.sb("picked", [P, 2, H, T])
        iota = st.sb("iota", [P, T])
        total = st.sb("total", [P, H])
        scores = st.ps("scores", [P, hc, PEER_KEYS])
        landed, scored, sc_ready, sc_used, top_ready, exp_ready, top_used, dve_order = (
            st.sem(x) for x in ("landed", "scored", "sc_ready", "sc_used", "top_ready", "exp_ready", "top_used",
                                "dve_order"))
        with nc.Block() as block:

            @block.sync
            def _(sp):
                sp.dma_start(keys[:, :, :], io["sub_keys"]).then_inc(landed, 16)
                sp.dma_start(iota[:, :], io["c_iota16"].partition_broadcast(P)).then_inc(landed, 16)
                sp.wait_ge(landed, 32)

            @block.tensor
            def _(pe):
                pe.wait_ge(landed, 32)
                for i in range(NT):
                    if i:
                        pe.wait_ge(sc_ready, i)
                    for c in range(hc):
                        last = pe.matmul(scores[:, c, :], qT[:, c, i * P:(i + 1) * P], keys[:, c, :],
                                         start=True, stop=True)
                    last.then_inc(scored, 1)

            @block.scalar
            def _(act):
                for i in range(NT):
                    act.wait_ge(scored, i + 1)
                    if i >= 2:
                        act.wait_ge(sc_used, i - 1)
                    act.copy(sc[:, i % 2, :, :], scores[:, :, :]).then_inc(sc_ready, 1)
                    if i:
                        act.wait_ge(top_ready, i)
                        act.activation(top[:, (i - 1) % 2, :, :], top[:, (i - 1) % 2, :, :], ACT.Exp
                                       ).then_inc(exp_ready, 1)
                act.wait_ge(top_ready, NT)
                act.activation(top[:, (NT - 1) % 2, :, :], top[:, (NT - 1) % 2, :, :], ACT.Exp
                               ).then_inc(exp_ready, 1)

            @block.vector
            def _(dve):
                order = InOrder(dve, dve_order)
                dve.wait_ge(landed, 32)

                def best16(vals, where, x):
                    order(dve.max(vals[:, 0:8], x))
                    order(dve.max_index(where[:, 0:8], vals[:, 0:8], x))
                    order(dve.match_replace(x, vals[:, 0:8], x, -3.0e38))
                    order(dve.max(vals[:, 8:16], x))
                    order(dve.max_index(where[:, 8:16], vals[:, 8:16], x))

                def finish(i):
                    dve.wait_ge(exp_ready, i + 1)
                    t = top[:, i % 2, :, :]
                    order(dve.tensor_reduce(total[:, :], t, AX_X, ALU.add))
                    order(dve.reciprocal(total[:, :], total[:, :]))
                    order(dve.tensor_tensor(gates[:, i, :].rearrange("p (h t) -> p h t", h=H), t,
                                            total[:, :].unsqueeze(2).broadcast_to([P, H, T]), ALU.mult))

                for i in range(NT):
                    dve.wait_ge(sc_ready, i + 1)
                    for c in range(hc):
                        best16(v[:, c, :], ix[:, c, :], sc[:, i % 2, c, :])
                    dve.sem_inc(sc_used, 1)
                    order(dve.tensor_copy(ixf[:, :, :], ix[:, :, :]))
                    v4 = v[:, :, :].rearrange("p (h c) t -> p h c t", c=2)
                    i4 = ixf[:, :, :].rearrange("p (h c) t -> p h c t", c=2)
                    order(dve.tensor_tensor(cand[:, :, :, :], v4[:, :, 0, :].unsqueeze(3).broadcast_to([P, H, T, T]),
                                            v4[:, :, 1, :].unsqueeze(2).broadcast_to([P, H, T, T]), ALU.add))
                    for h in range(H):
                        best16(top[:, i % 2, h, :], pos[:, h, :], cand[:, h, :, :].rearrange("p a b -> p (a b)"))
                    order(dve.tensor_scalar(part[:, 0, :, :], pos[:, :, :], 4, None, ALU.logical_shift_right))
                    order(dve.tensor_scalar(part[:, 1, :, :], pos[:, :, :], T - 1, None, ALU.bitwise_and))
                    order(dve.tensor_copy(partf[:, :, :, :], part[:, :, :, :]))
                    for c in range(2):
                        order(dve.tensor_tensor(
                            match[:, :, :, :].rearrange("p h t a -> p (h t) a"),
                            partf[:, c, :, :].rearrange("p h t -> p (h t)").unsqueeze(2).broadcast_to([P, H * T, T]),
                            iota[:, :].unsqueeze(1).broadcast_to([P, H * T, T]), ALU.is_equal))
                        order(dve.tensor_tensor(match[:, :, :, :], match[:, :, :, :],
                                                i4[:, :, c, :].unsqueeze(2).broadcast_to([P, H, T, T]), ALU.mult))
                        order(dve.tensor_reduce(picked[:, c, :, :], match[:, :, :, :], AX_X, ALU.add))
                    order(dve.scalar_tensor_tensor(
                        chosen[:, i, :].rearrange("p (h t) -> p h t", h=H), picked[:, 0, :, :], float(PEER_KEYS),
                        picked[:, 1, :, :], ALU.mult, ALU.add))
                    order(dve.tensor_tensor(picked[:, 0, :, :], top[:, i % 2, :, :],
                                            top[:, i % 2, :, 0:1].broadcast_to([P, H, T]), ALU.subtract))
                    dve.tensor_copy(top[:, i % 2, :, :], picked[:, 0, :, :]).then_inc(top_ready, 1)
                    dve.wait_ge(top_ready, i + 1)
                    if i:
                        finish(i - 1)
                finish(NT - 1)


GROUP = 8
RING = 2 * GROUP
ROUNDS = PEER_SLOTS // RING


def peer_experts(nc, io, hn, h, chosen, gates, out):
    down = io["peer_down_2"][0]
    up = io["peer_up_2"][0]
    with Stage(nc, "peer") as st:
        down_rows = [st.sb(f"down{u}", [P, D]) for u in range(RING)]
        up_rows = [st.sb(f"up{u}", [P, D]) for u in range(RING)]
        junk = st.sb("junk", [P, 2, D])
        idx_d = st.sb("idx_d", [P, 2, GROUP], U32)
        idx_u = st.sb("idx_u", [P, 2, GROUP], U32)
        dots = st.sb("dots", [P, NT, PEER_SLOTS])
        coef = st.sb("coef", [P, NT, PEER_SLOTS])
        diag = st.sb("diag", [P, 4, P])
        ident = st.sb("ident", [P, P])
        zeros = st.sb("zeros", [P, 512])
        acc = st.ps("acc", [P, 2, D])
        down_in = [st.sem(f"down_in{u}") for u in range(RING)]
        up_in = [st.sem(f"up_in{u}") for u in range(RING)]
        landed, down_used, up_used, gelu_done, coef_done, diag_done, diag_used, sum_done, added, stored = (
            st.sem(x) for x in ("landed", "down_used", "up_used", "gelu_done", "coef_done", "diag_done",
                                "diag_used", "sum_done", "added", "stored"))
        dve_order, ready, idx_ready, idx_seen = (st.sem(x) for x in ("dve_order", "ready", "idx_ready", "idx_seen"))

        steps = [(j < NT, j >= 1) for j in range(NT + 1)]

        with nc.Block() as block:

            @block.sync
            def _(sp):
                sp.dma_start(ident[:, :], io["c_ident"]).then_inc(landed, 16)
                for i in range(NT):
                    sp.wait_ge(added, i + 1)
                    sp.dma_start(out[i * P:(i + 1) * P, :], h[:, i, :]).then_inc(stored, 16)
                sp.wait_ge(stored, 16 * NT)

            @block.gpsimd
            def _(pool):
                pool.sem_inc(down_used, RING)
                pool.sem_inc(up_used, RING)
                copies = 0
                for j, (has_down, has_up) in enumerate(steps):
                    kinds = ([("down", j)] if has_down else []) + ([("up", j - 1)] if has_up else [])
                    with pool.Fori(0, ROUNDS) as r:
                        for b in range(2):
                            for n, (kind, i) in enumerate(kinds):
                                used = down_used if kind == "down" else up_used
                                idx = idx_d if kind == "down" else idx_u
                                first = r * RING + b * GROUP
                                pool.wait_ge(used, first + (i * PEER_SLOTS + GROUP))
                                pool.tensor_copy(idx[:, b, :], chosen[:, i, bass.ds(first, GROUP)]
                                                 ).then_inc(idx_ready, 1)
                                pool.wait_ge(idx_ready, r * (2 * len(kinds)) + (copies + b * len(kinds) + n + 1))
                                pool.sem_inc(idx_seen, 1)
                            for u in range(GROUP):
                                for kind, i in kinds:
                                    rows, table, sems, idx = ((down_rows, down, down_in, idx_d) if kind == "down"
                                                              else (up_rows, up, up_in, idx_u))
                                    pool.indirect_dma_start(
                                        rows[b * GROUP + u][:, :], None, table,
                                        bass.IndirectOffsetOnAxis(ap=idx[:, b, u:u + 1], axis=0)
                                    ).then_inc(sems[b * GROUP + u], 16)
                    copies += ROUNDS * 2 * len(kinds)

            @block.vector
            def _(dve):
                order = InOrder(dve, dve_order)
                dve.memset(zeros[:, :], 0.0).then_inc(ready, 1)
                for j, (has_down, has_up) in enumerate(steps):
                    if has_down:
                        with dve.Fori(0, ROUNDS) as r:
                            for u in range(RING):
                                slot = r * RING + u
                                dve.wait_ge(down_in[u], (r + (j * ROUNDS + 1)) * 16)
                                dve.wait_ge(down_used, slot + (j * PEER_SLOTS + RING - 1))
                                dve.scalar_tensor_tensor(junk[:, u % 2, :], down_rows[u][:, :], 1.0, hn[:, j, :],
                                                         ALU.mult, ALU.mult,
                                                         accum_out=dots[:, j, bass.ds(slot, 1)]
                                                         ).then_inc(down_used, 1)
                        dve.wait_ge(gelu_done, j + 1)
                        dve.tensor_tensor(coef[:, j, :], dots[:, j, :], gates[:, j, :], ALU.mult
                                          ).then_inc(coef_done, 1)
                    if has_up:
                        i = j - 1
                        dve.wait_ge(sum_done, i + 1)
                        dve.tensor_tensor(h[:, i, :], h[:, i, :], acc[:, i % 2, :], ALU.add).then_inc(added, 1)

            @block.scalar
            def _(act):
                act.sem_inc(diag_used, 4)
                act.wait_ge(landed, 16)
                for j, (has_down, has_up) in enumerate(steps):
                    if has_up:
                        i = j - 1
                        act.wait_ge(coef_done, i + 1)
                        with act.Fori(0, ROUNDS) as r:
                            for u in range(RING):
                                slot = r * RING + u
                                act.wait_ge(diag_used, slot + (i * PEER_SLOTS + 1))
                                act.activation(diag[:, u % 4, :], ident[:, :], ACT.Copy,
                                               scale=coef[:, i, bass.ds(slot, 1)]).then_inc(diag_done, 1)
                    if has_down:
                        act.wait_ge(down_used, (j + 1) * PEER_SLOTS + RING)
                        act.activation(dots[:, j, :], dots[:, j, :], ACT.Gelu).then_inc(gelu_done, 1)

            @block.tensor
            def _(pe):
                pe.wait_ge(ready, 1)
                for i in range(NT):
                    if i >= 2:
                        pe.wait_ge(added, i - 1)
                    for half in range(2):
                        pe.matmul(acc[:, i % 2, half * 512:(half + 1) * 512], zeros[:, 0:P], zeros[:, :],
                                  start=True, stop=False, skip_group_check=True)
                    with pe.Fori(0, ROUNDS) as r:
                        for u in range(RING):
                            slot = r * RING + u
                            pe.wait_ge(diag_done, slot + (i * PEER_SLOTS + 1))
                            pe.wait_ge(up_in[u], (r + (i * ROUNDS + 1)) * 16)
                            for half in range(2):
                                last = pe.matmul(acc[:, i % 2, half * 512:(half + 1) * 512], diag[:, u % 4, :],
                                                 up_rows[u][:, half * 512:(half + 1) * 512],
                                                 start=False, stop=False, skip_group_check=True)
                            last.then_inc(up_used, 1)
                            pe.wait_ge(up_used, slot + (i * PEER_SLOTS + RING + 1))
                            pe.sem_inc(diag_used, 1)
                    for half in range(2):
                        last = pe.matmul(acc[:, i % 2, half * 512:(half + 1) * 512], zeros[:, 0:P], zeros[:, :],
                                         start=False, stop=True, skip_group_check=True)
                    last.then_inc(sum_done, 1)


def second_block(nc, io, x, ident, out, dbg=None):
    w_in = io["w_in_2"][0].rearrange("(k p) c -> p k c", p=P)
    acum_dram = nc.dram_tensor("scratch_acum", [SSD_HEADS, SEQ], F32).ap()

    def copy_jobs(tiles, width, dst):
        return [Job("token", 0, width, (lambda nc, ps, i=i: (nc.scalar.copy if i % 2 else nc.vector.tensor_copy)(
            dst(i), ps)), "act" if i % 2 else "dve", col=col, rows=rows) for i, rows, col in tiles]

    with Stage(nc, "b2") as st:
        cols = st.sb("cols", [P, COLS_2_N])
        load(nc, "load2", [(cols[:, :], io["p_cols_2"])])

        def gain(name):
            a, n = COLS_2[name]
            return cols[:, a:a + n]

        with own_semaphores(nc), Stage(nc, "branches") as br:
            uT = br.sb("uT", [P, KD, SEQ])
            ssdT = br.sb("ssdT", [P, KD, SEQ])
            normalise(nc, "norm3", x, SEQ_TILES, gain("mix_g"), ident, uT)

            def source(k):
                return uT[:, k, :]

            def w_cols(first, width):
                return w_in[:, :, first:first + width]

            with Stage(nc, "ssdbuf") as s1:
                y = s1.sb("y", [P, NT, D])
                z = s1.sb("z", [P, NT, D])
                xbc = s1.sb("xbc", [P, XBC_TILES, SEQ + SSD_CONV - 1])
                dt_raw = s1.sb("dt_raw", [SSD_HEADS, SEQ])
                chunks = [(w_cols(OFF_XBC + n * 512, 512), source, [
                    Job("channel", c * P, P, (lambda nc, ps, t=4 * n + c, eng=eng: (
                        nc.scalar.copy if eng == "act" else nc.vector.tensor_copy)(
                            xbc[:, t, SSD_CONV - 1:SSD_CONV - 1 + SEQ], ps)), eng)
                    for c, eng in enumerate(("act", "dve") * 2)]) for n in range(XBC // 512)]
                chunks.append((w_cols(OFF_DT, SSD_HEADS), source, [
                    Job("channel", 0, SSD_HEADS, lambda nc, ps: nc.vector.tensor_copy(dt_raw[:, :], ps), "dve")]))
                chunks += [(w_cols(n * 512, 512), source, token_jobs(
                    SEQ_TILES, 512, lambda nc, i, r, ps, n=n: nc.scalar.activation(
                        z[:, i, n * 512:(n + 1) * 512], ps, ACT.Silu))) for n in range(2)]
                project(nc, "proj_ssd", chunks)
                clear(nc, "clear_ssd", [xbc[:, :, 0:SSD_CONV - 1]])
                w0, b0 = COLS_2["conv_w"][0], COLS_2["conv_b"][0]
                conv_silu(nc, "ssc", xbc, XBC_TILES, SSD_CONV, SEQ,
                          lambda c, j: cols[:, w0 + c * SSD_CONV + j:w0 + c * SSD_CONV + j + 1],
                          lambda c: cols[:, b0 + c:b0 + c + 1], xbc)
                with Stage(nc, "ssdbuf2") as s2:
                    acum_rows = s2.sb("acum_rows", [P, SSD_HEADS, SEQ])
                    acum_col = s2.sb("acum_col", [P, NT, SSD_HEADS])
                    x_dt = s2.sb("x_dt", [P, NT, D])
                    ssd_prepare(nc, io, cols, dt_raw, xbc, ident, acum_rows, acum_col, y, x_dt, acum_dram)
                    ssd(nc, io, xbc, acum_rows, acum_col, x_dt, z, y)
                gain_row = s1.sb("gain_row", [P, D])
                load(nc, "load_ssd_g", [(gain_row[:, :], io["ssd_g_row"].partition_broadcast(P))])
                rms_groups(nc, "ssd_norm", [y[:, i, :] for i in range(NT)], SSD_GROUPS, D // SSD_GROUPS,
                           gain_row[:, :])
                if dbg: dbg("y_ssd", y[:, :, :])
                turn_rows(nc, "turn_ssd", y, SEQ_TILES, ident, ssdT)

            dilT = br.sb("dilT", [P, DIL_J * DIL_HD // P, SEQ])
            with Stage(nc, "dilbuf") as s1:
                qkv = s1.sb("qkv", [P, NT, 3 * DIL_W])
                y = s1.sb("y", [P, NT, DIL_J * DIL_HD])
                qkT = s1.sb("qkT", [P, 2 * DIL_W // P, SEQ])
                q_gain = s1.sb("q_gain", [P, DIL_HD])
                k_gain = s1.sb("k_gain", [P, DIL_HD])
                mask = s1.sb("mask", [P, len(DIL), SEQ])
                project(nc, "proj_dil", [
                    (w_cols(OFF_DQ + n * 384, 384), source,
                     copy_jobs(SEQ_TILES, 384, lambda i, n=n: qkv[:, i, n * 384:(n + 1) * 384]))
                    for n in range(3 * DIL_W // 384)])
                load(nc, "load_dil", [(q_gain[:, :], io["dil_q_row"].partition_broadcast(P)),
                                      (k_gain[:, :], io["dil_k_row"].partition_broadcast(P)),
                                      (mask[:, :, :], io["c_dilated"])])
                rms_groups(nc, "norm_dq", [qkv[:, i, 0:DIL_W] for i in range(NT)], DIL_HEADS, DIL_HD, q_gain[:, :])
                rms_groups(nc, "norm_dk", [qkv[:, i, DIL_W:2 * DIL_W] for i in range(NT)], DIL_HEADS, DIL_HD,
                           k_gain[:, :])
                rope(nc, io, qkv[:, :, 0:2 * DIL_W].rearrange("p i (h e) -> p i h e", e=DIL_HD))
                turn_rows(nc, "turn_dil_q", qkv, SEQ_TILES, ident, qkT[:, 0:6, :], DIL_W // P)
                turn_rows(nc, "turn_dil_k", qkv[:, :, DIL_W:2 * DIL_W], SEQ_TILES, ident, qkT[:, 6:12, :],
                          DIL_W // P)
                units = []
                for i in range(NT):
                    w = (i + 1) * P
                    for j in range(DIL_J):
                        pieces = []
                        for g in range(len(DIL)):
                            head = g * DIL_J + j
                            a = (head % 2) * DIL_HD
                            pieces.append([(qkT[a:a + DIL_HD, head // 2, i * P:(i + 1) * P],
                                            qkT[a:a + DIL_HD, 6 + head // 2, 0:w])])
                        units.append((pieces, w, mask[:, :, SEQ - w:SEQ],
                                      (lambda g, n, j=j: qkv[:, n, 2 * DIL_W + (g * DIL_J + j) * DIL_HD:
                                                             2 * DIL_W + (g * DIL_J + j + 1) * DIL_HD]),
                                      y[:, i, j * DIL_HD:(j + 1) * DIL_HD]))
                attend(nc, "dil", units, ident, len(DIL), SEQ, float(DIL_HD) ** -0.5)
                if dbg: dbg("y_dil", y[:, :, :])
                turn_rows(nc, "turn_dil", y, SEQ_TILES, ident, dilT, DIL_J * DIL_HD // P)

            memT = br.sb("memT", [P, MEM_W // P, SEQ])
            with Stage(nc, "membuf") as s1:
                mem = s1.sb("mem", [P, N_MEM // P, D])
                mem_uT = s1.sb("mem_uT", [P, KD, N_MEM])
                mkv = s1.sb("mkv", [P, N_MEM // P, 2 * MEM_W])
                mq = s1.sb("mq", [P, NT, MEM_W])
                mqT = s1.sb("mqT", [P, MEM_W // P, SEQ])
                mkT = s1.sb("mkT", [P, MEM_W // P, N_MEM])
                q_gain = s1.sb("q_gain", [P, MEM_HD])
                k_gain = s1.sb("k_gain", [P, MEM_HD])
                y = s1.sb("y", [P, NT, MEM_W])
                mem_tiles = [(i, P, P * i) for i in range(N_MEM // P)]
                load(nc, "load_mem", [(mem[:, :, :], io["mem_2"][0].rearrange("(i p) d -> p i d", p=P)),
                                      (q_gain[:, :], io["mem_q_row"].partition_broadcast(P)),
                                      (k_gain[:, :], io["mem_k_row"].partition_broadcast(P))])
                normalise(nc, "norm_mem", mem, mem_tiles, gain("mem_g"), ident, mem_uT)
                w_kv = io["w_mem_kv_2"][0].rearrange("(k p) c -> p k c", p=P)
                project(nc, "proj_mem", [
                    (w_kv[:, :, n * 384:(n + 1) * 384], lambda k: mem_uT[:, k, :],
                     copy_jobs(mem_tiles, 384, lambda i, n=n: mkv[:, i, n * 384:(n + 1) * 384]))
                    for n in range(2 * MEM_W // 384)] + [
                    (w_cols(OFF_MQ + n * 384, 384), source,
                     copy_jobs(SEQ_TILES, 384, lambda i, n=n: mq[:, i, n * 384:(n + 1) * 384]))
                    for n in range(MEM_W // 384)])
                rms_groups(nc, "norm_mq", [mq[:, i, :] for i in range(NT)], HEADS, MEM_HD, q_gain[:, :])
                rms_groups(nc, "norm_mk", [mkv[:, i, 0:MEM_W] for i in range(N_MEM // P)], HEADS, MEM_HD,
                           k_gain[:, :])
                turn_rows(nc, "turn_mq", mq, SEQ_TILES, ident, mqT, MEM_W // P)
                turn_rows(nc, "turn_mk", mkv, mem_tiles, ident, mkT, MEM_W // P)

                def pieces_of(hd):
                    a, end = hd * MEM_HD, (hd + 1) * MEM_HD
                    while a < end:
                        b = min(end, (a // P + 1) * P)
                        yield a // P, a % P, b - a
                        a = b

                units = [([[(mqT[a:a + n, t, i * P:(i + 1) * P], mkT[a:a + n, t, :]) for t, a, n in pieces_of(hd)]],
                          N_MEM, None,
                          (lambda g, n, hd=hd: mkv[:, n, MEM_W + hd * MEM_HD:MEM_W + (hd + 1) * MEM_HD]),
                          y[:, i, hd * MEM_HD:(hd + 1) * MEM_HD]) for i in range(NT) for hd in range(HEADS)]
                attend(nc, "mem", units, ident, 1, N_MEM, float(MEM_HD) ** -0.5)
                if dbg: dbg("y_mem", y[:, :, :])
                turn_rows(nc, "turn_mem", y, SEQ_TILES, ident, memT, MEM_W // P)

            with Stage(nc, "mergebuf") as s1:
                prod = s1.sb("prod", [P, BRANCHES, NT, D])
                chunks = []
                for b, (wt, turned, nk) in enumerate((("w_ssd_br_2", ssdT, KD), ("w_dil_br_2", dilT, 2),
                                                      ("w_mem_br_2", memT, MEM_W // P))):
                    wb = io[wt][0].rearrange("(k p) c -> p k c", p=P)
                    for n in range(2):
                        part = slice(n * 512, (n + 1) * 512)
                        chunks.append((w_cols(OFF_GATE + b * D + n * 512, 512), source, token_jobs(
                            SEQ_TILES, 512, lambda nc, i, r, ps, b=b, part=part: nc.scalar.activation(
                                prod[:, b, i, part], ps, ACT.Sigmoid))))
                        jobs = token_jobs(SEQ_TILES, 512, lambda nc, i, r, ps, b=b, part=part: nc.vector.tensor_tensor(
                            prod[:, b, i, part], prod[:, b, i, part], ps, ALU.mult), "dve")
                        for i, job in enumerate(jobs):
                            job.after = (len(chunks) - 1) * NT + i
                        chunks.append((wb[:, :, part], (lambda k, turned=turned: turned[:, k, :]), jobs))
                project(nc, "proj_merge", chunks)
                dve_done = s1.sem("dve_done")
                with nc.Block() as block:

                    @block.vector
                    def _(dve):
                        order = InOrder(dve, dve_done)
                        for b in range(1, BRANCHES):
                            order(dve.tensor_tensor(prod[:, 0, :, :], prod[:, 0, :, :], prod[:, b, :, :], ALU.add))

                turn_rows(nc, "turn_merged", prod[:, 0, :, :], SEQ_TILES, ident, uT)
                w_out = io["w_out_2"][0].rearrange("(k p) c -> p k c", p=P)
                project(nc, "proj_out2", [
                    (w_out[:, :, n * 512:(n + 1) * 512], source,
                     token_jobs(SEQ_TILES, 512, lambda nc, i, r, ps, n=n: nc.vector.tensor_tensor(
                         x[:, i, n * 512:(n + 1) * 512], x[:, i, n * 512:(n + 1) * 512], ps, ALU.add), "dve"))
                    for n in range(2)])
        if dbg: dbg("hmix2", x[:, 0:NT, :])

        with Stage(nc, "peerbuf") as s1:
            hn = s1.sb("hn", [P, NT, D])
            chosen = s1.sb("chosen", [P, NT, PEER_SLOTS])
            gates = s1.sb("gates", [P, NT, PEER_SLOTS])
            with Stage(nc, "selbuf") as s2:
                hnT = s2.sb("hnT", [P, KD, SEQ])
                gain_row = s2.sb("gain_row", [P, D])
                qT = s2.sb("qT", [P, 2 * PEER_HEADS, SEQ])
                load(nc, "load_peer_g", [(gain_row[:, :], io["ffn_g_row_2"].partition_broadcast(P))])
                normalise(nc, "norm4", x, SEQ_TILES, None, ident, hnT, gain_row=gain_row, kept=hn)
                w_q = io["peer_w_query_2"][0].rearrange("(k p) c -> p k c", p=P)
                project(nc, "proj_query", [(w_q[:, :, n * 512:(n + 1) * 512], lambda k: hnT[:, k, :], [
                    Job("channel", c * P, P, (lambda nc, ps, t=4 * n + c, eng=eng: (
                        nc.scalar.copy if eng == "act" else nc.vector.tensor_copy)(qT[:, t, :], ps)), eng)
                    for c, eng in enumerate(("act", "dve") * 2)]) for n in range(4)])
                peer_select(nc, io, qT, chosen, gates)
            peer_experts(nc, io, hn, x, chosen, gates, out)


def two_blocks(nc, io, out):
    with Stage(nc, "top") as st:
        h = st.sb("h", [P, NT + 1, D])
        ident = st.sb("ident", [P, P])
        with own_semaphores(nc):
            first_block(nc, io, h, ident)
        with Stage(nc, "between") as s1:
            gain_row = s1.sb("gain_row", [P, D])
            load(nc, "load_final_g", [(gain_row[:, :], io["final_g_row"].partition_broadcast(P))])
            normalise(nc, "norm_final", h, SEQ_TILES, None, ident, None, gain_row=gain_row, kept=h)
        second_block(nc, io, h, ident, out)


def constants():
    import numpy as np

    f = np.float32
    half = P // 2
    inv = (f(10000.0) ** (-np.arange(half, dtype=f) / f(half))).astype(f)
    ang = np.arange(TOK, dtype=f)[None, :] * inv[:, None]
    x = np.arange(REL_W)[None, :] - REL_BASE - np.arange(P)[:, None]
    p, c = np.arange(P)[:, None], np.arange(P)[None, :]
    back = p + SEQ - P - np.arange(SEQ)[None, :]
    dilated = np.stack([np.where((back >= 0) & (back <= window) & (back % step == 0), 0.0, NEG)
                        for window, step in DIL], 1)
    inv2 = np.exp(f(-np.log(500000.0) * (2.0 / ROT)) * np.arange(ROT_HALF, dtype=f)).astype(f)
    token_id = np.zeros((P, NT + 1), f)
    for i, rows, col in ALL_TILES:
        token_id[:, i] = col + np.arange(P)
    return {
        "c_ident": np.eye(P, dtype=f),
        "c_cos": np.concatenate([np.cos(ang)] * 2).astype(f),
        "c_sin": np.concatenate([-np.sin(ang), np.sin(ang)]).astype(f),
        "c_ahead": np.maximum(x, 0).astype(f),
        "c_behind": np.maximum(-x, 0).astype(f),
        "c_diag": (1.0 + (x == 0)).astype(f),
        "c_keep": np.stack([c >= p, c <= p], 1).astype(f),
        "c_token_id": token_id,
        "c_dilated": dilated.astype(f),
        "c_inv": inv2[None, :],
        "c_iota16": np.arange(PEER_TOP, dtype=f)[None, :],
        "c_ids": (META + np.arange(SEQ, dtype=f))[None, :],
    }


def channel_columns(v):
    return v.reshape((-1, P) + v.shape[1:]).swapaxes(0, 1)


def layouts(inputs):
    import numpy as np

    cat = np.concatenate
    conv = channel_columns(inputs["conv_w"][0].T)
    gate_b = np.zeros((P, 4), np.float32)
    gate_b[:HEADS] = inputs["b_gates"][0].reshape(4, HEADS).T
    heads = np.zeros((P, 2), np.float32)
    heads[:SSD_HEADS, 0] = inputs["ssd_dt_bias_2"][0]
    heads[:SSD_HEADS, 1] = inputs["ssd_a_log_2"][0]
    return {
        "p_cols_2": np.ascontiguousarray(cat([
            channel_columns(inputs["norm_mix_w_2"][0]), channel_columns(inputs["mem_norm_w_2"][0]),
            channel_columns(inputs["ssd_conv_w_2"][0].T).reshape(P, -1), channel_columns(inputs["ssd_conv_b_2"][0]),
            heads], axis=1)),
        "positions": np.ascontiguousarray(inputs["positions_2"][0].reshape(NT, P).T),
        "sub_keys": np.ascontiguousarray(inputs["peer_sub_keys_2"][0].reshape(-1, PEER_KEYS, P).transpose(2, 0, 1)),
        "ssd_d_row": inputs["ssd_d_2"], "ssd_g_row": inputs["ssd_norm_w_2"], "dil_q_row": inputs["dil_q_norm_w_2"],
        "dil_k_row": inputs["dil_k_norm_w_2"], "mem_q_row": inputs["mem_q_norm_w_2"],
        "mem_k_row": inputs["mem_k_norm_w_2"], "ffn_g_row_2": inputs["norm_ffn_w_2"],
        "final_g_row": inputs["final_norm_g"].reshape(1, D),
        **{k: inputs[k] for k in ("mem_2", "w_in_2", "w_mem_kv_2", "w_ssd_br_2", "w_dil_br_2", "w_mem_br_2",
                                  "w_out_2", "peer_w_query_2", "peer_down_2", "peer_up_2")},
        "p_cols_1": np.ascontiguousarray(cat([
            channel_columns(inputs["mix_norm_g"][0]), channel_columns(inputs["ffn_norm_g"][0]),
            conv.reshape(P, -1), channel_columns(inputs["conv_b"][0]), gate_b], axis=1)),
        "decay_logit": inputs["ret_decay_logit"][0].reshape(1, 8),
        "ret_gn_row": inputs["ret_gn_g"], "mlstm_gn_row": inputs["mlstm_gn_g"], "ffn_g_row": inputs["ffn_norm_g"],
        **{k: inputs[k] for k in ("x", "meta_tokens", "w_in", "w_out", "w_router", "w_gate", "w_up", "w_down")},
    }


def kernel(**inputs):
    import concourse.bacc as bacc
    import numpy as np
    from concourse.bass_utils import run_bass_kernel_spmd

    nc = bacc.Bacc("TRN2", target_bir_lowering=False, num_devices=1)
    arrays, io = {}, {}
    for name, a in {**constants(), **layouts({k: np.asarray(v) for k, v in inputs.items()})}.items():
        arrays[f"in_{name}"] = np.ascontiguousarray(a)
        io[name] = nc.dram_tensor(f"in_{name}", a.shape, mybir.dt.from_np(a.dtype), kind="ExternalInput").ap()
    out = nc.dram_tensor("result", (1, SEQ, D), F32, kind="ExternalOutput").ap()
    two_blocks(nc, io, out[0])
    done = run_bass_kernel_spmd(nc, [arrays], core_ids=[0])
    return done.results[0]["result"]
```

```python
from contextlib import ExitStack, contextmanager

import concourse.bass as bass
from concourse import mybir

ALU = mybir.AluOpType
ACT = mybir.ActivationFunctionType
F32 = mybir.dt.float32
I32 = mybir.dt.int32
U32 = mybir.dt.uint32
F32R = mybir.dt.float32r
AX_X = mybir.AxisListType.X

P = 128
D = 1024
KD = D // P
SEQ = 512
META = 16
TOK = SEQ + META
HALF = TOK // 2
EPS = 1e-6
NEG = -1e30
NT = SEQ // P

X_TILES = [(i, P, META + P * i) for i in range(NT)]
META_TILE = (NT, META, 0)
ALL_TILES = X_TILES + [META_TILE]
BY_POSITION = [META_TILE] + X_TILES

HEADS = 4
MIX = D // 2
N_GATES = 4 * HEADS
CONV_K = 5
REL_BASE = 400
REL_W = REL_BASE + TOK

EXPERTS = 16
CAP = 2 * TOK // EXPERTS
D_FF = 128 * ((8 * D // 3 + 127) // 128)
SLOTS = EXPERTS * CAP
TOP_ROUNDS = (CAP + 7) // 8

COLS_1 = {}
for _name, _count in (("mix_g", KD), ("ffn_g", KD), ("conv_w", KD * CONV_K), ("conv_b", KD), ("gate_b", 4)):
    COLS_1[_name] = (sum(c for _, c in COLS_1.values()), _count)
COLS_1_N = sum(c for _, c in COLS_1.values())


class Stage:

    def __init__(self, nc, name):
        self.nc, self.name, self.stack = nc, name, ExitStack()

    def __enter__(self):
        return self

    def __exit__(self, kind, *_):
        if kind is None:
            self.stack.close()

    def sb(self, name, shape, dt=F32, side="left"):
        return self.stack.enter_context(self.nc.sbuf_tensor(f"{self.name}_{name}", shape, dt, side=side))

    def ps(self, name, shape, dt=F32):
        return self.stack.enter_context(self.nc.psum_tensor(f"{self.name}_{name}", shape, dt))

    def sem(self, name):
        return self.nc.alloc_semaphore(f"{self.name}_{name}")


@contextmanager
def own_semaphores(nc):
    before = nc.snapshot_sems()
    yield
    nc.clear_and_free_semaphores(nc.allocated_since(before))
    nc.all_engine_barrier()


class InOrder:

    def __init__(self, eng, sem):
        self.eng, self.sem, self.n = eng, sem, 0

    def __call__(self, ins):
        self.n += 1
        ins.then_inc(self.sem, 1)
        self.eng.wait_ge(self.sem, self.n)


def load(nc, name, pairs):
    with Stage(nc, name) as st:
        landed = st.sem("landed")
        with nc.Block() as block:

            @block.sync
            def _(sp):
                for dst, src in pairs:
                    sp.dma_start(dst, src).then_inc(landed, 16)
                sp.wait_ge(landed, 16 * len(pairs))


def normalise(nc, name, x, tiles, gain_col, ident, xT, gain_row=None, kept=None):
    n_tiles = len(tiles)
    with Stage(nc, name) as st:
        ssq = st.sb("ssq", [P, n_tiles])
        inv = st.sb("inv", [P, n_tiles])
        rstd = st.sb("rstd", [P, n_tiles])
        squares = st.sb("squares", [P, 2, D])
        scaled = st.sb("scaled", [P, 2, D])
        turned = st.ps("turned", [P, 2, D])
        cleared, squared, inverted, rooted = (st.sem(s) for s in ("cleared", "squared", "inverted", "rooted"))
        scale_done, turn_done, evac_done = st.sem("scale_done"), st.sem("turn_done"), st.sem("evac_done")
        dve_order = st.sem("dve_order")

        def row(n):
            i, rows, _ = tiles[n]
            return kept[:rows, i, :] if kept is not None else scaled[:rows, n % 2, :]

        with nc.Block() as block:

            @block.scalar
            def _(act):
                act.wait_ge(cleared, 1)
                for n, (i, rows, _) in enumerate(tiles):
                    if n >= 2:
                        act.wait_ge(squared, n - 1)
                    act.activation(squares[:rows, n % 2, :], x[:rows, i, :], ACT.Square,
                                   accum_out=ssq[:rows, n:n + 1]).then_inc(squared, 1)
                act.wait_ge(inverted, 1)
                act.activation(rstd[:, :], inv[:, :], ACT.Sqrt).then_inc(rooted, 1)

            @block.vector
            def _(dve):
                order = InOrder(dve, dve_order)
                dve.memset(ssq[:, :], 1.0).then_inc(cleared, 1)
                dve.wait_ge(squared, n_tiles)
                order(dve.tensor_scalar(ssq[:, :], ssq[:, :], 1.0 / D, EPS, ALU.mult, ALU.add))
                dve.reciprocal(inv[:, :], ssq[:, :]).then_inc(inverted, 1)
                dve.wait_ge(rooted, 1)

                def scale(n):
                    i, rows, _ = tiles[n]
                    if n >= 2 and kept is None:
                        dve.wait_ge(turn_done, n - 1)
                    if kept is None:
                        dve.tensor_scalar(row(n), x[:rows, i, :], rstd[:rows, n:n + 1], None,
                                          ALU.mult).then_inc(scale_done, 1)
                    else:
                        dve.scalar_tensor_tensor(row(n), x[:rows, i, :], rstd[:rows, n:n + 1],
                                                 gain_row[:rows, :], ALU.mult, ALU.mult).then_inc(scale_done, 1)

                def evacuate(n):
                    _, rows, col = tiles[n]
                    dve.wait_ge(turn_done, n + 1)
                    src = turned[:, n % 2, :].rearrange("p (k c) -> p k c", k=KD)[:, :, 0:rows]
                    if kept is None:
                        gain = gain_col.unsqueeze(2).broadcast_to([P, KD, rows])
                        dve.tensor_tensor(xT[:, :, col:col + rows], src, gain, ALU.mult).then_inc(evac_done, 1)
                    else:
                        dve.tensor_copy(xT[:, :, col:col + rows], src).then_inc(evac_done, 1)

                scale(0)
                for n in range(n_tiles):
                    if n + 1 < n_tiles:
                        scale(n + 1)
                    if xT is not None:
                        evacuate(n)
                dve.wait_ge(scale_done, n_tiles)

            @block.tensor
            def _(pe):
                for n, (_, rows, _) in enumerate(tiles if xT is not None else []):
                    pe.wait_ge(scale_done, n + 1)
                    if n >= 2:
                        pe.wait_ge(evac_done, n - 1)
                    for k in range(KD):
                        last = pe.transpose(turned[:, n % 2, k * P:k * P + rows],
                                            row(n)[:, k * P:(k + 1) * P], ident[:rows, :rows])
                    last.then_inc(turn_done, 1)


class Job:

    def __init__(self, kind, offset, width, emit, eng, col=0, rows=P, parts=1, tokens=SEQ, after=None):
        self.kind, self.offset, self.width, self.emit, self.eng = kind, offset, width, emit, eng
        self.col, self.rows, self.parts, self.tokens, self.after = col, rows, parts, tokens, after


def token_jobs(tiles, width, emit, eng="act"):
    return [Job("token", 0, width, (lambda nc, ps, i=i, rows=rows: emit(nc, i, rows, ps)), eng, col=col, rows=rows)
            for i, rows, col in tiles]


def halves(ap):
    return ap.rearrange("p (a b) -> p a b", a=2)


def project(nc, name, chunks, wide=512, k_max=KD):
    slots = 4
    jobs = [(c, job) for c, (_, _, js) in enumerate(chunks) for job in js]
    place = []
    taken = {"act": 0, "dve": 0}
    for _, job in jobs:
        taken[job.eng] += 1
        place.append((job.eng, taken[job.eng]))
    with Stage(nc, name) as st:
        weights = st.sb("weights", [P, 2, k_max, wide])
        out = st.ps("out", [P, slots, 2 * 512])
        w_landed = [st.sem("w_landed0"), st.sem("w_landed1")]
        w_used, product_done = st.sem("w_used"), st.sem("product_done")
        taken_by = {"act": st.sem("taken_by_act"), "dve": st.sem("taken_by_dve")}

        def view(n, job):
            if job.kind == "token":
                return out[:job.rows, n % slots, 0:job.width]
            each = job.tokens // job.parts
            v = out[:job.width, n % slots, :].rearrange("p (a b) -> p a b", a=2)
            return v[:, 0:job.parts, 0:each] if job.parts > 1 else v[:, 0, 0:each]

        with nc.Block() as block:

            @block.sync
            def _(sp):
                for c, (w, _, _) in enumerate(chunks):
                    if c >= 2:
                        sp.wait_ge(w_used, c - 1)
                    kp, nk, cols = w.shape
                    sp.dma_start(weights[:kp, c % 2, 0:nk, 0:cols], w).then_inc(w_landed[c % 2], 16)

            @block.tensor
            def _(pe):
                last_of_chunk = {c: max(n for n, (cc, _) in enumerate(jobs) if cc == c) for c in range(len(chunks))}
                for n, (c, job) in enumerate(jobs):
                    w, source, _ = chunks[c]
                    kp, nk, _ = w.shape
                    pe.wait_ge(w_landed[c % 2], 16 * (c // 2 + 1))
                    if n >= slots:
                        eng, count = place[n - slots]
                        pe.wait_ge(taken_by[eng], count)
                    for a in range(job.parts):
                        each = job.tokens // job.parts
                        for k in range(nk):
                            if job.kind == "token":
                                last = pe.matmul(out[:job.rows, n % slots, 0:job.width],
                                                 source(k)[:, job.col:job.col + job.rows],
                                                 weights[:kp, c % 2, k, job.offset:job.offset + job.width],
                                                 start=(k == 0), stop=(k == nk - 1))
                            else:
                                last = pe.matmul(out[:job.width, n % slots, a * 512:a * 512 + each],
                                                 weights[:kp, c % 2, k, job.offset:job.offset + job.width],
                                                 source(k)[:, job.col + a * each:job.col + (a + 1) * each],
                                                 start=(k == 0), stop=(k == nk - 1))
                    last.then_inc(product_done, 1)
                    if n == last_of_chunk[c]:
                        pe.wait_ge(product_done, n + 1)
                        pe.sem_inc(w_used, 1)

            def take_out(engine, which):
                for n, (_, job) in enumerate(jobs):
                    if job.eng != which:
                        continue
                    engine.wait_ge(product_done, n + 1)
                    if job.after is not None:
                        eng, count = place[job.after]
                        engine.wait_ge(taken_by[eng], count)
                    job.emit(nc, view(n, job)).then_inc(taken_by[which], 1)

            @block.scalar
            def _(act):
                take_out(act, "act")

            @block.vector
            def _(dve):
                take_out(dve, "dve")


def head_norm(dve, order, act_sem, dve_sem, y, tiles, stats, moments, inv):
    for n, (i, rows, _) in enumerate(tiles):
        for h in range(HEADS):
            c = n * HEADS + h
            order(dve.bn_stats(stats[:rows, c, :], y[:rows, i, h * P:(h + 1) * P]))
            order(dve.bn_aggr(moments[:rows, c, :], stats[:rows, c, :]))
    order(dve.tensor_scalar(inv[:, :], moments[:, :, 1], EPS, None, ALU.add))
    dve.reciprocal(inv[:, :], inv[:, :]).then_inc(dve_sem, 1)
    dve.wait_ge(act_sem, 1)
    for n, (i, rows, _) in enumerate(tiles):
        for h in range(HEADS):
            c = n * HEADS + h
            last = dve.tensor_scalar(y[:rows, i, h * P:(h + 1) * P], y[:rows, i, h * P:(h + 1) * P],
                                     moments[:rows, c, 0:1], inv[:rows, c:c + 1], ALU.subtract, ALU.mult)
            order(last)


def retention(nc, io, rqk, rv, rg, y):
    scale = float(P) ** -0.5
    n_t = len(ALL_TILES)
    with Stage(nc, "ret") as st:
        cos = st.sb("cos", [P, TOK])
        sin = st.sb("sin", [P, TOK])
        swapped = st.sb("swapped", [P, HEADS, TOK])
        ahead = st.sb("ahead", [P, REL_W])
        behind = st.sb("behind", [P, REL_W])
        diag = st.sb("diag", [P, REL_W])
        arg = st.sb("arg", [P, REL_W])
        decay = st.sb("decay", [P, 2, REL_W])
        logit = st.sb("logit", [P, 8])
        lg = st.sb("lg", [P, 8])
        tmp8 = st.sb("tmp8", [P, 8])
        gn = st.sb("gn", [P, MIX])
        weighted = st.sb("weighted", [P, 2, n_t, TOK])
        stats = st.sb("stats", [P, n_t * HEADS, 6])
        moments = st.sb("moments", [P, n_t * HEADS, 2])
        inv = st.sb("inv", [P, n_t * HEADS])
        scores = st.ps("scores", [P, 2, 1024])
        mixed = st.ps("mixed", [P, 4, 512])
        landed, rot_half, rotated, abs_done, soft_done, arg_done = (
            st.sem(s) for s in ("landed", "rot_half", "rotated", "abs_done", "soft_done", "arg_done"))
        exp_done, decay_ready, scored, weighted_ready, mix_done, mix_out = (
            st.sem(s) for s in ("exp_done", "decay_ready", "scored", "weighted_ready", "mix_done", "mix_out"))
        var_ready, root_ready, dve_order, act_order = (
            st.sem(s) for s in ("var_ready", "root_ready", "dve_order", "act_order"))

        with nc.Block() as block:

            @block.sync
            def _(sp):
                for dst, src in ((cos[:, :], io["c_cos"]), (sin[:, :], io["c_sin"]), (ahead[:, :], io["c_ahead"]),
                                 (behind[:, :], io["c_behind"]), (diag[:, :], io["c_diag"]),
                                 (logit[:, :], io["decay_logit"].partition_broadcast(P)),
                                 (gn[:, :], io["ret_gn_row"].partition_broadcast(P))):
                    sp.dma_start(dst, src).then_inc(landed, 16)
                sp.wait_ge(landed, 7 * 16)

            @block.scalar
            def _(act):
                order = InOrder(act, act_order)
                for g in range(2):
                    if g:
                        act.wait_ge(rotated, 1)
                    order(act.copy(swapped[0:64, :, :], rqk[64:P, g * HEADS:(g + 1) * HEADS, :]))
                    act.copy(swapped[64:P, :, :], rqk[0:64, g * HEADS:(g + 1) * HEADS, :]).then_inc(rot_half, 1)
                act.wait_ge(abs_done, 1)
                order(act.activation(tmp8[:, :], tmp8[:, :], ACT.Exp, scale=-1.0))
                act.activation(tmp8[:, :], tmp8[:, :], ACT.Ln, bias=1.0).then_inc(soft_done, 1)
                for h in range(HEADS):
                    act.wait_ge(arg_done, h + 1)
                    act.activation(arg[:, :], arg[:, :], ACT.Exp).then_inc(exp_done, 1)
                    for n, (i, rows, _) in enumerate(ALL_TILES):
                        m = h * n_t + n
                        act.wait_ge(mix_done, m + 1)
                        act.copy(y[:rows, i, h * P:(h + 1) * P], mixed[:rows, m % 4, 0:P]).then_inc(mix_out, 1)
                act.wait_ge(var_ready, 1)
                act.activation(inv[:, :], inv[:, :], ACT.Sqrt).then_inc(root_ready, 1)

            @block.vector
            def _(dve):
                order = InOrder(dve, dve_order)
                order(dve.memset(moments[:, :, :], 1.0))
                dve.wait_ge(landed, 7 * 16)
                for g in range(2):
                    x = rqk[:, g * HEADS:(g + 1) * HEADS, :]
                    dve.wait_ge(rot_half, g + 1)
                    order(dve.tensor_tensor(x, x, cos[:, :].unsqueeze(1).broadcast_to([P, HEADS, TOK]), ALU.mult))
                    order(dve.tensor_tensor(swapped[:, :, :], swapped[:, :, :],
                                            sin[:, :].unsqueeze(1).broadcast_to([P, HEADS, TOK]), ALU.mult))
                    dve.tensor_tensor(x, x, swapped[:, :, :], ALU.add).then_inc(rotated, 1)
                dve.scalar_tensor_tensor(tmp8[:, :], logit[:, :], -1.0, logit[:, :], ALU.mult,
                                         ALU.max).then_inc(abs_done, 1)
                dve.wait_ge(soft_done, 1)
                order(dve.scalar_tensor_tensor(lg[:, :], logit[:, :], 0.0, tmp8[:, :], ALU.min, ALU.subtract))
                for h in range(HEADS):
                    order(dve.tensor_scalar(arg[:, :], ahead[:, :], lg[:, h:h + 1], None, ALU.mult))
                    dve.scalar_tensor_tensor(arg[:, :], behind[:, :], lg[:, HEADS + h:HEADS + h + 1], arg[:, :],
                                             ALU.mult, ALU.add).then_inc(arg_done, 1)
                    dve.wait_ge(exp_done, h + 1)
                    if h >= 1:
                        dve.wait_ge(weighted_ready, n_t * h)
                    dve.tensor_tensor(decay[:, h % 2, :], arg[:, :], diag[:, :], ALU.mult).then_inc(decay_ready, 1)
                    dve.wait_ge(decay_ready, h + 1)
                    for n, (_, rows, col) in enumerate(ALL_TILES):
                        m = h * n_t + n
                        dve.wait_ge(scored, m + 1)
                        if h >= 2:
                            dve.wait_ge(mix_done, n_t * (h - 1))
                        first = REL_BASE - col
                        dve.scalar_tensor_tensor(
                            halves(weighted[:rows, h % 2, n, :]),
                            scores[:rows, m % 2, :].rearrange("p (a b) -> p a b", a=2)[:, :, 0:HALF], scale,
                            halves(decay[:rows, h % 2, first:first + TOK]), ALU.mult, ALU.mult,
                        ).then_inc(weighted_ready, 1)
                dve.wait_ge(mix_out, n_t * HEADS)
                head_norm(dve, order, root_ready, var_ready, y, ALL_TILES, stats, moments, inv)
                for i, rows, _ in ALL_TILES:
                    order(dve.tensor_tensor(y[:rows, i, 0:MIX], y[:rows, i, 0:MIX], gn[:rows, :], ALU.mult))
                    order(dve.tensor_tensor(y[:rows, i, 0:MIX], y[:rows, i, 0:MIX], rg[:rows, i, :], ALU.mult))

            @block.tensor
            def _(pe):
                pe.wait_ge(rotated, 2)
                for h in range(HEADS):
                    for n, (_, rows, col) in enumerate(ALL_TILES):
                        m = h * n_t + n
                        if m >= 2:
                            pe.wait_ge(weighted_ready, m - 1)
                        for a in range(2):
                            last = pe.matmul(scores[:rows, m % 2, a * 512:a * 512 + HALF],
                                             rqk[:, HEADS + h, col:col + rows],
                                             rqk[:, h, a * HALF:(a + 1) * HALF], start=True, stop=True)
                        last.then_inc(scored, 1)
                    pe.wait_ge(weighted_ready, n_t * (h + 1))
                    for n, (_, rows, col) in enumerate(ALL_TILES):
                        m = h * n_t + n
                        if m >= 4:
                            pe.wait_ge(mix_out, m - 3)
                        for s, (si, srows, _) in enumerate(ALL_TILES):
                            last = pe.matmul(mixed[:rows, m % 4, 0:P], weighted[:srows, h % 2, s, col:col + rows],
                                             rv[:srows, si, h * P:(h + 1) * P],
                                             start=(s == 0), stop=(s == n_t - 1))
                        last.then_inc(mix_done, 1)


def mlstm_gates(nc, io, cols, gates, ident, g_col, exp_col, max_rows, scratch):
    with Stage(nc, "mlg") as st:
        ones = st.sb("ones", [HEADS, TOK])
        soft = st.sb("soft", [HEADS, 2, TOK])
        lf = st.sb("lf", [HEADS, 2, TOK])
        run = st.sb("run", [HEADS, 2, TOK])
        rows4 = st.sb("rows4", [HEADS, 4, TOK])
        top = st.sb("top", [HEADS, 2, TOK])
        turned = st.ps("turned", [P, len(ALL_TILES), 16])
        abs_done, soft_done, top_done, rows_done, turn_done, copied, stored, landed, dve_order, act_order = (
            st.sem(s) for s in ("abs_done", "soft_done", "top_done", "rows_done", "turn_done", "copied", "stored",
                                "landed", "dve_order", "act_order"))
        first = COLS_1["gate_b"][0]

        with nc.Block() as block:

            @block.vector
            def _(dve):
                order = InOrder(dve, dve_order)
                order(dve.memset(ones[:, :], 1.0))
                for g in range(4):
                    order(dve.tensor_scalar(gates[:, g, :], gates[:, g, :], cols[:HEADS, first + g:first + g + 1],
                                            None, ALU.add))
                forget = gates[:, 2:4, :]
                dve.scalar_tensor_tensor(soft[:, :, :], forget, -1.0, forget, ALU.mult,
                                         ALU.max).then_inc(abs_done, 1)
                dve.wait_ge(soft_done, 1)
                order(dve.scalar_tensor_tensor(lf[:, :, :], forget, 0.0, soft[:, :, :], ALU.min, ALU.subtract))
                for d in range(2):
                    def way(ap):
                        return ap if d == 0 else ap[:, ::-1]
                    order(dve.tensor_tensor_scan(way(run[:, d, :]), ones[:, :], way(lf[:, d, :]), 0.0,
                                                 ALU.mult, ALU.add))
                    order(dve.tensor_tensor(rows4[:, d, :], gates[:, d, :], run[:, d, :], ALU.subtract))
                    order(dve.tensor_tensor_scan(way(top[:, d, :]), ones[:, :], way(rows4[:, d, :]), 0.0,
                                                 ALU.mult, ALU.max))
                    order(dve.tensor_tensor(rows4[:, 2 + d, :], run[:, d, :], top[:, d, :], ALU.add))
                dve.sem_inc(rows_done, 1)
                dve.wait_ge(turn_done, 1)
                for i, rows, _ in ALL_TILES:
                    order(dve.tensor_copy(g_col[:rows, i, :], turned[:rows, i, 0:8]))
                dve.sem_inc(copied, 1)

            @block.scalar
            def _(act):
                order = InOrder(act, act_order)
                act.wait_ge(abs_done, 1)
                order(act.activation(soft[:, :, :], soft[:, :, :], ACT.Exp, scale=-1.0))
                act.activation(soft[:, :, :], soft[:, :, :], ACT.Ln, bias=1.0).then_inc(soft_done, 1)
                act.wait_ge(copied, 1)
                for i, rows, _ in ALL_TILES:
                    order(act.activation(exp_col[:rows, i, :], turned[:rows, i, 8:16], ACT.Exp, scale=-1.0))

            @block.tensor
            def _(pe):
                pe.wait_ge(rows_done, 1)
                for i, rows, col in ALL_TILES:
                    for g in range(4):
                        last = pe.transpose(turned[:rows, i, g * HEADS:(g + 1) * HEADS],
                                            rows4[:, g, col:col + rows], ident[:HEADS, :HEADS])
                last.then_inc(turn_done, 1)

            @block.sync
            def _(sp):
                sp.wait_ge(rows_done, 1)
                sp.dma_start(scratch, top[:, :, :]).then_inc(stored, 16)
                sp.wait_ge(stored, 16)
                for h in range(HEADS):
                    for d in range(2):
                        sp.dma_start(max_rows[:, 2 * h + d, :], scratch[h, d:d + 1, :].partition_broadcast(P)
                                     ).then_inc(landed, 16)
                sp.wait_ge(landed, 16 * 8)


def conv_silu(nc, name, padded, n_tiles, taps, tokens, weight, bias, out):
    with Stage(nc, name) as st:
        acc = st.sb("acc", [P, 2, tokens])
        conv_done, silu_done, dve_order = st.sem("conv_done"), st.sem("silu_done"), st.sem("dve_order")

        with nc.Block() as block:

            @block.vector
            def _(dve):
                order = InOrder(dve, dve_order)
                for c in range(n_tiles):
                    if c >= 2:
                        dve.wait_ge(silu_done, c - 1)
                    a = acc[:, c % 2, :]
                    order(dve.tensor_scalar(a, padded[:, c, 0:tokens], weight(c, 0), bias(c), ALU.mult, ALU.add))
                    for j in range(1, taps):
                        ins = dve.scalar_tensor_tensor(a, padded[:, c, j:j + tokens], weight(c, j), a,
                                                       ALU.mult, ALU.add)
                        if j < taps - 1:
                            order(ins)
                    ins.then_inc(conv_done, 1)

            @block.scalar
            def _(act):
                for c in range(n_tiles):
                    act.wait_ge(conv_done, c + 1)
                    act.activation(out[:, c, 0:tokens], acc[:, c % 2, :], ACT.Silu).then_inc(silu_done, 1)
                act.wait_ge(silu_done, n_tiles)


def clear(nc, name, aps, value=0.0):
    with Stage(nc, name) as st:
        done = st.sem("done")
        with nc.Block() as block:

            @block.vector
            def _(dve):
                for ap in aps:
                    dve.memset(ap, value).then_inc(done, 1)
                dve.wait_ge(done, len(aps))


def mlstm(nc, io, qk, v1, mo, y, g_col, exp_col, max_rows):
    scale = float(P) ** -0.5
    order_of = BY_POSITION
    n_t = len(order_of)
    passes = [(h, d) for h in range(HEADS) for d in range(2)]
    with Stage(nc, "mls") as st:
        raw = st.sb("raw", [P, n_t, TOK])
        arg = st.sb("arg", [P, 3, TOK])
        weight = st.sb("weight", [P, 2, n_t, TOK])
        keep = st.sb("keep", [P, 2, P])
        gn = st.sb("gn", [P, MIX])
        den = st.sb("den", [P, 4])
        stats = st.sb("stats", [P, n_t * HEADS, 6])
        moments = st.sb("moments", [P, n_t * HEADS, 2])
        inv = st.sb("inv", [P, n_t * HEADS])
        scores = st.ps("scores", [P, 2, 1024])
        mixed = st.ps("mixed", [P, 4, 512])
        landed, scored, raw_ready, arg_ready, exp_ready, weight_ready, mix_done, mix_out = (
            st.sem(s) for s in ("landed", "scored", "raw_ready", "arg_ready", "exp_ready", "weight_ready",
                                "mix_done", "mix_out"))
        var_ready, root_ready, dve_order, act_order = (
            st.sem(s) for s in ("var_ready", "root_ready", "dve_order", "act_order"))

        def span(d, col, rows):
            return (col, TOK) if d == 0 else (0, col + rows)

        with nc.Block() as block:

            @block.sync
            def _(sp):
                sp.dma_start(keep[:, :, :], io["c_keep"]).then_inc(landed, 16)
                sp.dma_start(gn[:, :], io["mlstm_gn_row"].partition_broadcast(P)).then_inc(landed, 16)
                sp.wait_ge(landed, 32)

            @block.scalar
            def _(act):
                for p, (h, d) in enumerate(passes):
                    if d == 0:
                        if h >= 1:
                            act.wait_ge(weight_ready, n_t * p)
                        for n, (_, rows, _) in enumerate(order_of):
                            act.wait_ge(scored, h * n_t + n + 1)
                            act.activation(halves(raw[:rows, n, :]),
                                           scores[:rows, (h * n_t + n) % 2, :].rearrange(
                                               "p (a b) -> p a b", a=2)[:, :, 0:HALF],
                                           ACT.Copy, scale=scale).then_inc(raw_ready, 1)
                    for n, (_, rows, col) in enumerate(order_of):
                        m = p * n_t + n
                        lo, hi = span(d, col, rows)
                        act.wait_ge(arg_ready, m + 1)
                        act.activation(arg[:rows, m % 3, lo:hi], arg[:rows, m % 3, lo:hi], ACT.Exp,
                                       scale=-1.0).then_inc(exp_ready, 1)
                act.wait_ge(var_ready, 1)
                act.activation(inv[:, :], inv[:, :], ACT.Sqrt).then_inc(root_ready, 1)

            @block.vector
            def _(dve):
                order = InOrder(dve, dve_order)
                order(dve.memset(moments[:, :, :], 1.0))
                dve.wait_ge(landed, 32)

                def exponents(p, n):
                    h, d = passes[p]
                    i, rows, col = order_of[n]
                    m = p * n_t + n
                    lo, hi = span(d, col, rows)
                    if m >= 3:
                        dve.wait_ge(weight_ready, m - 2)
                    dve.tensor_scalar(arg[:rows, m % 3, lo:hi], max_rows[:rows, 2 * h + d, lo:hi],
                                      g_col[:rows, i, d * HEADS + h:d * HEADS + h + 1], 0.0,
                                      ALU.subtract, ALU.max).then_inc(arg_ready, 1)

                def weigh(p, n):
                    h, d = passes[p]
                    _, rows, col = order_of[n]
                    m = p * n_t + n
                    lo, hi = span(d, col, rows)
                    dve.wait_ge(exp_ready, m + 1)
                    if p >= 2:
                        dve.wait_ge(mix_done, n_t * (p - 1))
                    if n == 0:
                        dve.wait_ge(raw_ready, n_t * (h + 1))
                    order(dve.tensor_tensor(weight[:rows, p % 2, n, lo:hi], arg[:rows, m % 3, lo:hi],
                                            raw[:rows, n, lo:hi], ALU.mult))
                    dve.tensor_tensor(weight[:rows, p % 2, n, col:col + rows],
                                      weight[:rows, p % 2, n, col:col + rows], keep[:rows, d, 0:rows],
                                      ALU.mult).then_inc(weight_ready, 1)

                def take_out(p):
                    h, d = passes[p]
                    for n, (i, rows, _) in enumerate(order_of):
                        m = p * n_t + n
                        dve.wait_ge(mix_done, m + 1)
                        ps = mixed[:rows, m % 4, :]
                        c = den[:rows, 0:1]
                        out = y[:rows, i, h * P:(h + 1) * P]
                        order(dve.tensor_scalar(den[:rows, 1:2], ps[:, P:P + 1], -1.0, None, ALU.mult))
                        order(dve.tensor_tensor(c, ps[:, P:P + 1], den[:rows, 1:2], ALU.max))
                        order(dve.tensor_tensor(c, c, exp_col[:rows, i, d * HEADS + h:d * HEADS + h + 1], ALU.max))
                        order(dve.reciprocal(c, c))
                        if d == 0:
                            ins = dve.tensor_scalar(out, ps[:, 0:P], c, None, ALU.mult)
                        else:
                            ins = dve.scalar_tensor_tensor(out, ps[:, 0:P], c, out, ALU.mult, ALU.add)
                        ins.then_inc(mix_out, 1)
                        dve.wait_ge(mix_out, m + 1)

                for p in range(len(passes)):
                    exponents(p, 0)
                    exponents(p, 1)
                    for n in range(n_t):
                        if n + 2 < n_t:
                            exponents(p, n + 2)
                        weigh(p, n)
                    if p >= 1:
                        take_out(p - 1)
                take_out(len(passes) - 1)
                for i, rows, _ in ALL_TILES:
                    order(dve.tensor_tensor(y[:rows, i, :], y[:rows, i, :], mo[:rows, i, :], ALU.mult))
                head_norm(dve, order, root_ready, var_ready, y, ALL_TILES, stats, moments, inv)
                for i, rows, _ in ALL_TILES:
                    order(dve.tensor_tensor(y[:rows, i, :], y[:rows, i, :], gn[:rows, :], ALU.mult))

            @block.tensor
            def _(pe):
                def score(h):
                    for n, (_, rows, col) in enumerate(order_of):
                        m = h * n_t + n
                        if m >= 2:
                            pe.wait_ge(raw_ready, m - 1)
                        for a in range(2):
                            last = pe.matmul(scores[:rows, m % 2, a * 512:a * 512 + HALF],
                                             qk[:, HEADS + h, col:col + rows],
                                             qk[:, h, a * HALF:(a + 1) * HALF], start=True, stop=True)
                        last.then_inc(scored, 1)

                def mix(p):
                    h, d = passes[p]
                    pe.wait_ge(weight_ready, n_t * (p + 1))
                    for n, (_, rows, col) in enumerate(order_of):
                        m = p * n_t + n
                        if m >= 4:
                            pe.wait_ge(mix_out, m - 3)
                        keys = range(0, n + 1) if d == 0 else range(n, n_t)
                        for s in keys:
                            si, srows, _ = order_of[s]
                            last = pe.matmul(mixed[:rows, m % 4, 0:P + 1],
                                             weight[:srows, p % 2, s, col:col + rows], v1[:srows, si, h, :],
                                             start=(s == keys[0]), stop=(s == keys[-1]))
                        last.then_inc(mix_done, 1)

                score(0)
                for h in range(HEADS):
                    mix(2 * h)
                    if h + 1 < HEADS:
                        score(h + 1)
                    mix(2 * h + 1)


def turn_rows(nc, name, x, tiles, ident, xT, k_tiles=KD):
    with Stage(nc, name) as st:
        turned = st.ps("turned", [P, 2, D])
        turn_done, taken = st.sem("turn_done"), st.sem("taken")
        with nc.Block() as block:

            @block.tensor
            def _(pe):
                for n, (i, rows, _) in enumerate(tiles):
                    if n >= 2:
                        pe.wait_ge(taken, n - 1)
                    for k in range(k_tiles):
                        last = pe.transpose(turned[:, n % 2, k * P:k * P + rows], x[:rows, i, k * P:(k + 1) * P],
                                            ident[:rows, :rows])
                    last.then_inc(turn_done, 1)

            @block.vector
            def _(dve):
                for n, (_, rows, col) in enumerate(tiles):
                    dve.wait_ge(turn_done, n + 1)
                    dve.tensor_copy(xT[:, :, col:col + rows],
                                    turned[:, n % 2, 0:k_tiles * P].rearrange("p (k c) -> p k c", k=k_tiles)[:, :, 0:rows]
                                    ).then_inc(taken, 1)


def route(nc, io, u, uT, ident, xs, slot_gate, scratch):
    n_t = len(ALL_TILES)
    parts = [(0, 6), (6, 5), (11, 5)]
    assert sum(n for _, n in parts) == EXPERTS
    with Stage(nc, "route") as st:
        w = st.sb("w", [P, KD, EXPERTS])
        logits = st.sb("logits", [P, n_t, EXPERTS])
        top1 = st.sb("top1", [P, n_t])
        total = st.sb("total", [P, n_t])
        affT = st.sb("affT", [EXPERTS, TOK])
        vals = st.sb("vals", [EXPERTS, TOP_ROUNDS * 8])
        idx = st.sb("idx", [EXPERTS, TOP_ROUNDS * 8], U32)
        idx_f = st.sb("idx_f", [EXPERTS, TOP_ROUNDS * 8])
        idx_all = st.sb("idx_all", [P, SLOTS])
        token_id = st.sb("token_id", [P, n_t])
        onehot = st.sb("onehot", [P, n_t, SLOTS], F32R)
        u_high = st.sb("u_high", [P, n_t, D], F32R)
        u_low = st.sb("u_low", [P, n_t, D], F32R)
        small = st.ps("small", [P, 512])
        turned = st.ps("turned", [P, 1024])
        gathered = st.ps("gathered", [P, 4, 512])
        landed, logits_done, shifted, exp_done, aff_done, turn_done, idx_done, stored, spread = (
            st.sem(s) for s in ("landed", "logits_done", "shifted", "exp_done", "aff_done", "turn_done", "idx_done",
                                "stored", "spread"))
        slot_turned, onehot_done, gather_done, act_taken, dve_taken, dve_order, act_order, u_high_done = (
            st.sem(s) for s in ("slot_turned", "onehot_done", "gather_done", "act_taken", "dve_taken", "dve_order",
                                "act_order", "u_high_done"))
        pieces = [(k, c) for k in range(KD) for c in parts]

        def part_of(m, k, c):
            first, n = c
            return (xs[:, first:first + n, k, :],
                    gathered[:, m % 4, 0:n * CAP].rearrange("p (e c) -> p e c", e=n))

        with nc.Block() as block:

            @block.sync
            def _(sp):
                sp.dma_start(w[:, :, :], io["w_router"][0].rearrange("(k p) e -> p k e", p=P)).then_inc(landed, 16)
                sp.dma_start(token_id[:, :], io["c_token_id"]).then_inc(landed, 16)
                sp.wait_ge(idx_done, 1)
                sp.dma_start(scratch, idx_f[:, 0:CAP]).then_inc(stored, 16)
                sp.wait_ge(stored, 16)
                sp.dma_start(idx_all[:, :], scratch.rearrange("e c -> (e c)").unsqueeze(0).partition_broadcast(P)
                             ).then_inc(spread, 16)
                sp.wait_ge(spread, 16)
                sp.wait_ge(landed, 32)

            @block.tensor
            def _(pe):
                pe.wait_ge(landed, 32)
                for n, (i, rows, col) in enumerate(ALL_TILES):
                    for k in range(KD):
                        last = pe.matmul(small[:rows, i * EXPERTS:(i + 1) * EXPERTS], uT[:, k, col:col + rows],
                                         w[:, k, :], start=(k == 0), stop=(k == KD - 1))
                last.then_inc(logits_done, 1)
                pe.wait_ge(aff_done, 1)
                for i, rows, col in ALL_TILES:
                    at = 512 if i == NT else i * P
                    last = pe.transpose(turned[:EXPERTS, at:at + rows], logits[:rows, i, :], ident[:rows, :rows])
                last.then_inc(turn_done, 1)
                pe.wait_ge(idx_done, 1)
                pe.transpose(small[:CAP, 160:160 + EXPERTS], vals[:, 0:CAP],
                             ident[:EXPERTS, :EXPERTS]).then_inc(slot_turned, 1)
                pe.wait_ge(onehot_done, 1)
                for m, (k, c) in enumerate(pieces):
                    if m >= 4:
                        pe.wait_ge(act_taken if m % 2 == 0 else dve_taken, m // 2 - 1)
                    first, n = c
                    for i, rows, _ in ALL_TILES:
                        for part in (u_high, u_low):
                            last = pe.matmul(gathered[:, m % 4, 0:n * CAP], part[:rows, i, k * P:(k + 1) * P],
                                             onehot[:rows, i, first * CAP:(first + n) * CAP],
                                             start=(i == 0 and part is u_high), stop=(i == NT and part is u_low))
                    last.then_inc(gather_done, 1)

            @block.vector
            def _(dve):
                order = InOrder(dve, dve_order)
                order(dve.memset(logits[:, :, :], 0.0))
                dve.wait_ge(logits_done, 1)
                for i, rows, _ in ALL_TILES:
                    order(dve.tensor_copy(logits[:rows, i, :], small[:rows, i * EXPERTS:(i + 1) * EXPERTS]))
                order(dve.tensor_reduce(top1[:, :], logits[:, :, :], AX_X, ALU.max))
                dve.tensor_tensor(logits[:, :, :], logits[:, :, :],
                                  top1[:, :].unsqueeze(2).broadcast_to([P, n_t, EXPERTS]),
                                  ALU.subtract).then_inc(shifted, 1)
                dve.wait_ge(exp_done, 1)
                order(dve.tensor_reduce(total[:, :], logits[:, :, :], AX_X, ALU.add))
                order(dve.reciprocal(total[:, :], total[:, :]))
                dve.tensor_tensor(logits[:, :, :], logits[:, :, :],
                                  total[:, :].unsqueeze(2).broadcast_to([P, n_t, EXPERTS]),
                                  ALU.mult).then_inc(aff_done, 1)
                dve.wait_ge(turn_done, 1)
                order(dve.tensor_copy(affT[:, META:TOK], turned[:EXPERTS, 0:SEQ]))
                order(dve.tensor_copy(affT[:, 0:META], turned[:EXPERTS, 512:512 + META]))
                for r in range(TOP_ROUNDS):
                    eight = slice(8 * r, 8 * r + 8)
                    order(dve.max(vals[:, eight], affT[:, :]))
                    order(dve.max_index(idx[:, eight], vals[:, eight], affT[:, :]))
                    if r + 1 < TOP_ROUNDS:
                        order(dve.match_replace(affT[:, :], vals[:, eight], affT[:, :], -1.0))
                dve.tensor_copy(idx_f[:, :], idx[:, :]).then_inc(idx_done, 1)
                dve.wait_ge(slot_turned, 1)
                order(dve.tensor_copy(slot_gate[:, :], small[:CAP, 160:160 + EXPERTS]))
                dve.wait_ge(spread, 16)
                for i, rows, _ in ALL_TILES:
                    order(dve.tensor_scalar(onehot[:rows, i, :], idx_all[:rows, :], token_id[:rows, i:i + 1], None,
                                            ALU.is_equal))
                for i, rows, _ in ALL_TILES:
                    dve.wait_ge(u_high_done, i + 1)
                    order(dve.tensor_tensor(u_low[:rows, i, :], u[:rows, i, :], u_high[:rows, i, :].bitcast(F32),
                                            ALU.subtract))
                dve.sem_inc(onehot_done, 1)
                for m, (k, c) in enumerate(pieces):
                    if m % 2:
                        dve.wait_ge(gather_done, m + 1)
                        dve.tensor_copy(*part_of(m, k, c)).then_inc(dve_taken, 1)

            @block.scalar
            def _(act):
                order = InOrder(act, act_order)
                act.wait_ge(shifted, 1)
                act.activation(logits[:, :, :], logits[:, :, :], ACT.Exp).then_inc(exp_done, 1)
                for i, rows, _ in ALL_TILES:
                    act.copy(u_high[:rows, i, :], u[:rows, i, :]).then_inc(u_high_done, 1)
                for m, (k, c) in enumerate(pieces):
                    if m % 2 == 0:
                        act.wait_ge(gather_done, m + 1)
                        act.copy(*part_of(m, k, c)).then_inc(act_taken, 1)


FF_CHUNK = 512
FF_CHUNKS = [(c, min(FF_CHUNK, D_FF - c)) for c in range(0, D_FF, FF_CHUNK)]
FF_N = len(FF_CHUNKS)
FF_BLOCKS = [b for c in range(FF_N) for b in [("gate", c), ("up", c)] + ([("down", c - 2)] if c >= 2 else [])]
FF_BLOCKS += [("down", FF_N - 2), ("down", FF_N - 1)]
FF_NB = len(FF_BLOCKS)
FF_RING = 3


def split_matmul(pe, out, hi_l, lo_l, hi_r, lo_r, start, stop):
    pe.matmul(out, hi_l, hi_r, start=start, stop=False)
    pe.matmul(out, lo_l, hi_r, start=False, stop=False)
    return pe.matmul(out, hi_l, lo_r, start=False, stop=stop)


def expert_ffn(nc, io, xs_dram, slot_gate, ident, y_dram):
    assert FF_NB % FF_RING == 0 and FF_N % 2 == 0
    per_slot = FF_NB // FF_RING
    at = {b: q for q, b in enumerate(FF_BLOCKS)}
    tensors = {
        "gate": io["w_gate"][0].rearrange("e (k p) f -> e p k f", p=P),
        "up": io["w_up"][0].rearrange("e (k p) f -> e p k f", p=P),
        "down": io["w_down"][0].rearrange("e (t p) d -> e p t d", p=P),
    }

    def shape_of(q):
        kind, c = FF_BLOCKS[q]
        width = FF_CHUNKS[c][1]
        return (KD, width) if kind != "down" else (width // P, D)

    def block_of(ring, q):
        a, b = shape_of(q)
        return ring[:, q % FF_RING, 0:a * b].rearrange("p (a b) -> p a b", a=a)

    def half_of(ring, q, h):
        a, b = shape_of(q)
        n = a * b // 2
        return ring[:, q % FF_RING, h * n:(h + 1) * n]

    with Stage(nc, "ffn") as st:
        raw = st.sb("raw", [P, FF_RING, KD * FF_CHUNK])
        high = st.sb("high", [P, FF_RING, KD * FF_CHUNK], F32R)
        low = st.sb("low", [P, FF_RING, KD * FF_CHUNK], F32R)
        x_raw = st.sb("x_raw", [P, KD, CAP])
        x_high = st.sb("x_high", [P, KD, CAP], F32R)
        x_low = st.sb("x_low", [P, KD, CAP], F32R)
        silu = st.sb("silu", [CAP, 2, FF_CHUNK])
        hidden = st.sb("hidden", [CAP, 2, FF_CHUNK])
        t_high = st.sb("t_high", [P, 2, FF_CHUNK // P * CAP], F32R)
        t_low = st.sb("t_low", [P, 2, FF_CHUNK // P * CAP], F32R)
        result = st.sb("result", [CAP, D])
        gate_p = st.ps("gate_p", [P, 2, 512])
        up_p = st.ps("up_p", [P, 2, 512])
        turn_p = st.ps("turn_p", [P, 2, 512])
        down_p = st.ps("down_p", [P, D])
        raw_in = [st.sem(f"raw_in{s}") for s in range(FF_RING)]
        high_done, low_done, block_used = (st.sem(s) for s in ("high_done", "low_done", "block_used"))
        x_in, x_high_done, x_low_done = (st.sem(s) for s in ("x_in", "x_high_done", "x_low_done"))
        silu_done, hidden_done, turn_done, t_high_done, t_low_done, result_out, y_stored, result_free = (
            st.sem(s) for s in ("silu_done", "hidden_done", "turn_done", "t_high_done", "t_low_done",
                                "result_out", "y_stored", "result_free"))

        def used(e, kind, c):
            return e * FF_NB + at[(kind, c)] + 1 + FF_RING

        def follow_ups(q):
            steps = []
            for c in range(FF_N):
                if q == at[("up", c)] + 2:
                    steps.append(("hidden", c))
                    if c >= 1:
                        steps.append(("turned", c - 1))
            if q == FF_NB - 1:
                steps.append(("turned", FF_N - 1))
            return steps

        with nc.Block() as block:

            @block.sync
            def _(sp):
                with sp.Fori(0, EXPERTS) as e:
                    for q, (kind, c) in enumerate(FF_BLOCKS):
                        first, width = FF_CHUNKS[c]
                        src = tensors[kind][bass.ds(e, 1)].squeeze(0)
                        if kind == "down":
                            src = src[:, first // P:(first + width) // P, :]
                        else:
                            src = src[:, :, first:first + width]
                        sp.wait_ge(low_done, (e * FF_NB + q) * 2 + 2)
                        sp.dma_start(block_of(raw, q), src).then_inc(raw_in[q % FF_RING], 16)

            @block.gpsimd
            def _(pool):
                pool.sem_inc(result_free, 1)

                def load_x(e):
                    pool.wait_ge(x_low_done, e + 1)
                    pool.dma_start(x_raw[:, :, :].rearrange("p k c -> p (k c)"),
                                   xs_dram[:, bass.ds(e * KD * CAP, KD * CAP)]).then_inc(x_in, 16)

                def store(e):
                    pool.wait_ge(result_out, 2 * e + 4)
                    pool.dma_start(y_dram[bass.ds(e, 1), :, :].squeeze(0), result[:, :]).then_inc(y_stored, 16)
                    pool.wait_ge(y_stored, e * 16 + 16)
                    pool.sem_inc(result_free, 1)

                load_x(0)
                with pool.Fori(1, EXPERTS) as e:
                    load_x(e)
                    store(e - 1)
                store(EXPERTS - 1)

            @block.tensor
            def _(pe):
                pe.sem_inc(block_used, FF_RING)
                pe.sem_inc(turn_done, 2)
                with pe.Fori(0, EXPERTS) as e:

                    def split_in(q):
                        pe.wait_ge(high_done, (e * FF_NB + q) * 2 + 2)
                        pe.wait_ge(low_done, (e * FF_NB + q + FF_RING) * 2 + 2)

                    def columns(kind, c, psum):
                        q, s, width = at[(kind, c)], c % 2, FF_CHUNKS[c][1]
                        split_in(q)
                        hi, lo = block_of(high, q), block_of(low, q)
                        for k in range(KD):
                            last = split_matmul(pe, psum[:CAP, s, 0:width], x_high[:, k, :], x_low[:, k, :],
                                                hi[:, k, :], lo[:, k, :], start=(k == 0), stop=(k == KD - 1))
                        last.then_inc(block_used, 1)

                    def turn(c):
                        s, width = c % 2, FF_CHUNKS[c][1]
                        pe.wait_ge(hidden_done, e * FF_N + c + 3)
                        pe.wait_ge(t_low_done, e * FF_N + c + 1)
                        for t in range(width // P):
                            last = pe.transpose(turn_p[:, s, t * CAP:(t + 1) * CAP],
                                                hidden[:, s, t * P:(t + 1) * P], ident[:CAP, :CAP])
                        last.then_inc(turn_done, 1)

                    def down(c):
                        q, s, width = at[("down", c)], c % 2, FF_CHUNKS[c][1]
                        if c == 0:
                            pe.wait_ge(result_out, 2 * e + 2)
                        split_in(q)
                        pe.wait_ge(t_high_done, e * FF_N + c + 1)
                        pe.wait_ge(t_low_done, e * FF_N + c + 3)
                        hi, lo = block_of(high, q), block_of(low, q)
                        for t in range(width // P):
                            mine = slice(t * CAP, (t + 1) * CAP)
                            for half in range(2):
                                cols = slice(half * 512, (half + 1) * 512)
                                last = split_matmul(pe, down_p[:CAP, cols], t_high[:, s, mine], t_low[:, s, mine],
                                                    hi[:, t, cols], lo[:, t, cols],
                                                    start=(c == 0 and t == 0),
                                                    stop=(c == FF_N - 1 and t == width // P - 1))
                        last.then_inc(block_used, 1)

                    pe.wait_ge(x_high_done, e + 1)
                    pe.wait_ge(x_low_done, e + 2)
                    for c in range(FF_N):
                        pe.wait_ge(hidden_done, e * FF_N + c + 1)
                        columns("gate", c, gate_p)
                        columns("up", c, up_p)
                        if c >= 1:
                            turn(c - 1)
                        if c >= 2:
                            down(c - 2)
                    turn(FF_N - 1)
                    down(FF_N - 2)
                    down(FF_N - 1)

            @block.scalar
            def _(act):
                act.sem_inc(result_out, 2)

                def take_result(e):
                    act.wait_ge(block_used, used(e, "down", FF_N - 1))
                    act.wait_ge(result_free, e + 1)
                    act.activation(result[:, 0:512], down_p[:CAP, 0:512], ACT.Copy,
                                   scale=slot_gate[:, bass.ds(e, 1)]).then_inc(result_out, 1)

                def expert(e, first=False):
                    for q in range(FF_NB):
                        act.wait_ge(block_used, e * FF_NB + q + 1)
                        act.wait_ge(raw_in[q % FF_RING], (e * per_slot + q // FF_RING) * 16 + 16)
                        for h in range(2):
                            act.copy(half_of(high, q, h), half_of(raw, q, h)).then_inc(high_done, 1)
                        if q == 0:
                            act.wait_ge(x_in, e * 16 + 16)
                            act.copy(x_high[:, :, :], x_raw[:, :, :]).then_inc(x_high_done, 1)
                        if q == FF_RING - 1 and not first:
                            take_result(e - 1)
                        for step, c in follow_ups(q):
                            s, width = c % 2, FF_CHUNKS[c][1]
                            if step == "hidden":
                                act.wait_ge(block_used, used(e, "gate", c))
                                act.wait_ge(hidden_done, e * FF_N + c + 1)
                                act.activation(silu[:, s, 0:width], gate_p[:CAP, s, 0:width], ACT.Silu
                                               ).then_inc(silu_done, 1)
                            else:
                                n = width // P * CAP
                                act.wait_ge(turn_done, e * FF_N + c + 3)
                                if c >= 2:
                                    act.wait_ge(block_used, used(e, "down", c - 2))
                                act.copy(t_high[:, s, 0:n], turn_p[:, s, 0:n]).then_inc(t_high_done, 1)

                expert(0, first=True)
                with act.Fori(1, EXPERTS) as e:
                    expert(e)
                take_result(EXPERTS - 1)

            @block.vector
            def _(dve):
                dve.sem_inc(hidden_done, 2)
                dve.sem_inc(t_low_done, 2)
                dve.sem_inc(low_done, 2 * FF_RING)
                dve.sem_inc(x_low_done, 1)

                def take_result(e):
                    dve.wait_ge(block_used, used(e, "down", FF_N - 1))
                    dve.wait_ge(result_free, e + 1)
                    dve.tensor_scalar(result[:, 512:D], down_p[:CAP, 512:D], slot_gate[:, bass.ds(e, 1)], None,
                                      ALU.mult).then_inc(result_out, 1)

                def expert(e, first=False):
                    for q in range(FF_NB):
                        for h in range(2):
                            dve.wait_ge(high_done, (e * FF_NB + q) * 2 + h + 1)
                            dve.tensor_tensor(half_of(low, q, h), half_of(raw, q, h),
                                              half_of(high, q, h).bitcast(F32), ALU.subtract).then_inc(low_done, 1)
                        if q == 0:
                            dve.wait_ge(x_high_done, e + 1)
                            dve.tensor_tensor(x_low[:, :, :], x_raw[:, :, :], x_high[:, :, :].bitcast(F32),
                                              ALU.subtract).then_inc(x_low_done, 1)
                        if q == FF_RING - 1 and not first:
                            take_result(e - 1)
                        for step, c in follow_ups(q):
                            s, width = c % 2, FF_CHUNKS[c][1]
                            if step == "hidden":
                                dve.wait_ge(block_used, used(e, "up", c))
                                dve.wait_ge(silu_done, e * FF_N + c + 1)
                                dve.wait_ge(turn_done, e * FF_N + c + 1)
                                dve.tensor_tensor(hidden[:, s, 0:width], silu[:, s, 0:width], up_p[:CAP, s, 0:width],
                                                  ALU.mult).then_inc(hidden_done, 1)
                            else:
                                n = width // P * CAP
                                dve.wait_ge(t_high_done, e * FF_N + c + 1)
                                dve.tensor_tensor(t_low[:, s, 0:n], turn_p[:, s, 0:n],
                                                  t_high[:, s, 0:n].bitcast(F32), ALU.subtract
                                                  ).then_inc(t_low_done, 1)

                expert(0, first=True)
                with dve.Fori(1, EXPERTS) as e:
                    expert(e)
                take_result(EXPERTS - 1)


SLOT_TILES = [(t, min(P, SLOTS - t * P)) for t in range((SLOTS + P - 1) // P)]


def combine(nc, io, h, idx_dram, y_dram):
    n_s = len(SLOT_TILES)
    with Stage(nc, "comb") as st:
        y = st.sb("y", [P, n_s, D])
        high = st.sb("high", [P, n_s, D], F32R)
        low = st.sb("low", [P, n_s, D], F32R)
        scatter = st.sb("scatter", [P, n_s, SEQ], F32R)
        ids = st.sb("ids", [P, SEQ])
        slot_tok = st.sb("slot_tok", [P, n_s])
        out = st.ps("out", [P, 2, D])
        ids_in = st.sem("ids_in")
        y_in = [st.sem(f"y_in{t}") for t in range(n_s)]
        high_done, low_done, scatter_done, sum_done, added = (
            st.sem(s) for s in ("high_done", "low_done", "scatter_done", "sum_done", "added"))
        slot_rows = idx_dram.rearrange("e c -> (e c)").unsqueeze(1)
        y_rows = y_dram.rearrange("e c d -> (e c) d")
        with nc.Block() as block:

            @block.sync
            def _(sp):
                sp.dma_start(ids[:, :], io["c_ids"].partition_broadcast(P)).then_inc(ids_in, 16)
                for t, rows in SLOT_TILES:
                    sp.dma_start(slot_tok[:rows, t:t + 1], slot_rows[t * P:t * P + rows, :]).then_inc(ids_in, 16)
                for t, rows in SLOT_TILES:
                    sp.dma_start(y[:rows, t, :], y_rows[t * P:t * P + rows, :]).then_inc(y_in[t], 16)

            @block.scalar
            def _(act):
                for t, rows in SLOT_TILES:
                    act.wait_ge(y_in[t], 16)
                    act.copy(high[:rows, t, :], y[:rows, t, :]).then_inc(high_done, 1)

            @block.vector
            def _(dve):
                dve.wait_ge(ids_in, 16 * (1 + n_s))
                for t, rows in SLOT_TILES:
                    dve.tensor_scalar(scatter[:rows, t, :], ids[:rows, :], slot_tok[:rows, t:t + 1], None,
                                      ALU.is_equal).then_inc(scatter_done, 1)
                    dve.wait_ge(high_done, t + 1)
                    dve.tensor_tensor(low[:rows, t, :], y[:rows, t, :], high[:rows, t, :].bitcast(F32),
                                      ALU.subtract).then_inc(low_done, 1)
                for i in range(NT):
                    dve.wait_ge(sum_done, i + 1)
                    dve.tensor_tensor(h[:, i, :], h[:, i, :], out[:, i % 2, :], ALU.add).then_inc(added, 1)

            @block.tensor
            def _(pe):
                pe.wait_ge(high_done, n_s)
                pe.wait_ge(low_done, n_s)
                pe.wait_ge(scatter_done, n_s)
                for i in range(NT):
                    if i >= 2:
                        pe.wait_ge(added, i - 1)
                    for half in range(2):
                        cols = slice(half * 512, (half + 1) * 512)
                        for t, rows in SLOT_TILES:
                            for part in (high, low):
                                last = pe.matmul(out[:, i % 2, cols], scatter[:rows, t, i * P:(i + 1) * P],
                                                 part[:rows, t, cols], start=(t == 0 and part is high),
                                                 stop=(t == n_s - 1 and part is low))
                    last.then_inc(sum_done, 1)


def first_block(nc, io, h, ident, dbg=None):
    w_in = io["w_in"][0].rearrange("(k p) c -> p k c", p=P)
    w_out = io["w_out"][0].rearrange("(k p) c -> p k c", p=P)
    max_dram = nc.dram_tensor("scratch_max", [HEADS, 2, TOK], F32).ap()
    idx_dram = nc.dram_tensor("scratch_idx", [EXPERTS, CAP], F32).ap()
    xs_dram = nc.dram_tensor("scratch_xs", [P, SLOTS * KD], F32).ap()
    y_dram = nc.dram_tensor("scratch_y", [EXPERTS, CAP, D], F32).ap()

    with Stage(nc, "b1") as st:
        cols = st.sb("cols", [P, COLS_1_N])
        load(nc, "load1", [(cols[:, :], io["p_cols_1"]), (ident[:, :], io["c_ident"]),
                           (h[:, 0:NT, :], io["x"][0].rearrange("(i p) d -> p i d", p=P)),
                           (h[0:META, NT, :], io["meta_tokens"])])

        def gain(name):
            a, n = COLS_1[name]
            return cols[:, a:a + n]

        with Stage(nc, "mix") as mx:
            y = mx.sb("y", [P, NT + 1, D])
            with Stage(nc, "mixin") as s1:
                uT = s1.sb("uT", [P, KD, TOK], side="right")
                normalise(nc, "norm1", h, ALL_TILES, gain("mix_g"), ident, uT)

                def source(k):
                    return uT[:, k, :]

                def chunk(index, jobs):
                    return (w_in[:, :, index * 512:(index + 1) * 512], source, jobs)

                def channel_jobs(dst, base, pad=0):
                    return [Job("channel", c * P, P,
                                (lambda nc, ps, c=c, eng=eng: (nc.scalar.copy if eng == "act" else nc.vector.tensor_copy)(
                                    halves(dst[:, base + c, pad:pad + TOK]), ps)),
                                eng, parts=2, tokens=TOK) for c, eng in enumerate(("act", "dve") * 2)]

                with Stage(nc, "retbuf") as s2:
                    rqk = s2.sb("rqk", [P, 2 * HEADS, TOK])
                    rv = s2.sb("rv", [P, NT + 1, MIX])
                    rg = s2.sb("rg", [P, NT + 1, MIX])
                    project(nc, "proj_ret", [
                        chunk(0, channel_jobs(rqk, 0)), chunk(1, channel_jobs(rqk, HEADS)),
                        chunk(2, token_jobs(ALL_TILES, MIX, lambda nc, i, r, ps: nc.vector.tensor_copy(
                            rv[:r, i, :], ps), "dve")),
                        chunk(3, token_jobs(ALL_TILES, MIX, lambda nc, i, r, ps: nc.scalar.activation(
                            rg[:r, i, :], ps, ACT.Silu))),
                    ])
                    retention(nc, io, rqk, rv, rg, y)
                    if dbg: dbg("yret", y[:, :, 0:MIX])

                qk = mx.sb("qk", [P, 2 * HEADS, TOK])
                v1 = mx.sb("v1", [P, NT + 1, HEADS, P + 1])
                mo = mx.sb("mo", [P, NT + 1, MIX])
                gates = mx.sb("gates", [HEADS, 4, TOK])
                with Stage(nc, "convbuf") as s2:
                    padded = s2.sb("padded", [P, KD, TOK + CONV_K - 1])
                    gate_jobs = [Job("channel", g * HEADS, HEADS,
                                     (lambda nc, ps, g=g: nc.vector.tensor_copy(halves(gates[:, g, :]), ps)),
                                     "dve", parts=2, tokens=TOK) for g in range(4)]
                    project(nc, "proj_ml", [
                        chunk(4, channel_jobs(padded, 0, 2)), chunk(5, channel_jobs(padded, HEADS, 2)),
                        chunk(6, token_jobs(ALL_TILES, MIX, lambda nc, i, r, ps: nc.vector.tensor_copy(
                            v1[:r, i, :, 0:P], ps.rearrange("p (h e) -> p h e", h=HEADS)), "dve")),
                        chunk(7, token_jobs(ALL_TILES, MIX, lambda nc, i, r, ps: nc.scalar.activation(
                            mo[:r, i, :], ps, ACT.Sigmoid))),
                        (w_in[:, :, 8 * 512:8 * 512 + N_GATES], source, gate_jobs),
                    ])
                    clear(nc, "clear_ml", [padded[:, :, 0:2], padded[:, :, TOK + 2:TOK + 4]])
                    w0, b0 = COLS_1["conv_w"][0], COLS_1["conv_b"][0]
                    conv_silu(nc, "mlc", padded, KD, CONV_K, TOK,
                              lambda c, j: cols[:, w0 + c * CONV_K + j:w0 + c * CONV_K + j + 1],
                              lambda c: cols[:, b0 + c:b0 + c + 1], qk)
            with Stage(nc, "mlbuf") as s2:
                g_col = s2.sb("g_col", [P, NT + 1, 2 * HEADS])
                exp_col = s2.sb("exp_col", [P, NT + 1, 2 * HEADS])
                max_rows = s2.sb("max_rows", [P, 2 * HEADS, TOK])
                mlstm_gates(nc, io, cols, gates, ident, g_col, exp_col, max_rows, max_dram)
                clear(nc, "ones_ml", [v1[:, :, :, P:P + 1]], 1.0)
                mlstm(nc, io, qk, v1, mo, y[:, :, MIX:D], g_col, exp_col, max_rows)
            if dbg: dbg("y", y[:, :, :])
            with Stage(nc, "mixout") as s2:
                yT = s2.sb("yT", [P, KD, TOK])
                turn_rows(nc, "turn_y", y, ALL_TILES, ident, yT)
                project(nc, "proj_out", [
                    (w_out[:, :, n * 512:(n + 1) * 512], lambda k: yT[:, k, :],
                     token_jobs(ALL_TILES, 512, lambda nc, i, r, ps, n=n: nc.vector.tensor_tensor(
                         h[:r, i, n * 512:(n + 1) * 512], h[:r, i, n * 512:(n + 1) * 512], ps, ALU.add), "dve"))
                    for n in range(2)])
        if dbg: dbg("hmix", h[:, :, :])

        slot_gate = st.sb("slot_gate", [CAP, EXPERTS])
        with Stage(nc, "moe") as s1:
            with Stage(nc, "routebuf") as s2:
                xs = s2.sb("xs", [P, EXPERTS, KD, CAP])
                u = s2.sb("u", [P, NT + 1, D])
                uT = s2.sb("uT", [P, KD, TOK])
                gain_row = s2.sb("gain_row", [P, D])
                load(nc, "load_g", [(gain_row[:, :], io["ffn_g_row"].partition_broadcast(P))])
                normalise(nc, "norm2", h, ALL_TILES, None, ident, uT, gain_row=gain_row, kept=u)
                route(nc, io, u, uT, ident, xs, slot_gate, idx_dram)
                load(nc, "store_xs", [(xs_dram, xs[:, :, :, :].rearrange("p e k c -> p (e k c)"))])
            expert_ffn(nc, io, xs_dram, slot_gate, ident, y_dram)
        combine(nc, io, h, idx_dram, y_dram)


N_MEM = 256
SSD_HEADS = 16
SSD_HD = D // SSD_HEADS
SSD_GROUPS = 4
SSD_RATIO = SSD_HEADS // SSD_GROUPS
SSD_CONV = 4
XBC = D + 2 * SSD_GROUPS * P
XBC_TILES = XBC // P
DIL = ((128, 1), (512, 4), (2048, 16))
DIL_J = 4
DIL_HD = 64
DIL_HEADS = len(DIL) * DIL_J
DIL_W = DIL_HEADS * DIL_HD
MEM_HD = 192
MEM_W = HEADS * MEM_HD
ROT = DIL_HD // 4
ROT_HALF = ROT // 2
OFF_XBC = D
OFF_DT = OFF_XBC + XBC
OFF_DQ = OFF_DT + SSD_HEADS
OFF_MQ = OFF_DQ + 3 * DIL_W
OFF_GATE = OFF_MQ + MEM_W
BRANCHES = 3

PEER_HEADS = 8
PEER_KEYS = 128
PEER_TOP = 16
PEER_SLOTS = PEER_HEADS * PEER_TOP

SEQ_TILES = [(i, P, P * i) for i in range(NT)]

COLS_2 = {}
for _name, _count in (("mix_g", KD), ("mem_g", KD), ("conv_w", XBC_TILES * SSD_CONV), ("conv_b", XBC_TILES),
                      ("dt_bias", 1), ("a_log", 1)):
    COLS_2[_name] = (sum(c for _, c in COLS_2.values()), _count)
COLS_2_N = sum(c for _, c in COLS_2.values())


def rms_groups(nc, name, xs, groups, width, gain):
    n = len(xs)
    with Stage(nc, name) as st:
        squares = st.sb("squares", [P, 2, groups * width])
        ssq = st.sb("ssq", [P, n, groups])
        squared, summed, inverted, rooted, dve_order = (
            st.sem(s) for s in ("squared", "summed", "inverted", "rooted", "dve_order"))

        def grouped(ap):
            return ap.rearrange("p (g w) -> p g w", g=groups)

        with nc.Block() as block:

            @block.scalar
            def _(act):
                for i in range(n):
                    if i >= 2:
                        act.wait_ge(summed, i - 1)
                    act.activation(squares[:, i % 2, :], xs[i], ACT.Square).then_inc(squared, 1)
                act.wait_ge(inverted, 1)
                act.activation(ssq[:, :, :], ssq[:, :, :], ACT.Sqrt).then_inc(rooted, 1)

            @block.vector
            def _(dve):
                order = InOrder(dve, dve_order)
                for i in range(n):
                    dve.wait_ge(squared, i + 1)
                    dve.tensor_reduce(ssq[:, i, :], grouped(squares[:, i % 2, :]), AX_X, ALU.add
                                      ).then_inc(summed, 1)
                dve.wait_ge(summed, n)
                order(dve.tensor_scalar(ssq[:, :, :], ssq[:, :, :], 1.0 / width, EPS, ALU.mult, ALU.add))
                dve.reciprocal(ssq[:, :, :], ssq[:, :, :]).then_inc(inverted, 1)
                dve.wait_ge(rooted, 1)
                for i in range(n):
                    x = grouped(xs[i])
                    order(dve.tensor_tensor(x, x, ssq[:, i, :].unsqueeze(2).broadcast_to([P, groups, width]),
                                            ALU.mult))
                    g = (gain.unsqueeze(1).broadcast_to([P, groups, width]) if gain.shape[1] == width
                         else grouped(gain))
                    order(dve.tensor_tensor(x, x, g, ALU.mult))


def ssd_prepare(nc, io, cols, dt_raw, xbc, ident, acum_rows, acum_col, xs, x_dt, scratch):
    with Stage(nc, "ssp") as st:
        dt = st.sb("dt", [SSD_HEADS, SEQ])
        soft = st.sb("soft", [SSD_HEADS, SEQ])
        acum = st.sb("acum", [SSD_HEADS, SEQ])
        ones = st.sb("ones", [SSD_HEADS, SEQ])
        a = st.sb("a", [SSD_HEADS, 1])
        dt_col = st.sb("dt_col", [P, NT, SSD_HEADS])
        small = st.ps("small", [P, NT, 2, SSD_HEADS])
        turned = st.ps("turned", [P, 2, D])
        abs_done, soft_done, a_done, rows_done, cols_turned, x_turned, x_out, stored, landed, dve_order, act_order = (
            st.sem(s) for s in ("abs_done", "soft_done", "a_done", "rows_done", "cols_turned", "x_turned", "x_out",
                                "stored", "landed", "dve_order", "act_order"))
        bias, a_log = COLS_2["dt_bias"][0], COLS_2["a_log"][0]

        with nc.Block() as block:

            @block.vector
            def _(dve):
                order = InOrder(dve, dve_order)
                order(dve.memset(ones[:, :], 1.0))
                order(dve.tensor_scalar(dt_raw[:, :], dt_raw[:, :], cols[:SSD_HEADS, bias:bias + 1], None, ALU.add))
                dve.scalar_tensor_tensor(soft[:, :], dt_raw[:, :], -1.0, dt_raw[:, :], ALU.mult,
                                         ALU.max).then_inc(abs_done, 1)
                dve.wait_ge(soft_done, 1)
                order(dve.scalar_tensor_tensor(dt[:, :], dt_raw[:, :], 0.0, soft[:, :], ALU.max, ALU.add))
                dve.wait_ge(a_done, 1)
                order(dve.tensor_scalar(soft[:, :], dt[:, :], a[:, :], -1.0, ALU.mult, ALU.mult))
                dve.tensor_tensor_scan(acum[:, :], ones[:, :], soft[:, :], 0.0, ALU.mult, ALU.add
                                       ).then_inc(rows_done, 1)
                dve.wait_ge(cols_turned, 1)
                order(dve.tensor_copy(acum_col[:, :, :], small[:, :, 0, :]))
                order(dve.tensor_copy(dt_col[:, :, :], small[:, :, 1, :]))
                for i in range(NT):
                    dve.wait_ge(x_turned, i + 1)
                    order(dve.tensor_copy(xs[:, i, :], turned[:, i % 2, :]))
                    dve.sem_inc(x_out, 1)
                    order(dve.tensor_tensor(
                        x_dt[:, i, :].rearrange("p (h e) -> p h e", h=SSD_HEADS),
                        xs[:, i, :].rearrange("p (h e) -> p h e", h=SSD_HEADS),
                        dt_col[:, i, :].unsqueeze(2).broadcast_to([P, SSD_HEADS, SSD_HD]), ALU.mult))

            @block.scalar
            def _(act):
                order = InOrder(act, act_order)
                act.activation(a[:, :], cols[:SSD_HEADS, a_log:a_log + 1], ACT.Exp).then_inc(a_done, 1)
                act.wait_ge(abs_done, 1)
                order(act.activation(soft[:, :], soft[:, :], ACT.Exp, scale=-1.0))
                act.activation(soft[:, :], soft[:, :], ACT.Ln, bias=1.0).then_inc(soft_done, 1)

            @block.tensor
            def _(pe):
                def turn_x(i):
                    if i >= 2:
                        pe.wait_ge(x_out, i - 1)
                    for k in range(KD):
                        last = pe.transpose(turned[:, i % 2, k * P:(k + 1) * P], xbc[:, k, i * P:(i + 1) * P],
                                            ident[:, :])
                    last.then_inc(x_turned, 1)

                turn_x(0)
                turn_x(1)
                pe.wait_ge(rows_done, 1)
                for i in range(NT):
                    pe.transpose(small[:, i, 0, :], acum[:, i * P:(i + 1) * P], ident[:SSD_HEADS, :SSD_HEADS])
                    last = pe.transpose(small[:, i, 1, :], dt[:, i * P:(i + 1) * P], ident[:SSD_HEADS, :SSD_HEADS])
                last.then_inc(cols_turned, 1)
                turn_x(2)
                turn_x(3)

            @block.sync
            def _(sp):
                sp.wait_ge(rows_done, 1)
                sp.dma_start(scratch, acum[:, :]).then_inc(stored, 16)
                sp.wait_ge(stored, 16)
                for hd in range(SSD_HEADS):
                    sp.dma_start(acum_rows[:, hd, :], scratch[hd:hd + 1, :].partition_broadcast(P)
                                 ).then_inc(landed, 16)
                sp.wait_ge(landed, 16 * SSD_HEADS)


def ssd(nc, io, xbc, acum_rows, acum_col, x_dt, z, y):
    with Stage(nc, "ssd") as st:
        raw = st.sb("raw", [P, NT, SEQ])
        arg = st.sb("arg", [P, 3, SEQ])
        weight = st.sb("weight", [P, 2, NT, SEQ])
        keep = st.sb("keep", [P, 2, P])
        skip = st.sb("skip", [P, SSD_HEADS])
        scores = st.ps("scores", [P, 2, 512])
        mixed = st.ps("mixed", [P, 4, 512])
        landed, scored, raw_ready, arg_ready, exp_ready, weight_ready, mix_done, mix_out, dve_order = (
            st.sem(s) for s in ("landed", "scored", "raw_ready", "arg_ready", "exp_ready", "weight_ready",
                                "mix_done", "mix_out", "dve_order"))

        with nc.Block() as block:

            @block.sync
            def _(sp):
                sp.dma_start(keep[:, :, :], io["c_keep"]).then_inc(landed, 16)
                sp.dma_start(skip[:, :], io["ssd_d_row"].partition_broadcast(P)).then_inc(landed, 16)
                sp.wait_ge(landed, 32)

            @block.scalar
            def _(act):
                for p in range(SSD_HEADS):
                    g = p // SSD_RATIO
                    if p % SSD_RATIO == 0:
                        if p:
                            act.wait_ge(weight_ready, NT * p)
                        for n in range(NT):
                            act.wait_ge(scored, g * NT + n + 1)
                            act.copy(raw[:, n, n * P:], scores[:, (g * NT + n) % 2, n * P:]).then_inc(raw_ready, 1)
                    for n in range(NT):
                        m = p * NT + n
                        act.wait_ge(arg_ready, m + 1)
                        act.activation(arg[:, m % 3, n * P:], arg[:, m % 3, n * P:], ACT.Exp
                                       ).then_inc(exp_ready, 1)

            @block.vector
            def _(dve):
                order = InOrder(dve, dve_order)
                dve.wait_ge(landed, 32)

                def exponents(p, n):
                    m = p * NT + n
                    if m >= 3:
                        dve.wait_ge(weight_ready, m - 2)
                    dve.tensor_scalar(arg[:, m % 3, n * P:], acum_rows[:, p, n * P:], acum_col[:, n, p:p + 1], 0.0,
                                      ALU.subtract, ALU.min).then_inc(arg_ready, 1)

                def weigh(p, n):
                    m = p * NT + n
                    dve.wait_ge(exp_ready, m + 1)
                    if p >= 2:
                        dve.wait_ge(mix_done, NT * (p - 1))
                    dve.tensor_tensor(weight[:, p % 2, n, n * P:], arg[:, m % 3, n * P:], raw[:, n, n * P:],
                                      ALU.mult).then_inc(weight_ready, 1)

                def take_out(p):
                    part = slice(p * SSD_HD, (p + 1) * SSD_HD)
                    for i in range(NT):
                        m = p * NT + i
                        dve.wait_ge(mix_done, m + 1)
                        dve.scalar_tensor_tensor(y[:, i, part], y[:, i, part], skip[:, p:p + 1],
                                                 mixed[:, m % 4, 0:SSD_HD], ALU.mult, ALU.add).then_inc(mix_out, 1)

                for p in range(SSD_HEADS):
                    exponents(p, 0)
                    exponents(p, 1)
                    if p % SSD_RATIO == 0:
                        dve.wait_ge(raw_ready, NT * (p // SSD_RATIO + 1))
                        for n in range(NT):
                            order(dve.tensor_tensor(raw[:, n, n * P:(n + 1) * P], raw[:, n, n * P:(n + 1) * P],
                                                    keep[:, 0, :], ALU.mult))
                    for n in range(NT):
                        if n + 2 < NT:
                            exponents(p, n + 2)
                        weigh(p, n)
                    if p:
                        take_out(p - 1)
                take_out(SSD_HEADS - 1)
                dve.wait_ge(mix_out, NT * SSD_HEADS)
                for i in range(NT):
                    order(dve.tensor_tensor(y[:, i, :], y[:, i, :], z[:, i, :], ALU.mult))

            @block.tensor
            def _(pe):
                def score(g):
                    for n in range(NT):
                        m = g * NT + n
                        if m >= 2:
                            pe.wait_ge(raw_ready, m - 1)
                        pe.matmul(scores[:, m % 2, n * P:], xbc[:, KD + g, n * P:(n + 1) * P],
                                  xbc[:, KD + SSD_GROUPS + g, n * P:SEQ], start=True, stop=True
                                  ).then_inc(scored, 1)

                def mix(p):
                    pe.wait_ge(weight_ready, NT * (p + 1))
                    for i in range(NT):
                        m = p * NT + i
                        if m >= 4:
                            pe.wait_ge(mix_out, m - 3)
                        for n in range(i + 1):
                            last = pe.matmul(mixed[:, m % 4, 0:SSD_HD], weight[:, p % 2, n, i * P:(i + 1) * P],
                                             x_dt[:, n, p * SSD_HD:(p + 1) * SSD_HD], start=(n == 0), stop=(n == i))
                        last.then_inc(mix_done, 1)

                score(0)
                for p in range(SSD_HEADS):
                    if p % SSD_RATIO == SSD_RATIO - 1 and p + 1 < SSD_HEADS:
                        score(p // SSD_RATIO + 1)
                    mix(p)


def rope(nc, io, qk):
    heads = 2 * DIL_HEADS
    two_pi = (6.28125, 0.00193500518798828125, 3.0199159819567e-07)
    magic = 1.5 * 2.0 ** 23
    pi = 3.1415925
    with Stage(nc, "rope") as st:
        pos_i = st.sb("pos_i", [P, NT], I32)
        pos = st.sb("pos", [P, NT])
        inv = st.sb("inv", [P, ROT_HALF])
        ang = st.sb("ang", [P, NT, ROT_HALF])
        turns = st.sb("turns", [P, 2, NT, ROT_HALF])
        rest = st.sb("rest", [P, 2, NT, ROT_HALF])
        a, b, c, d = (st.sb(s, [P, heads, ROT_HALF]) for s in "abcd")
        landed, reduced, sines, dve_order = (st.sem(s) for s in ("landed", "reduced", "sines", "dve_order"))
        with nc.Block() as block:

            @block.sync
            def _(sp):
                sp.dma_start(pos_i[:, :], io["positions"]).then_inc(landed, 16)
                sp.dma_start(inv[:, :], io["c_inv"].partition_broadcast(P)).then_inc(landed, 16)
                sp.wait_ge(landed, 32)

            @block.vector
            def _(dve):
                order = InOrder(dve, dve_order)
                dve.wait_ge(landed, 32)
                order(dve.tensor_copy(pos[:, :], pos_i[:, :]))
                order(dve.tensor_tensor(ang[:, :, :], pos[:, :].unsqueeze(2).broadcast_to([P, NT, ROT_HALF]),
                                        inv[:, :].unsqueeze(1).broadcast_to([P, NT, ROT_HALF]), ALU.mult))
                for w in range(2):
                    t, r = turns[:, w, :, :], rest[:, w, :, :]
                    order(dve.tensor_scalar(t, ang[:, :, :], 0.15915494309189535, 0.25 * w, ALU.mult, ALU.add))
                    order(dve.tensor_scalar(t, t, magic, None, ALU.add))
                    order(dve.tensor_scalar(t, t, magic, None, ALU.subtract))
                    order(dve.scalar_tensor_tensor(r, t, -two_pi[0], ang[:, :, :], ALU.mult, ALU.add))
                    order(dve.scalar_tensor_tensor(r, t, -two_pi[1], r, ALU.mult, ALU.add))
                    order(dve.scalar_tensor_tensor(r, t, -two_pi[2], r, ALU.mult, ALU.add))
                    if w:
                        order(dve.tensor_scalar(r, r, 1.5707963267948966, None, ALU.add))
                    order(dve.tensor_scalar(r, r, pi, -pi, ALU.min, ALU.max))
                dve.sem_inc(reduced, 1)
                dve.wait_ge(sines, 1)
                for i in range(NT):
                    x1, x2 = qk[:, i, :, 0:ROT_HALF], qk[:, i, :, ROT_HALF:ROT]
                    sin = rest[:, 0, i, :].unsqueeze(1).broadcast_to([P, heads, ROT_HALF])
                    cos = rest[:, 1, i, :].unsqueeze(1).broadcast_to([P, heads, ROT_HALF])
                    order(dve.tensor_tensor(a[:, :, :], x1, cos, ALU.mult))
                    order(dve.tensor_tensor(b[:, :, :], x2, sin, ALU.mult))
                    order(dve.tensor_tensor(c[:, :, :], x2, cos, ALU.mult))
                    order(dve.tensor_tensor(d[:, :, :], x1, sin, ALU.mult))
                    order(dve.tensor_tensor(x1, a[:, :, :], b[:, :, :], ALU.subtract))
                    order(dve.tensor_tensor(x2, c[:, :, :], d[:, :, :], ALU.add))

            @block.scalar
            def _(act):
                act.wait_ge(reduced, 1)
                act.activation(rest[:, :, :, :], rest[:, :, :, :], ACT.Sin).then_inc(sines, 1)


def attend(nc, name, units, ident, groups, wide, scale):
    n_u = len(units)
    with Stage(nc, name) as st:
        s = st.sb("s", [P, 2, groups, wide])
        pT = st.sb("pT", [P, 2, groups, wide])
        peak = st.sb("peak", [P, 2])
        total = st.sb("total", [P, 2])
        scores = st.ps("scores", [P, groups, 512])
        turned = st.ps("turned", [P, groups, 512])
        mixed = st.ps("mixed", [P, 2, 512])
        scored, masked, peaked, exped, turn_done, turn_out, mix_done, mix_out, dve_order = (
            st.sem(x) for x in ("scored", "masked", "peaked", "exped", "turn_done", "turn_out", "mix_done",
                                "mix_out", "dve_order"))
        with nc.Block() as block:

            @block.tensor
            def _(pe):
                def score(u):
                    pieces, w, _, _, _ = units[u]
                    if u:
                        pe.wait_ge(masked, u)
                    for g in range(groups):
                        for n, (q, k) in enumerate(pieces[g]):
                            last = pe.matmul(scores[:, g, 0:w], q, k, start=(n == 0), stop=(n == len(pieces[g]) - 1))
                    last.then_inc(scored, 1)

                def turn(u):
                    _, w, _, _, _ = units[u]
                    pe.wait_ge(exped, u + 1)
                    if u:
                        pe.wait_ge(turn_out, u)
                    for g in range(groups):
                        for n in range(w // P):
                            last = pe.transpose(turned[:, g, n * P:(n + 1) * P], s[:, u % 2, g, n * P:(n + 1) * P],
                                                ident[:, :])
                    last.then_inc(turn_done, 1)

                def mix(u):
                    _, w, _, values, out = units[u]
                    pe.wait_ge(turn_out, u + 1)
                    if u >= 2:
                        pe.wait_ge(mix_out, u - 1)
                    blocks = [(g, n) for g in range(groups) for n in range(w // P)]
                    for g, n in blocks:
                        last = pe.matmul(mixed[:, u % 2, 0:out.shape[1]], pT[:, u % 2, g, n * P:(n + 1) * P],
                                         values(g, n), start=((g, n) == blocks[0]), stop=((g, n) == blocks[-1]))
                    last.then_inc(mix_done, 1)

                for u in range(n_u + 2):
                    if u < n_u:
                        score(u)
                    if u >= 2:
                        mix(u - 2)
                    if 1 <= u <= n_u:
                        turn(u - 1)

            @block.vector
            def _(dve):
                order = InOrder(dve, dve_order)
                for u in range(n_u + 2):
                    if u < n_u:
                        _, w, mask, _, _ = units[u]
                        dve.wait_ge(scored, u + 1)
                        if u >= 2:
                            dve.wait_ge(turn_done, u - 1)
                        now = s[:, u % 2, :, 0:w]
                        if mask is None:
                            order(dve.tensor_scalar(now, scores[:, :, 0:w], scale, None, ALU.mult))
                        else:
                            order(dve.scalar_tensor_tensor(now, scores[:, :, 0:w], scale, mask, ALU.mult, ALU.add))
                        dve.sem_inc(masked, 1)
                        order(dve.tensor_reduce(peak[:, u % 2:u % 2 + 1], now, mybir.AxisListType.XY, ALU.max))
                        dve.tensor_scalar(peak[:, u % 2:u % 2 + 1], peak[:, u % 2:u % 2 + 1], -1.0, None,
                                          ALU.mult).then_inc(peaked, 1)
                    if u >= 2:
                        v, out = u - 2, units[u - 2][4]
                        dve.wait_ge(mix_done, v + 1)
                        order(dve.reciprocal(total[:, v % 2:v % 2 + 1], total[:, v % 2:v % 2 + 1]))
                        order(dve.tensor_scalar(out, mixed[:, v % 2, 0:out.shape[1]], total[:, v % 2:v % 2 + 1],
                                                None, ALU.mult))
                        dve.sem_inc(mix_out, 1)

            @block.scalar
            def _(act):
                for u in range(n_u + 1):
                    if u < n_u:
                        w = units[u][1]
                        act.wait_ge(peaked, u + 1)
                        if u >= 2:
                            act.wait_ge(mix_out, u - 1)
                        now = s[:, u % 2, :, 0:w]
                        act.activation(now, now, ACT.Exp, bias=peak[:, u % 2:u % 2 + 1],
                                       accum_out=total[:, u % 2:u % 2 + 1]).then_inc(exped, 1)
                    if u >= 1:
                        v, w = u - 1, units[u - 1][1]
                        act.wait_ge(turn_done, v + 1)
                        if v >= 2:
                            act.wait_ge(mix_done, v - 1)
                        act.copy(pT[:, v % 2, :, 0:w], turned[:, :, 0:w]).then_inc(turn_out, 1)


def peer_select(nc, io, qT, chosen, gates):
    hc = 2 * PEER_HEADS
    H, T = PEER_HEADS, PEER_TOP
    with Stage(nc, "sel") as st:
        keys = st.sb("keys", [P, hc, PEER_KEYS])
        sc = st.sb("sc", [P, 2, hc, PEER_KEYS])
        v = st.sb("v", [P, hc, T])
        ix = st.sb("ix", [P, hc, T], U32)
        ixf = st.sb("ixf", [P, hc, T])
        cand = st.sb("cand", [P, H, T, T])
        match = st.sb("match", [P, H, T, T])
        top = st.sb("top", [P, 2, H, T])
        pos = st.sb("pos", [P, H, T], U32)
        part = st.sb("part", [P, 2, H, T], U32)
        partf = st.sb("partf", [P, 2, H, T])
        picked = st.sb("picked", [P, 2, H, T])
        iota = st.sb("iota", [P, T])
        total = st.sb("total", [P, H])
        scores = st.ps("scores", [P, hc, PEER_KEYS])
        landed, scored, sc_ready, sc_used, top_ready, exp_ready, top_used, dve_order = (
            st.sem(x) for x in ("landed", "scored", "sc_ready", "sc_used", "top_ready", "exp_ready", "top_used",
                                "dve_order"))
        with nc.Block() as block:

            @block.sync
            def _(sp):
                sp.dma_start(keys[:, :, :], io["sub_keys"]).then_inc(landed, 16)
                sp.dma_start(iota[:, :], io["c_iota16"].partition_broadcast(P)).then_inc(landed, 16)
                sp.wait_ge(landed, 32)

            @block.tensor
            def _(pe):
                pe.wait_ge(landed, 32)
                for i in range(NT):
                    if i:
                        pe.wait_ge(sc_ready, i)
                    for c in range(hc):
                        last = pe.matmul(scores[:, c, :], qT[:, c, i * P:(i + 1) * P], keys[:, c, :],
                                         start=True, stop=True)
                    last.then_inc(scored, 1)

            @block.scalar
            def _(act):
                for i in range(NT):
                    act.wait_ge(scored, i + 1)
                    if i >= 2:
                        act.wait_ge(sc_used, i - 1)
                    act.copy(sc[:, i % 2, :, :], scores[:, :, :]).then_inc(sc_ready, 1)
                    if i:
                        act.wait_ge(top_ready, i)
                        act.activation(top[:, (i - 1) % 2, :, :], top[:, (i - 1) % 2, :, :], ACT.Exp
                                       ).then_inc(exp_ready, 1)
                act.wait_ge(top_ready, NT)
                act.activation(top[:, (NT - 1) % 2, :, :], top[:, (NT - 1) % 2, :, :], ACT.Exp
                               ).then_inc(exp_ready, 1)

            @block.vector
            def _(dve):
                order = InOrder(dve, dve_order)
                dve.wait_ge(landed, 32)

                def best16(vals, where, x):
                    order(dve.max(vals[:, 0:8], x))
                    order(dve.max_index(where[:, 0:8], vals[:, 0:8], x))
                    order(dve.match_replace(x, vals[:, 0:8], x, -3.0e38))
                    order(dve.max(vals[:, 8:16], x))
                    order(dve.max_index(where[:, 8:16], vals[:, 8:16], x))

                def finish(i):
                    dve.wait_ge(exp_ready, i + 1)
                    t = top[:, i % 2, :, :]
                    order(dve.tensor_reduce(total[:, :], t, AX_X, ALU.add))
                    order(dve.reciprocal(total[:, :], total[:, :]))
                    order(dve.tensor_tensor(gates[:, i, :].rearrange("p (h t) -> p h t", h=H), t,
                                            total[:, :].unsqueeze(2).broadcast_to([P, H, T]), ALU.mult))

                for i in range(NT):
                    dve.wait_ge(sc_ready, i + 1)
                    for c in range(hc):
                        best16(v[:, c, :], ix[:, c, :], sc[:, i % 2, c, :])
                    dve.sem_inc(sc_used, 1)
                    order(dve.tensor_copy(ixf[:, :, :], ix[:, :, :]))
                    v4 = v[:, :, :].rearrange("p (h c) t -> p h c t", c=2)
                    i4 = ixf[:, :, :].rearrange("p (h c) t -> p h c t", c=2)
                    order(dve.tensor_tensor(cand[:, :, :, :], v4[:, :, 0, :].unsqueeze(3).broadcast_to([P, H, T, T]),
                                            v4[:, :, 1, :].unsqueeze(2).broadcast_to([P, H, T, T]), ALU.add))
                    for h in range(H):
                        best16(top[:, i % 2, h, :], pos[:, h, :], cand[:, h, :, :].rearrange("p a b -> p (a b)"))
                    order(dve.tensor_scalar(part[:, 0, :, :], pos[:, :, :], 4, None, ALU.logical_shift_right))
                    order(dve.tensor_scalar(part[:, 1, :, :], pos[:, :, :], T - 1, None, ALU.bitwise_and))
                    order(dve.tensor_copy(partf[:, :, :, :], part[:, :, :, :]))
                    for c in range(2):
                        order(dve.tensor_tensor(
                            match[:, :, :, :].rearrange("p h t a -> p (h t) a"),
                            partf[:, c, :, :].rearrange("p h t -> p (h t)").unsqueeze(2).broadcast_to([P, H * T, T]),
                            iota[:, :].unsqueeze(1).broadcast_to([P, H * T, T]), ALU.is_equal))
                        order(dve.tensor_tensor(match[:, :, :, :], match[:, :, :, :],
                                                i4[:, :, c, :].unsqueeze(2).broadcast_to([P, H, T, T]), ALU.mult))
                        order(dve.tensor_reduce(picked[:, c, :, :], match[:, :, :, :], AX_X, ALU.add))
                    order(dve.scalar_tensor_tensor(
                        chosen[:, i, :].rearrange("p (h t) -> p h t", h=H), picked[:, 0, :, :], float(PEER_KEYS),
                        picked[:, 1, :, :], ALU.mult, ALU.add))
                    order(dve.tensor_tensor(picked[:, 0, :, :], top[:, i % 2, :, :],
                                            top[:, i % 2, :, 0:1].broadcast_to([P, H, T]), ALU.subtract))
                    dve.tensor_copy(top[:, i % 2, :, :], picked[:, 0, :, :]).then_inc(top_ready, 1)
                    dve.wait_ge(top_ready, i + 1)
                    if i:
                        finish(i - 1)
                finish(NT - 1)


GROUP = 8
RING = 2 * GROUP
ROUNDS = PEER_SLOTS // RING


def peer_experts(nc, io, hn, h, chosen, gates, out):
    down = io["peer_down_2"][0]
    up = io["peer_up_2"][0]
    with Stage(nc, "peer") as st:
        down_rows = [st.sb(f"down{u}", [P, D]) for u in range(RING)]
        up_rows = [st.sb(f"up{u}", [P, D]) for u in range(RING)]
        junk = st.sb("junk", [P, 2, D])
        idx_d = st.sb("idx_d", [P, 2, GROUP], U32)
        idx_u = st.sb("idx_u", [P, 2, GROUP], U32)
        dots = st.sb("dots", [P, NT, PEER_SLOTS])
        coef = st.sb("coef", [P, NT, PEER_SLOTS])
        diag = st.sb("diag", [P, 4, P])
        ident = st.sb("ident", [P, P])
        zeros = st.sb("zeros", [P, 512])
        acc = st.ps("acc", [P, 2, D])
        down_in = [st.sem(f"down_in{u}") for u in range(RING)]
        up_in = [st.sem(f"up_in{u}") for u in range(RING)]
        landed, down_used, up_used, gelu_done, coef_done, diag_done, diag_used, sum_done, added, stored = (
            st.sem(x) for x in ("landed", "down_used", "up_used", "gelu_done", "coef_done", "diag_done",
                                "diag_used", "sum_done", "added", "stored"))
        dve_order, ready, idx_ready, idx_seen = (st.sem(x) for x in ("dve_order", "ready", "idx_ready", "idx_seen"))

        steps = [(j < NT, j >= 1) for j in range(NT + 1)]

        with nc.Block() as block:

            @block.sync
            def _(sp):
                sp.dma_start(ident[:, :], io["c_ident"]).then_inc(landed, 16)
                for i in range(NT):
                    sp.wait_ge(added, i + 1)
                    sp.dma_start(out[i * P:(i + 1) * P, :], h[:, i, :]).then_inc(stored, 16)
                sp.wait_ge(stored, 16 * NT)

            @block.gpsimd
            def _(pool):
                pool.sem_inc(down_used, RING)
                pool.sem_inc(up_used, RING)
                copies = 0
                for j, (has_down, has_up) in enumerate(steps):
                    kinds = ([("down", j)] if has_down else []) + ([("up", j - 1)] if has_up else [])
                    with pool.Fori(0, ROUNDS) as r:
                        for b in range(2):
                            for n, (kind, i) in enumerate(kinds):
                                used = down_used if kind == "down" else up_used
                                idx = idx_d if kind == "down" else idx_u
                                first = r * RING + b * GROUP
                                pool.wait_ge(used, first + (i * PEER_SLOTS + GROUP))
                                pool.tensor_copy(idx[:, b, :], chosen[:, i, bass.ds(first, GROUP)]
                                                 ).then_inc(idx_ready, 1)
                                pool.wait_ge(idx_ready, r * (2 * len(kinds)) + (copies + b * len(kinds) + n + 1))
                                pool.sem_inc(idx_seen, 1)
                            for u in range(GROUP):
                                for kind, i in kinds:
                                    rows, table, sems, idx = ((down_rows, down, down_in, idx_d) if kind == "down"
                                                              else (up_rows, up, up_in, idx_u))
                                    pool.indirect_dma_start(
                                        rows[b * GROUP + u][:, :], None, table,
                                        bass.IndirectOffsetOnAxis(ap=idx[:, b, u:u + 1], axis=0)
                                    ).then_inc(sems[b * GROUP + u], 16)
                    copies += ROUNDS * 2 * len(kinds)

            @block.vector
            def _(dve):
                order = InOrder(dve, dve_order)
                dve.memset(zeros[:, :], 0.0).then_inc(ready, 1)
                for j, (has_down, has_up) in enumerate(steps):
                    if has_down:
                        with dve.Fori(0, ROUNDS) as r:
                            for u in range(RING):
                                slot = r * RING + u
                                dve.wait_ge(down_in[u], (r + (j * ROUNDS + 1)) * 16)
                                dve.wait_ge(down_used, slot + (j * PEER_SLOTS + RING - 1))
                                dve.scalar_tensor_tensor(junk[:, u % 2, :], down_rows[u][:, :], 1.0, hn[:, j, :],
                                                         ALU.mult, ALU.mult,
                                                         accum_out=dots[:, j, bass.ds(slot, 1)]
                                                         ).then_inc(down_used, 1)
                        dve.wait_ge(gelu_done, j + 1)
                        dve.tensor_tensor(coef[:, j, :], dots[:, j, :], gates[:, j, :], ALU.mult
                                          ).then_inc(coef_done, 1)
                    if has_up:
                        i = j - 1
                        dve.wait_ge(sum_done, i + 1)
                        dve.tensor_tensor(h[:, i, :], h[:, i, :], acc[:, i % 2, :], ALU.add).then_inc(added, 1)

            @block.scalar
            def _(act):
                act.sem_inc(diag_used, 4)
                act.wait_ge(landed, 16)
                for j, (has_down, has_up) in enumerate(steps):
                    if has_up:
                        i = j - 1
                        act.wait_ge(coef_done, i + 1)
                        with act.Fori(0, ROUNDS) as r:
                            for u in range(RING):
                                slot = r * RING + u
                                act.wait_ge(diag_used, slot + (i * PEER_SLOTS + 1))
                                act.activation(diag[:, u % 4, :], ident[:, :], ACT.Copy,
                                               scale=coef[:, i, bass.ds(slot, 1)]).then_inc(diag_done, 1)
                    if has_down:
                        act.wait_ge(down_used, (j + 1) * PEER_SLOTS + RING)
                        act.activation(dots[:, j, :], dots[:, j, :], ACT.Gelu).then_inc(gelu_done, 1)

            @block.tensor
            def _(pe):
                pe.wait_ge(ready, 1)
                for i in range(NT):
                    if i >= 2:
                        pe.wait_ge(added, i - 1)
                    for half in range(2):
                        pe.matmul(acc[:, i % 2, half * 512:(half + 1) * 512], zeros[:, 0:P], zeros[:, :],
                                  start=True, stop=False, skip_group_check=True)
                    with pe.Fori(0, ROUNDS) as r:
                        for u in range(RING):
                            slot = r * RING + u
                            pe.wait_ge(diag_done, slot + (i * PEER_SLOTS + 1))
                            pe.wait_ge(up_in[u], (r + (i * ROUNDS + 1)) * 16)
                            for half in range(2):
                                last = pe.matmul(acc[:, i % 2, half * 512:(half + 1) * 512], diag[:, u % 4, :],
                                                 up_rows[u][:, half * 512:(half + 1) * 512],
                                                 start=False, stop=False, skip_group_check=True)
                            last.then_inc(up_used, 1)
                            pe.wait_ge(up_used, slot + (i * PEER_SLOTS + RING + 1))
                            pe.sem_inc(diag_used, 1)
                    for half in range(2):
                        last = pe.matmul(acc[:, i % 2, half * 512:(half + 1) * 512], zeros[:, 0:P], zeros[:, :],
                                         start=False, stop=True, skip_group_check=True)
                    last.then_inc(sum_done, 1)


def second_block(nc, io, x, ident, out, dbg=None):
    w_in = io["w_in_2"][0].rearrange("(k p) c -> p k c", p=P)
    acum_dram = nc.dram_tensor("scratch_acum", [SSD_HEADS, SEQ], F32).ap()

    def copy_jobs(tiles, width, dst):
        return [Job("token", 0, width, (lambda nc, ps, i=i: (nc.scalar.copy if i % 2 else nc.vector.tensor_copy)(
            dst(i), ps)), "act" if i % 2 else "dve", col=col, rows=rows) for i, rows, col in tiles]

    with Stage(nc, "b2") as st:
        cols = st.sb("cols", [P, COLS_2_N])
        load(nc, "load2", [(cols[:, :], io["p_cols_2"])])

        def gain(name):
            a, n = COLS_2[name]
            return cols[:, a:a + n]

        with own_semaphores(nc), Stage(nc, "branches") as br:
            uT = br.sb("uT", [P, KD, SEQ])
            ssdT = br.sb("ssdT", [P, KD, SEQ])
            normalise(nc, "norm3", x, SEQ_TILES, gain("mix_g"), ident, uT)

            def source(k):
                return uT[:, k, :]

            def w_cols(first, width):
                return w_in[:, :, first:first + width]

            with Stage(nc, "ssdbuf") as s1:
                y = s1.sb("y", [P, NT, D])
                z = s1.sb("z", [P, NT, D])
                xbc = s1.sb("xbc", [P, XBC_TILES, SEQ + SSD_CONV - 1])
                dt_raw = s1.sb("dt_raw", [SSD_HEADS, SEQ])
                chunks = [(w_cols(OFF_XBC + n * 512, 512), source, [
                    Job("channel", c * P, P, (lambda nc, ps, t=4 * n + c, eng=eng: (
                        nc.scalar.copy if eng == "act" else nc.vector.tensor_copy)(
                            xbc[:, t, SSD_CONV - 1:SSD_CONV - 1 + SEQ], ps)), eng)
                    for c, eng in enumerate(("act", "dve") * 2)]) for n in range(XBC // 512)]
                chunks.append((w_cols(OFF_DT, SSD_HEADS), source, [
                    Job("channel", 0, SSD_HEADS, lambda nc, ps: nc.vector.tensor_copy(dt_raw[:, :], ps), "dve")]))
                chunks += [(w_cols(n * 512, 512), source, token_jobs(
                    SEQ_TILES, 512, lambda nc, i, r, ps, n=n: nc.scalar.activation(
                        z[:, i, n * 512:(n + 1) * 512], ps, ACT.Silu))) for n in range(2)]
                project(nc, "proj_ssd", chunks)
                clear(nc, "clear_ssd", [xbc[:, :, 0:SSD_CONV - 1]])
                w0, b0 = COLS_2["conv_w"][0], COLS_2["conv_b"][0]
                conv_silu(nc, "ssc", xbc, XBC_TILES, SSD_CONV, SEQ,
                          lambda c, j: cols[:, w0 + c * SSD_CONV + j:w0 + c * SSD_CONV + j + 1],
                          lambda c: cols[:, b0 + c:b0 + c + 1], xbc)
                with Stage(nc, "ssdbuf2") as s2:
                    acum_rows = s2.sb("acum_rows", [P, SSD_HEADS, SEQ])
                    acum_col = s2.sb("acum_col", [P, NT, SSD_HEADS])
                    x_dt = s2.sb("x_dt", [P, NT, D])
                    ssd_prepare(nc, io, cols, dt_raw, xbc, ident, acum_rows, acum_col, y, x_dt, acum_dram)
                    ssd(nc, io, xbc, acum_rows, acum_col, x_dt, z, y)
                gain_row = s1.sb("gain_row", [P, D])
                load(nc, "load_ssd_g", [(gain_row[:, :], io["ssd_g_row"].partition_broadcast(P))])
                rms_groups(nc, "ssd_norm", [y[:, i, :] for i in range(NT)], SSD_GROUPS, D // SSD_GROUPS,
                           gain_row[:, :])
                if dbg: dbg("y_ssd", y[:, :, :])
                turn_rows(nc, "turn_ssd", y, SEQ_TILES, ident, ssdT)

            dilT = br.sb("dilT", [P, DIL_J * DIL_HD // P, SEQ])
            with Stage(nc, "dilbuf") as s1:
                qkv = s1.sb("qkv", [P, NT, 3 * DIL_W])
                y = s1.sb("y", [P, NT, DIL_J * DIL_HD])
                qkT = s1.sb("qkT", [P, 2 * DIL_W // P, SEQ])
                q_gain = s1.sb("q_gain", [P, DIL_HD])
                k_gain = s1.sb("k_gain", [P, DIL_HD])
                mask = s1.sb("mask", [P, len(DIL), SEQ])
                project(nc, "proj_dil", [
                    (w_cols(OFF_DQ + n * 384, 384), source,
                     copy_jobs(SEQ_TILES, 384, lambda i, n=n: qkv[:, i, n * 384:(n + 1) * 384]))
                    for n in range(3 * DIL_W // 384)])
                load(nc, "load_dil", [(q_gain[:, :], io["dil_q_row"].partition_broadcast(P)),
                                      (k_gain[:, :], io["dil_k_row"].partition_broadcast(P)),
                                      (mask[:, :, :], io["c_dilated"])])
                rms_groups(nc, "norm_dq", [qkv[:, i, 0:DIL_W] for i in range(NT)], DIL_HEADS, DIL_HD, q_gain[:, :])
                rms_groups(nc, "norm_dk", [qkv[:, i, DIL_W:2 * DIL_W] for i in range(NT)], DIL_HEADS, DIL_HD,
                           k_gain[:, :])
                rope(nc, io, qkv[:, :, 0:2 * DIL_W].rearrange("p i (h e) -> p i h e", e=DIL_HD))
                turn_rows(nc, "turn_dil_q", qkv, SEQ_TILES, ident, qkT[:, 0:6, :], DIL_W // P)
                turn_rows(nc, "turn_dil_k", qkv[:, :, DIL_W:2 * DIL_W], SEQ_TILES, ident, qkT[:, 6:12, :],
                          DIL_W // P)
                units = []
                for i in range(NT):
                    w = (i + 1) * P
                    for j in range(DIL_J):
                        pieces = []
                        for g in range(len(DIL)):
                            head = g * DIL_J + j
                            a = (head % 2) * DIL_HD
                            pieces.append([(qkT[a:a + DIL_HD, head // 2, i * P:(i + 1) * P],
                                            qkT[a:a + DIL_HD, 6 + head // 2, 0:w])])
                        units.append((pieces, w, mask[:, :, SEQ - w:SEQ],
                                      (lambda g, n, j=j: qkv[:, n, 2 * DIL_W + (g * DIL_J + j) * DIL_HD:
                                                             2 * DIL_W + (g * DIL_J + j + 1) * DIL_HD]),
                                      y[:, i, j * DIL_HD:(j + 1) * DIL_HD]))
                attend(nc, "dil", units, ident, len(DIL), SEQ, float(DIL_HD) ** -0.5)
                if dbg: dbg("y_dil", y[:, :, :])
                turn_rows(nc, "turn_dil", y, SEQ_TILES, ident, dilT, DIL_J * DIL_HD // P)

            memT = br.sb("memT", [P, MEM_W // P, SEQ])
            with Stage(nc, "membuf") as s1:
                mem = s1.sb("mem", [P, N_MEM // P, D])
                mem_uT = s1.sb("mem_uT", [P, KD, N_MEM])
                mkv = s1.sb("mkv", [P, N_MEM // P, 2 * MEM_W])
                mq = s1.sb("mq", [P, NT, MEM_W])
                mqT = s1.sb("mqT", [P, MEM_W // P, SEQ])
                mkT = s1.sb("mkT", [P, MEM_W // P, N_MEM])
                q_gain = s1.sb("q_gain", [P, MEM_HD])
                k_gain = s1.sb("k_gain", [P, MEM_HD])
                y = s1.sb("y", [P, NT, MEM_W])
                mem_tiles = [(i, P, P * i) for i in range(N_MEM // P)]
                load(nc, "load_mem", [(mem[:, :, :], io["mem_2"][0].rearrange("(i p) d -> p i d", p=P)),
                                      (q_gain[:, :], io["mem_q_row"].partition_broadcast(P)),
                                      (k_gain[:, :], io["mem_k_row"].partition_broadcast(P))])
                normalise(nc, "norm_mem", mem, mem_tiles, gain("mem_g"), ident, mem_uT)
                w_kv = io["w_mem_kv_2"][0].rearrange("(k p) c -> p k c", p=P)
                project(nc, "proj_mem", [
                    (w_kv[:, :, n * 384:(n + 1) * 384], lambda k: mem_uT[:, k, :],
                     copy_jobs(mem_tiles, 384, lambda i, n=n: mkv[:, i, n * 384:(n + 1) * 384]))
                    for n in range(2 * MEM_W // 384)] + [
                    (w_cols(OFF_MQ + n * 384, 384), source,
                     copy_jobs(SEQ_TILES, 384, lambda i, n=n: mq[:, i, n * 384:(n + 1) * 384]))
                    for n in range(MEM_W // 384)])
                rms_groups(nc, "norm_mq", [mq[:, i, :] for i in range(NT)], HEADS, MEM_HD, q_gain[:, :])
                rms_groups(nc, "norm_mk", [mkv[:, i, 0:MEM_W] for i in range(N_MEM // P)], HEADS, MEM_HD,
                           k_gain[:, :])
                turn_rows(nc, "turn_mq", mq, SEQ_TILES, ident, mqT, MEM_W // P)
                turn_rows(nc, "turn_mk", mkv, mem_tiles, ident, mkT, MEM_W // P)

                def pieces_of(hd):
                    a, end = hd * MEM_HD, (hd + 1) * MEM_HD
                    while a < end:
                        b = min(end, (a // P + 1) * P)
                        yield a // P, a % P, b - a
                        a = b

                units = [([[(mqT[a:a + n, t, i * P:(i + 1) * P], mkT[a:a + n, t, :]) for t, a, n in pieces_of(hd)]],
                          N_MEM, None,
                          (lambda g, n, hd=hd: mkv[:, n, MEM_W + hd * MEM_HD:MEM_W + (hd + 1) * MEM_HD]),
                          y[:, i, hd * MEM_HD:(hd + 1) * MEM_HD]) for i in range(NT) for hd in range(HEADS)]
                attend(nc, "mem", units, ident, 1, N_MEM, float(MEM_HD) ** -0.5)
                if dbg: dbg("y_mem", y[:, :, :])
                turn_rows(nc, "turn_mem", y, SEQ_TILES, ident, memT, MEM_W // P)

            with Stage(nc, "mergebuf") as s1:
                prod = s1.sb("prod", [P, BRANCHES, NT, D])
                chunks = []
                for b, (wt, turned, nk) in enumerate((("w_ssd_br_2", ssdT, KD), ("w_dil_br_2", dilT, 2),
                                                      ("w_mem_br_2", memT, MEM_W // P))):
                    wb = io[wt][0].rearrange("(k p) c -> p k c", p=P)
                    for n in range(2):
                        part = slice(n * 512, (n + 1) * 512)
                        chunks.append((w_cols(OFF_GATE + b * D + n * 512, 512), source, token_jobs(
                            SEQ_TILES, 512, lambda nc, i, r, ps, b=b, part=part: nc.scalar.activation(
                                prod[:, b, i, part], ps, ACT.Sigmoid))))
                        jobs = token_jobs(SEQ_TILES, 512, lambda nc, i, r, ps, b=b, part=part: nc.vector.tensor_tensor(
                            prod[:, b, i, part], prod[:, b, i, part], ps, ALU.mult), "dve")
                        for i, job in enumerate(jobs):
                            job.after = (len(chunks) - 1) * NT + i
                        chunks.append((wb[:, :, part], (lambda k, turned=turned: turned[:, k, :]), jobs))
                project(nc, "proj_merge", chunks)
                dve_done = s1.sem("dve_done")
                with nc.Block() as block:

                    @block.vector
                    def _(dve):
                        order = InOrder(dve, dve_done)
                        for b in range(1, BRANCHES):
                            order(dve.tensor_tensor(prod[:, 0, :, :], prod[:, 0, :, :], prod[:, b, :, :], ALU.add))

                turn_rows(nc, "turn_merged", prod[:, 0, :, :], SEQ_TILES, ident, uT)
                w_out = io["w_out_2"][0].rearrange("(k p) c -> p k c", p=P)
                project(nc, "proj_out2", [
                    (w_out[:, :, n * 512:(n + 1) * 512], source,
                     token_jobs(SEQ_TILES, 512, lambda nc, i, r, ps, n=n: nc.vector.tensor_tensor(
                         x[:, i, n * 512:(n + 1) * 512], x[:, i, n * 512:(n + 1) * 512], ps, ALU.add), "dve"))
                    for n in range(2)])
        if dbg: dbg("hmix2", x[:, 0:NT, :])

        with Stage(nc, "peerbuf") as s1:
            hn = s1.sb("hn", [P, NT, D])
            chosen = s1.sb("chosen", [P, NT, PEER_SLOTS])
            gates = s1.sb("gates", [P, NT, PEER_SLOTS])
            with Stage(nc, "selbuf") as s2:
                hnT = s2.sb("hnT", [P, KD, SEQ])
                gain_row = s2.sb("gain_row", [P, D])
                qT = s2.sb("qT", [P, 2 * PEER_HEADS, SEQ])
                load(nc, "load_peer_g", [(gain_row[:, :], io["ffn_g_row_2"].partition_broadcast(P))])
                normalise(nc, "norm4", x, SEQ_TILES, None, ident, hnT, gain_row=gain_row, kept=hn)
                w_q = io["peer_w_query_2"][0].rearrange("(k p) c -> p k c", p=P)
                project(nc, "proj_query", [(w_q[:, :, n * 512:(n + 1) * 512], lambda k: hnT[:, k, :], [
                    Job("channel", c * P, P, (lambda nc, ps, t=4 * n + c, eng=eng: (
                        nc.scalar.copy if eng == "act" else nc.vector.tensor_copy)(qT[:, t, :], ps)), eng)
                    for c, eng in enumerate(("act", "dve") * 2)]) for n in range(4)])
                peer_select(nc, io, qT, chosen, gates)
            peer_experts(nc, io, hn, x, chosen, gates, out)


def two_blocks(nc, io, out):
    with Stage(nc, "top") as st:
        h = st.sb("h", [P, NT + 1, D])
        ident = st.sb("ident", [P, P])
        with own_semaphores(nc):
            first_block(nc, io, h, ident)
        with Stage(nc, "between") as s1:
            gain_row = s1.sb("gain_row", [P, D])
            load(nc, "load_final_g", [(gain_row[:, :], io["final_g_row"].partition_broadcast(P))])
            normalise(nc, "norm_final", h, SEQ_TILES, None, ident, None, gain_row=gain_row, kept=h)
        second_block(nc, io, h, ident, out)


def constants():
    import numpy as np

    f = np.float32
    half = P // 2
    inv = (f(10000.0) ** (-np.arange(half, dtype=f) / f(half))).astype(f)
    ang = np.arange(TOK, dtype=f)[None, :] * inv[:, None]
    x = np.arange(REL_W)[None, :] - REL_BASE - np.arange(P)[:, None]
    p, c = np.arange(P)[:, None], np.arange(P)[None, :]
    back = p + SEQ - P - np.arange(SEQ)[None, :]
    dilated = np.stack([np.where((back >= 0) & (back <= window) & (back % step == 0), 0.0, NEG)
                        for window, step in DIL], 1)
    inv2 = np.exp(f(-np.log(500000.0) * (2.0 / ROT)) * np.arange(ROT_HALF, dtype=f)).astype(f)
    token_id = np.zeros((P, NT + 1), f)
    for i, rows, col in ALL_TILES:
        token_id[:, i] = col + np.arange(P)
    return {
        "c_ident": np.eye(P, dtype=f),
        "c_cos": np.concatenate([np.cos(ang)] * 2).astype(f),
        "c_sin": np.concatenate([-np.sin(ang), np.sin(ang)]).astype(f),
        "c_ahead": np.maximum(x, 0).astype(f),
        "c_behind": np.maximum(-x, 0).astype(f),
        "c_diag": (1.0 + (x == 0)).astype(f),
        "c_keep": np.stack([c >= p, c <= p], 1).astype(f),
        "c_token_id": token_id,
        "c_dilated": dilated.astype(f),
        "c_inv": inv2[None, :],
        "c_iota16": np.arange(PEER_TOP, dtype=f)[None, :],
        "c_ids": (META + np.arange(SEQ, dtype=f))[None, :],
    }


def channel_columns(v):
    return v.reshape((-1, P) + v.shape[1:]).swapaxes(0, 1)


def layouts(inputs):
    import numpy as np

    cat = np.concatenate
    conv = channel_columns(inputs["conv_w"][0].T)
    gate_b = np.zeros((P, 4), np.float32)
    gate_b[:HEADS] = inputs["b_gates"][0].reshape(4, HEADS).T
    heads = np.zeros((P, 2), np.float32)
    heads[:SSD_HEADS, 0] = inputs["ssd_dt_bias_2"][0]
    heads[:SSD_HEADS, 1] = inputs["ssd_a_log_2"][0]
    return {
        "p_cols_2": np.ascontiguousarray(cat([
            channel_columns(inputs["norm_mix_w_2"][0]), channel_columns(inputs["mem_norm_w_2"][0]),
            channel_columns(inputs["ssd_conv_w_2"][0].T).reshape(P, -1), channel_columns(inputs["ssd_conv_b_2"][0]),
            heads], axis=1)),
        "positions": np.ascontiguousarray(inputs["positions_2"][0].reshape(NT, P).T),
        "sub_keys": np.ascontiguousarray(inputs["peer_sub_keys_2"][0].reshape(-1, PEER_KEYS, P).transpose(2, 0, 1)),
        "ssd_d_row": inputs["ssd_d_2"], "ssd_g_row": inputs["ssd_norm_w_2"], "dil_q_row": inputs["dil_q_norm_w_2"],
        "dil_k_row": inputs["dil_k_norm_w_2"], "mem_q_row": inputs["mem_q_norm_w_2"],
        "mem_k_row": inputs["mem_k_norm_w_2"], "ffn_g_row_2": inputs["norm_ffn_w_2"],
        "final_g_row": inputs["final_norm_g"].reshape(1, D),
        **{k: inputs[k] for k in ("mem_2", "w_in_2", "w_mem_kv_2", "w_ssd_br_2", "w_dil_br_2", "w_mem_br_2",
                                  "w_out_2", "peer_w_query_2", "peer_down_2", "peer_up_2")},
        "p_cols_1": np.ascontiguousarray(cat([
            channel_columns(inputs["mix_norm_g"][0]), channel_columns(inputs["ffn_norm_g"][0]),
            conv.reshape(P, -1), channel_columns(inputs["conv_b"][0]), gate_b], axis=1)),
        "decay_logit": inputs["ret_decay_logit"][0].reshape(1, 8),
        "ret_gn_row": inputs["ret_gn_g"], "mlstm_gn_row": inputs["mlstm_gn_g"], "ffn_g_row": inputs["ffn_norm_g"],
        **{k: inputs[k] for k in ("x", "meta_tokens", "w_in", "w_out", "w_router", "w_gate", "w_up", "w_down")},
    }


def kernel(**inputs):
    import concourse.bacc as bacc
    import numpy as np
    from concourse.bass_utils import run_bass_kernel_spmd

    nc = bacc.Bacc("TRN2", target_bir_lowering=False, num_devices=1)
    arrays, io = {}, {}
    for name, a in {**constants(), **layouts({k: np.asarray(v) for k, v in inputs.items()})}.items():
        arrays[f"in_{name}"] = np.ascontiguousarray(a)
        io[name] = nc.dram_tensor(f"in_{name}", a.shape, mybir.dt.from_np(a.dtype), kind="ExternalInput").ap()
    out = nc.dram_tensor("result", (1, SEQ, D), F32, kind="ExternalOutput").ap()
    two_blocks(nc, io, out[0])
    done = run_bass_kernel_spmd(nc, [arrays], core_ids=[0])
    return done.results[0]["result"]
```

```python
from contextlib import ExitStack, contextmanager

import concourse.bass as bass
from concourse import mybir

ALU = mybir.AluOpType
ACT = mybir.ActivationFunctionType
F32 = mybir.dt.float32
I32 = mybir.dt.int32
U32 = mybir.dt.uint32
F32R = mybir.dt.float32r
AX_X = mybir.AxisListType.X

P = 128
D = 1024
KD = D // P
SEQ = 512
META = 16
TOK = SEQ + META
HALF = TOK // 2
EPS = 1e-6
NEG = -1e30
NT = SEQ // P

X_TILES = [(i, P, META + P * i) for i in range(NT)]
META_TILE = (NT, META, 0)
ALL_TILES = X_TILES + [META_TILE]
BY_POSITION = [META_TILE] + X_TILES

HEADS = 4
MIX = D // 2
N_GATES = 4 * HEADS
CONV_K = 5
REL_BASE = 400
REL_W = REL_BASE + TOK

EXPERTS = 16
CAP = 2 * TOK // EXPERTS
D_FF = 128 * ((8 * D // 3 + 127) // 128)
SLOTS = EXPERTS * CAP
TOP_ROUNDS = (CAP + 7) // 8

COLS_1 = {}
for _name, _count in (("mix_g", KD), ("ffn_g", KD), ("conv_w", KD * CONV_K), ("conv_b", KD), ("gate_b", 4)):
    COLS_1[_name] = (sum(c for _, c in COLS_1.values()), _count)
COLS_1_N = sum(c for _, c in COLS_1.values())


class Stage:

    def __init__(self, nc, name):
        self.nc, self.name, self.stack = nc, name, ExitStack()

    def __enter__(self):
        return self

    def __exit__(self, kind, *_):
        if kind is None:
            self.stack.close()

    def sb(self, name, shape, dt=F32, side="left"):
        return self.stack.enter_context(self.nc.sbuf_tensor(f"{self.name}_{name}", shape, dt, side=side))

    def ps(self, name, shape, dt=F32):
        return self.stack.enter_context(self.nc.psum_tensor(f"{self.name}_{name}", shape, dt))

    def sem(self, name):
        return self.nc.alloc_semaphore(f"{self.name}_{name}")


@contextmanager
def own_semaphores(nc):
    before = nc.snapshot_sems()
    yield
    nc.clear_and_free_semaphores(nc.allocated_since(before))
    nc.all_engine_barrier()


class InOrder:

    def __init__(self, eng, sem):
        self.eng, self.sem, self.n = eng, sem, 0

    def issue(self, ins):
        self.n += 1
        ins.then_inc(self.sem, 1)

    def settle(self):
        self.eng.wait_ge(self.sem, self.n)

    def __call__(self, ins):
        self.issue(ins)
        self.settle()


def load(nc, name, pairs):
    with Stage(nc, name) as st:
        landed = st.sem("landed")
        with nc.Block() as block:

            @block.sync
            def _(sp):
                for dst, src in pairs:
                    sp.dma_start(dst, src).then_inc(landed, 16)
                sp.wait_ge(landed, 16 * len(pairs))


def normalise(nc, name, x, tiles, gain_col, ident, xT, gain_row=None, kept=None):
    n_tiles = len(tiles)
    split = isinstance(xT, tuple)
    with Stage(nc, name) as st:
        ssq = st.sb("ssq", [P, n_tiles])
        inv = st.sb("inv", [P, n_tiles])
        rstd = st.sb("rstd", [P, n_tiles])
        squares = st.sb("squares", [P, 2, D])
        scaled = st.sb("scaled", [P, 2, D])
        turned = st.ps("turned", [P, 2, D])
        gained = st.sb("gained", [P, 2, KD, P]) if split and kept is None else None
        gain_done, high_done = st.sem("gain_done"), st.sem("high_done")
        cleared, squared, inverted, rooted = (st.sem(s) for s in ("cleared", "squared", "inverted", "rooted"))
        scale_done, turn_done, evac_done = st.sem("scale_done"), st.sem("turn_done"), st.sem("evac_done")
        dve_order = st.sem("dve_order")

        def turned_of(n):
            return turned[:, n % 2, :].rearrange("p (k c) -> p k c", k=KD)[:, :, 0:tiles[n][1]]

        def to_split(n):
            return gained[:, n % 2, :, 0:tiles[n][1]] if kept is None else turned_of(n)

        def part(buf, n):
            _, rows, col = tiles[n]
            return buf[:, :, col:col + rows]

        def row(n):
            i, rows, _ = tiles[n]
            return kept[:rows, i, :] if kept is not None else scaled[:rows, n % 2, :]

        with nc.Block() as block:

            @block.scalar
            def _(act):
                act.wait_ge(cleared, 1)
                for n, (i, rows, _) in enumerate(tiles):
                    if n >= 2:
                        act.wait_ge(squared, n - 1)
                    act.activation(squares[:rows, n % 2, :], x[:rows, i, :], ACT.Square,
                                   accum_out=ssq[:rows, n:n + 1]).then_inc(squared, 1)
                act.wait_ge(inverted, 1)
                act.activation(rstd[:, :], inv[:, :], ACT.Sqrt).then_inc(rooted, 1)
                for n in range(n_tiles if split else 0):
                    if kept is None:
                        act.wait_ge(gain_done, n + 1)
                    else:
                        act.wait_ge(turn_done, n + 1)
                    act.copy(part(xT[0], n), to_split(n)).then_inc(high_done, 1)

            @block.vector
            def _(dve):
                order = InOrder(dve, dve_order)
                dve.memset(ssq[:, :], 1.0).then_inc(cleared, 1)
                dve.wait_ge(squared, n_tiles)
                order(dve.tensor_scalar(ssq[:, :], ssq[:, :], 1.0 / D, EPS, ALU.mult, ALU.add))
                dve.reciprocal(inv[:, :], ssq[:, :]).then_inc(inverted, 1)
                dve.wait_ge(rooted, 1)

                def scale(n):
                    i, rows, _ = tiles[n]
                    if n >= 2 and kept is None:
                        dve.wait_ge(turn_done, n - 1)
                    if kept is None:
                        dve.tensor_scalar(row(n), x[:rows, i, :], rstd[:rows, n:n + 1], None,
                                          ALU.mult).then_inc(scale_done, 1)
                    else:
                        dve.scalar_tensor_tensor(row(n), x[:rows, i, :], rstd[:rows, n:n + 1],
                                                 gain_row[:rows, :], ALU.mult, ALU.mult).then_inc(scale_done, 1)

                def evacuate(n):
                    _, rows, col = tiles[n]
                    dve.wait_ge(turn_done, n + 1)
                    gain = gain_col.unsqueeze(2).broadcast_to([P, KD, rows]) if kept is None else None
                    if split:
                        if kept is None:
                            dve.tensor_tensor(to_split(n), turned_of(n), gain, ALU.mult).then_inc(gain_done, 1)
                        dve.wait_ge(high_done, n + 1)
                        dve.tensor_tensor(part(xT[1], n), to_split(n), part(xT[0], n).bitcast(F32),
                                          ALU.subtract).then_inc(evac_done, 1)
                    elif kept is None:
                        dve.tensor_tensor(part(xT, n), turned_of(n), gain, ALU.mult).then_inc(evac_done, 1)
                    else:
                        dve.tensor_copy(part(xT, n), turned_of(n)).then_inc(evac_done, 1)

                scale(0)
                for n in range(n_tiles):
                    if n + 1 < n_tiles:
                        scale(n + 1)
                    if xT is not None:
                        evacuate(n)
                dve.wait_ge(scale_done, n_tiles)

            @block.tensor
            def _(pe):
                for n, (_, rows, _) in enumerate(tiles if xT is not None else []):
                    pe.wait_ge(scale_done, n + 1)
                    if n >= 2:
                        pe.wait_ge(evac_done, n - 1)
                    for k in range(KD):
                        last = pe.transpose(turned[:, n % 2, k * P:k * P + rows],
                                            row(n)[:, k * P:(k + 1) * P], ident[:rows, :rows])
                    last.then_inc(turn_done, 1)


class Job:

    def __init__(self, kind, offset, width, emit, eng, col=0, rows=P, parts=1, tokens=SEQ, after=None):
        self.kind, self.offset, self.width, self.emit, self.eng = kind, offset, width, emit, eng
        self.col, self.rows, self.parts, self.tokens, self.after = col, rows, parts, tokens, after


def token_jobs(tiles, width, emit, eng="act"):
    return [Job("token", 0, width, (lambda nc, ps, i=i, rows=rows: emit(nc, i, rows, ps)), eng, col=col, rows=rows)
            for i, rows, col in tiles]


def added_chunks(w, source, x, tiles):
    return [(w[:, :, n * 256:(n + 1) * 256], source, token_jobs(
        tiles, 256, lambda nc, i, r, ps, n=n: nc.vector.tensor_tensor(
            x[:r, i, n * 256:(n + 1) * 256], x[:r, i, n * 256:(n + 1) * 256], ps, ALU.add), "dve"))
        for n in range(D // 256)]


def halves(ap):
    return ap.rearrange("p (a b) -> p a b", a=2)


def split_matmul(pe, out, hi_l, lo_l, hi_r, lo_r, start, stop):
    pe.matmul(out, hi_l, hi_r, start=start, stop=False)
    pe.matmul(out, lo_l, hi_r, start=False, stop=False)
    return pe.matmul(out, hi_l, lo_r, start=False, stop=stop)


def project(nc, name, chunks, wide=256, k_max=KD):
    slots = 4
    jobs = [(c, job) for c, (_, _, js) in enumerate(chunks) for job in js]
    last_of_chunk = {c: max(n for n, (cc, _) in enumerate(jobs) if cc == c) for c in range(len(chunks))}
    place = []
    taken = {"act": 0, "dve": 0}
    for _, job in jobs:
        taken[job.eng] += 1
        place.append((job.eng, taken[job.eng]))
    with Stage(nc, name) as st:
        raw = st.sb("raw", [P, 2, k_max, wide])
        high = st.sb("high", [P, 2, k_max, wide], F32R)
        low = st.sb("low", [P, 2, k_max, wide], F32R)
        out = st.ps("out", [P, slots, 2 * 512])
        raw_in = [st.sem("raw_in0"), st.sem("raw_in1")]
        high_done, low_done, product_done = st.sem("high_done"), st.sem("low_done"), st.sem("product_done")
        taken_by = {"act": st.sem("taken_by_act"), "dve": st.sem("taken_by_dve")}

        def view(n, job):
            if job.kind == "token":
                return out[:job.rows, n % slots, 0:job.width]
            each = job.tokens // job.parts
            v = out[:job.width, n % slots, :].rearrange("p (a b) -> p a b", a=2)
            return v[:, 0:job.parts, 0:each] if job.parts > 1 else v[:, 0, 0:each]

        def slot_of(ring, c):
            kp, nk, cols = chunks[c][0].shape
            return ring[:kp, c % 2, 0:nk, 0:cols]

        with nc.Block() as block:

            @block.sync
            def _(sp):
                for c, (w, _, _) in enumerate(chunks):
                    if c >= 2:
                        sp.wait_ge(low_done, c - 1)
                    sp.dma_start(slot_of(raw, c), w).then_inc(raw_in[c % 2], 16)

            @block.tensor
            def _(pe):
                for n, (c, job) in enumerate(jobs):
                    w, (s_high, s_low), _ = chunks[c]
                    kp, nk, _ = w.shape
                    pe.wait_ge(high_done, c + 1)
                    pe.wait_ge(low_done, c + 1)
                    if n >= slots:
                        eng, count = place[n - slots]
                        pe.wait_ge(taken_by[eng], count)
                    mine = slice(job.offset, job.offset + job.width)
                    for a in range(job.parts):
                        each = job.tokens // job.parts
                        for k in range(nk):
                            w_high, w_low = high[:kp, c % 2, k, mine], low[:kp, c % 2, k, mine]
                            if job.kind == "token":
                                rows = slice(job.col, job.col + job.rows)
                                last = split_matmul(pe, out[:job.rows, n % slots, 0:job.width],
                                                    s_high[:, k, rows], s_low[:, k, rows], w_high, w_low,
                                                    start=(k == 0), stop=(k == nk - 1))
                            else:
                                rows = slice(job.col + a * each, job.col + (a + 1) * each)
                                last = split_matmul(pe, out[:job.width, n % slots, a * 512:a * 512 + each],
                                                    w_high, w_low, s_high[:, k, rows], s_low[:, k, rows],
                                                    start=(k == 0), stop=(k == nk - 1))
                    last.then_inc(product_done, 1)

            def split_and_take_out(engine, which, split):
                split(0)
                if len(chunks) > 1:
                    split(1)
                for n, (c, job) in enumerate(jobs):
                    if job.eng == which:
                        engine.wait_ge(product_done, n + 1)
                        if job.after is not None:
                            eng, count = place[job.after]
                            engine.wait_ge(taken_by[eng], count)
                        job.emit(nc, view(n, job)).then_inc(taken_by[which], 1)
                    if n == last_of_chunk[c] and c + 2 < len(chunks):
                        engine.wait_ge(product_done, n + 1)
                        split(c + 2)

            @block.scalar
            def _(act):
                def split(c):
                    act.wait_ge(raw_in[c % 2], 16 * (c // 2 + 1))
                    act.copy(slot_of(high, c), slot_of(raw, c)).then_inc(high_done, 1)

                split_and_take_out(act, "act", split)

            @block.vector
            def _(dve):
                def split(c):
                    dve.wait_ge(high_done, c + 1)
                    dve.tensor_tensor(slot_of(low, c), slot_of(raw, c), slot_of(high, c).bitcast(F32),
                                      ALU.subtract).then_inc(low_done, 1)

                split_and_take_out(dve, "dve", split)


def split_of(st, name, shape, side="left"):
    return st.sb(name + "_high", shape, F32R, side=side), st.sb(name + "_low", shape, F32R, side=side)


def split_buffers(nc, name, pairs):
    with Stage(nc, name) as st:
        high_done, low_done = st.sem("high_done"), st.sem("low_done")
        with nc.Block() as block:

            @block.scalar
            def _(act):
                for src, (high, _) in pairs:
                    act.copy(high, src).then_inc(high_done, 1)

            @block.vector
            def _(dve):
                for n, (src, (high, low)) in enumerate(pairs):
                    dve.wait_ge(high_done, n + 1)
                    dve.tensor_tensor(low, src, high.bitcast(F32), ALU.subtract).then_inc(low_done, 1)
                dve.wait_ge(low_done, len(pairs))


def head_norm(dve, order, act_sem, dve_sem, y, tiles, stats, moments, inv):
    for n, (i, rows, _) in enumerate(tiles):
        for h in range(HEADS):
            c = n * HEADS + h
            order(dve.bn_stats(stats[:rows, c, :], y[:rows, i, h * P:(h + 1) * P]))
            order(dve.bn_aggr(moments[:rows, c, :], stats[:rows, c, :]))
    order(dve.tensor_scalar(inv[:, :], moments[:, :, 1], EPS, None, ALU.add))
    dve.reciprocal(inv[:, :], inv[:, :]).then_inc(dve_sem, 1)
    dve.wait_ge(act_sem, 1)
    for n, (i, rows, _) in enumerate(tiles):
        for h in range(HEADS):
            c = n * HEADS + h
            last = dve.tensor_scalar(y[:rows, i, h * P:(h + 1) * P], y[:rows, i, h * P:(h + 1) * P],
                                     moments[:rows, c, 0:1], inv[:rows, c:c + 1], ALU.subtract, ALU.mult)
            order(last)


def retention(nc, io, rqk, rv, rg, y):
    scale = float(P) ** -0.5
    n_t = len(ALL_TILES)
    with Stage(nc, "ret") as st:
        cos = st.sb("cos", [P, TOK])
        sin = st.sb("sin", [P, TOK])
        swapped = st.sb("swapped", [P, HEADS, TOK])
        ahead = st.sb("ahead", [P, REL_W])
        behind = st.sb("behind", [P, REL_W])
        diag = st.sb("diag", [P, REL_W])
        arg = st.sb("arg", [P, REL_W])
        decay = st.sb("decay", [P, 2, REL_W])
        logit = st.sb("logit", [P, 8])
        lg = st.sb("lg", [P, 8])
        tmp8 = st.sb("tmp8", [P, 8])
        gn = st.sb("gn", [P, MIX])
        weighted = st.sb("weighted", [P, 2, n_t, TOK])
        stats = st.sb("stats", [P, n_t * HEADS, 6])
        moments = st.sb("moments", [P, n_t * HEADS, 2])
        inv = st.sb("inv", [P, n_t * HEADS])
        scores = st.ps("scores", [P, 2, 1024])
        mixed = st.ps("mixed", [P, 4, 512])
        landed, rot_half, rotated, abs_done, soft_done, arg_done = (
            st.sem(s) for s in ("landed", "rot_half", "rotated", "abs_done", "soft_done", "arg_done"))
        exp_done, decay_ready, scored, weighted_ready, mix_done, mix_out = (
            st.sem(s) for s in ("exp_done", "decay_ready", "scored", "weighted_ready", "mix_done", "mix_out"))
        var_ready, root_ready, dve_order, act_order = (
            st.sem(s) for s in ("var_ready", "root_ready", "dve_order", "act_order"))

        with nc.Block() as block:

            @block.sync
            def _(sp):
                for dst, src in ((cos[:, :], io["c_cos"]), (sin[:, :], io["c_sin"]), (ahead[:, :], io["c_ahead"]),
                                 (behind[:, :], io["c_behind"]), (diag[:, :], io["c_diag"]),
                                 (logit[:, :], io["decay_logit"].partition_broadcast(P)),
                                 (gn[:, :], io["ret_gn_row"].partition_broadcast(P))):
                    sp.dma_start(dst, src).then_inc(landed, 16)
                sp.wait_ge(landed, 7 * 16)

            @block.scalar
            def _(act):
                order = InOrder(act, act_order)
                for g in range(2):
                    if g:
                        act.wait_ge(rotated, 1)
                    order(act.copy(swapped[0:64, :, :], rqk[64:P, g * HEADS:(g + 1) * HEADS, :]))
                    act.copy(swapped[64:P, :, :], rqk[0:64, g * HEADS:(g + 1) * HEADS, :]).then_inc(rot_half, 1)
                act.wait_ge(abs_done, 1)
                order(act.activation(tmp8[:, :], tmp8[:, :], ACT.Exp, scale=-1.0))
                act.activation(tmp8[:, :], tmp8[:, :], ACT.Ln, bias=1.0).then_inc(soft_done, 1)
                for h in range(HEADS):
                    act.wait_ge(arg_done, h + 1)
                    act.activation(arg[:, :], arg[:, :], ACT.Exp).then_inc(exp_done, 1)
                    for n, (i, rows, _) in enumerate(ALL_TILES):
                        m = h * n_t + n
                        act.wait_ge(mix_done, m + 1)
                        act.copy(y[:rows, i, h * P:(h + 1) * P], mixed[:rows, m % 4, 0:P]).then_inc(mix_out, 1)
                act.wait_ge(var_ready, 1)
                act.activation(inv[:, :], inv[:, :], ACT.Sqrt).then_inc(root_ready, 1)

            @block.vector
            def _(dve):
                order = InOrder(dve, dve_order)
                order(dve.memset(moments[:, :, :], 1.0))
                dve.wait_ge(landed, 7 * 16)
                for g in range(2):
                    x = rqk[:, g * HEADS:(g + 1) * HEADS, :]
                    dve.wait_ge(rot_half, g + 1)
                    order(dve.tensor_tensor(x, x, cos[:, :].unsqueeze(1).broadcast_to([P, HEADS, TOK]), ALU.mult))
                    order(dve.tensor_tensor(swapped[:, :, :], swapped[:, :, :],
                                            sin[:, :].unsqueeze(1).broadcast_to([P, HEADS, TOK]), ALU.mult))
                    dve.tensor_tensor(x, x, swapped[:, :, :], ALU.add).then_inc(rotated, 1)
                dve.scalar_tensor_tensor(tmp8[:, :], logit[:, :], -1.0, logit[:, :], ALU.mult,
                                         ALU.max).then_inc(abs_done, 1)
                dve.wait_ge(soft_done, 1)
                order(dve.scalar_tensor_tensor(lg[:, :], logit[:, :], 0.0, tmp8[:, :], ALU.min, ALU.subtract))
                for h in range(HEADS):
                    order(dve.tensor_scalar(arg[:, :], ahead[:, :], lg[:, h:h + 1], None, ALU.mult))
                    dve.scalar_tensor_tensor(arg[:, :], behind[:, :], lg[:, HEADS + h:HEADS + h + 1], arg[:, :],
                                             ALU.mult, ALU.add).then_inc(arg_done, 1)
                    dve.wait_ge(exp_done, h + 1)
                    if h >= 1:
                        dve.wait_ge(weighted_ready, n_t * h)
                    dve.tensor_tensor(decay[:, h % 2, :], arg[:, :], diag[:, :], ALU.mult).then_inc(decay_ready, 1)
                    dve.wait_ge(decay_ready, h + 1)
                    for n, (_, rows, col) in enumerate(ALL_TILES):
                        m = h * n_t + n
                        dve.wait_ge(scored, m + 1)
                        if h >= 2:
                            dve.wait_ge(mix_done, n_t * (h - 1))
                        first = REL_BASE - col
                        dve.scalar_tensor_tensor(
                            halves(weighted[:rows, h % 2, n, :]),
                            scores[:rows, m % 2, :].rearrange("p (a b) -> p a b", a=2)[:, :, 0:HALF], scale,
                            halves(decay[:rows, h % 2, first:first + TOK]), ALU.mult, ALU.mult,
                        ).then_inc(weighted_ready, 1)
                dve.wait_ge(mix_out, n_t * HEADS)
                head_norm(dve, order, root_ready, var_ready, y, ALL_TILES, stats, moments, inv)
                for i, rows, _ in ALL_TILES:
                    order(dve.tensor_tensor(y[:rows, i, 0:MIX], y[:rows, i, 0:MIX], gn[:rows, :], ALU.mult))
                    order(dve.tensor_tensor(y[:rows, i, 0:MIX], y[:rows, i, 0:MIX], rg[:rows, i, :], ALU.mult))

            @block.tensor
            def _(pe):
                pe.wait_ge(rotated, 2)
                for h in range(HEADS):
                    for n, (_, rows, col) in enumerate(ALL_TILES):
                        m = h * n_t + n
                        if m >= 2:
                            pe.wait_ge(weighted_ready, m - 1)
                        for a in range(2):
                            last = pe.matmul(scores[:rows, m % 2, a * 512:a * 512 + HALF],
                                             rqk[:, HEADS + h, col:col + rows],
                                             rqk[:, h, a * HALF:(a + 1) * HALF], start=True, stop=True)
                        last.then_inc(scored, 1)
                    pe.wait_ge(weighted_ready, n_t * (h + 1))
                    for n, (_, rows, col) in enumerate(ALL_TILES):
                        m = h * n_t + n
                        if m >= 4:
                            pe.wait_ge(mix_out, m - 3)
                        for s, (si, srows, _) in enumerate(ALL_TILES):
                            last = pe.matmul(mixed[:rows, m % 4, 0:P], weighted[:srows, h % 2, s, col:col + rows],
                                             rv[:srows, si, h * P:(h + 1) * P],
                                             start=(s == 0), stop=(s == n_t - 1))
                        last.then_inc(mix_done, 1)


def mlstm_gates(nc, io, cols, gates, ident, g_col, exp_col, max_rows, scratch):
    with Stage(nc, "mlg") as st:
        ones = st.sb("ones", [HEADS, TOK])
        soft = st.sb("soft", [HEADS, 2, TOK])
        lf = st.sb("lf", [HEADS, 2, TOK])
        run = st.sb("run", [HEADS, 2, TOK])
        rows4 = st.sb("rows4", [HEADS, 4, TOK])
        top = st.sb("top", [HEADS, 2, TOK])
        turned = st.ps("turned", [P, len(ALL_TILES), 16])
        abs_done, soft_done, top_done, rows_done, turn_done, copied, stored, landed, dve_order, act_order = (
            st.sem(s) for s in ("abs_done", "soft_done", "top_done", "rows_done", "turn_done", "copied", "stored",
                                "landed", "dve_order", "act_order"))
        first = COLS_1["gate_b"][0]

        with nc.Block() as block:

            @block.vector
            def _(dve):
                order = InOrder(dve, dve_order)
                order(dve.memset(ones[:, :], 1.0))
                for g in range(4):
                    order(dve.tensor_scalar(gates[:, g, :], gates[:, g, :], cols[:HEADS, first + g:first + g + 1],
                                            None, ALU.add))
                forget = gates[:, 2:4, :]
                dve.scalar_tensor_tensor(soft[:, :, :], forget, -1.0, forget, ALU.mult,
                                         ALU.max).then_inc(abs_done, 1)
                dve.wait_ge(soft_done, 1)
                order(dve.scalar_tensor_tensor(lf[:, :, :], forget, 0.0, soft[:, :, :], ALU.min, ALU.subtract))
                for d in range(2):
                    def way(ap):
                        return ap if d == 0 else ap[:, ::-1]
                    order(dve.tensor_tensor_scan(way(run[:, d, :]), ones[:, :], way(lf[:, d, :]), 0.0,
                                                 ALU.mult, ALU.add))
                    order(dve.tensor_tensor(rows4[:, d, :], gates[:, d, :], run[:, d, :], ALU.subtract))
                    order(dve.tensor_tensor_scan(way(top[:, d, :]), ones[:, :], way(rows4[:, d, :]), 0.0,
                                                 ALU.mult, ALU.max))
                    order(dve.tensor_tensor(rows4[:, 2 + d, :], run[:, d, :], top[:, d, :], ALU.add))
                dve.sem_inc(rows_done, 1)
                dve.wait_ge(turn_done, 1)
                for i, rows, _ in ALL_TILES:
                    order(dve.tensor_copy(g_col[:rows, i, :], turned[:rows, i, 0:8]))
                dve.sem_inc(copied, 1)

            @block.scalar
            def _(act):
                order = InOrder(act, act_order)
                act.wait_ge(abs_done, 1)
                order(act.activation(soft[:, :, :], soft[:, :, :], ACT.Exp, scale=-1.0))
                act.activation(soft[:, :, :], soft[:, :, :], ACT.Ln, bias=1.0).then_inc(soft_done, 1)
                act.wait_ge(copied, 1)
                for i, rows, _ in ALL_TILES:
                    order(act.activation(exp_col[:rows, i, :], turned[:rows, i, 8:16], ACT.Exp, scale=-1.0))

            @block.tensor
            def _(pe):
                pe.wait_ge(rows_done, 1)
                for i, rows, col in ALL_TILES:
                    for g in range(4):
                        last = pe.transpose(turned[:rows, i, g * HEADS:(g + 1) * HEADS],
                                            rows4[:, g, col:col + rows], ident[:HEADS, :HEADS])
                last.then_inc(turn_done, 1)

            @block.sync
            def _(sp):
                sp.wait_ge(rows_done, 1)
                sp.dma_start(scratch, top[:, :, :]).then_inc(stored, 16)
                sp.wait_ge(stored, 16)
                for h in range(HEADS):
                    for d in range(2):
                        sp.dma_start(max_rows[:, 2 * h + d, :], scratch[h, d:d + 1, :].partition_broadcast(P)
                                     ).then_inc(landed, 16)
                sp.wait_ge(landed, 16 * 8)


def conv_silu(nc, name, padded, n_tiles, taps, tokens, weight, bias, out):
    with Stage(nc, name) as st:
        acc = st.sb("acc", [P, 2, tokens])
        conv_done, silu_done, dve_order = st.sem("conv_done"), st.sem("silu_done"), st.sem("dve_order")

        with nc.Block() as block:

            @block.vector
            def _(dve):
                order = InOrder(dve, dve_order)
                for c in range(n_tiles):
                    if c >= 2:
                        dve.wait_ge(silu_done, c - 1)
                    a = acc[:, c % 2, :]
                    order(dve.tensor_scalar(a, padded[:, c, 0:tokens], weight(c, 0), bias(c), ALU.mult, ALU.add))
                    for j in range(1, taps):
                        ins = dve.scalar_tensor_tensor(a, padded[:, c, j:j + tokens], weight(c, j), a,
                                                       ALU.mult, ALU.add)
                        if j < taps - 1:
                            order(ins)
                    ins.then_inc(conv_done, 1)

            @block.scalar
            def _(act):
                for c in range(n_tiles):
                    act.wait_ge(conv_done, c + 1)
                    act.activation(out[:, c, 0:tokens], acc[:, c % 2, :], ACT.Silu).then_inc(silu_done, 1)
                act.wait_ge(silu_done, n_tiles)


def clear(nc, name, aps, value=0.0):
    with Stage(nc, name) as st:
        done = st.sem("done")
        with nc.Block() as block:

            @block.vector
            def _(dve):
                for ap in aps:
                    dve.memset(ap, value).then_inc(done, 1)
                dve.wait_ge(done, len(aps))


def mlstm(nc, io, qk, v1, mo, y, g_col, exp_col, max_rows):
    scale = float(P) ** -0.5
    order_of = BY_POSITION
    n_t = len(order_of)
    passes = [(h, d) for h in range(HEADS) for d in range(2)]
    with Stage(nc, "mls") as st:
        raw = st.sb("raw", [P, n_t, TOK])
        arg = st.sb("arg", [P, 3, TOK])
        weight = st.sb("weight", [P, 2, n_t, TOK])
        keep = st.sb("keep", [P, 2, P])
        gn = st.sb("gn", [P, MIX])
        den = st.sb("den", [P, 4])
        stats = st.sb("stats", [P, n_t * HEADS, 6])
        moments = st.sb("moments", [P, n_t * HEADS, 2])
        inv = st.sb("inv", [P, n_t * HEADS])
        scores = st.ps("scores", [P, 2, 1024])
        mixed = st.ps("mixed", [P, 4, 512])
        landed, scored, raw_ready, arg_ready, exp_ready, weight_ready, mix_done, mix_out = (
            st.sem(s) for s in ("landed", "scored", "raw_ready", "arg_ready", "exp_ready", "weight_ready",
                                "mix_done", "mix_out"))
        var_ready, root_ready, dve_order, act_order = (
            st.sem(s) for s in ("var_ready", "root_ready", "dve_order", "act_order"))

        def span(d, col, rows):
            return (col, TOK) if d == 0 else (0, col + rows)

        with nc.Block() as block:

            @block.sync
            def _(sp):
                sp.dma_start(keep[:, :, :], io["c_keep"]).then_inc(landed, 16)
                sp.dma_start(gn[:, :], io["mlstm_gn_row"].partition_broadcast(P)).then_inc(landed, 16)
                sp.wait_ge(landed, 32)

            @block.scalar
            def _(act):
                for p, (h, d) in enumerate(passes):
                    if d == 0:
                        if h >= 1:
                            act.wait_ge(weight_ready, n_t * p)
                        for n, (_, rows, _) in enumerate(order_of):
                            act.wait_ge(scored, h * n_t + n + 1)
                            act.activation(halves(raw[:rows, n, :]),
                                           scores[:rows, (h * n_t + n) % 2, :].rearrange(
                                               "p (a b) -> p a b", a=2)[:, :, 0:HALF],
                                           ACT.Copy, scale=scale).then_inc(raw_ready, 1)
                    for n, (_, rows, col) in enumerate(order_of):
                        m = p * n_t + n
                        lo, hi = span(d, col, rows)
                        act.wait_ge(arg_ready, m + 1)
                        act.activation(arg[:rows, m % 3, lo:hi], arg[:rows, m % 3, lo:hi], ACT.Exp,
                                       scale=-1.0).then_inc(exp_ready, 1)
                act.wait_ge(var_ready, 1)
                act.activation(inv[:, :], inv[:, :], ACT.Sqrt).then_inc(root_ready, 1)

            @block.vector
            def _(dve):
                order = InOrder(dve, dve_order)
                order(dve.memset(moments[:, :, :], 1.0))
                dve.wait_ge(landed, 32)

                def exponents(p, n):
                    h, d = passes[p]
                    i, rows, col = order_of[n]
                    m = p * n_t + n
                    lo, hi = span(d, col, rows)
                    if m >= 3:
                        dve.wait_ge(weight_ready, m - 2)
                    dve.tensor_scalar(arg[:rows, m % 3, lo:hi], max_rows[:rows, 2 * h + d, lo:hi],
                                      g_col[:rows, i, d * HEADS + h:d * HEADS + h + 1], 0.0,
                                      ALU.subtract, ALU.max).then_inc(arg_ready, 1)

                def weigh(p, n):
                    h, d = passes[p]
                    _, rows, col = order_of[n]
                    m = p * n_t + n
                    lo, hi = span(d, col, rows)
                    dve.wait_ge(exp_ready, m + 1)
                    if p >= 2:
                        dve.wait_ge(mix_done, n_t * (p - 1))
                    if n == 0:
                        dve.wait_ge(raw_ready, n_t * (h + 1))
                    order(dve.tensor_tensor(weight[:rows, p % 2, n, lo:hi], arg[:rows, m % 3, lo:hi],
                                            raw[:rows, n, lo:hi], ALU.mult))
                    dve.tensor_tensor(weight[:rows, p % 2, n, col:col + rows],
                                      weight[:rows, p % 2, n, col:col + rows], keep[:rows, d, 0:rows],
                                      ALU.mult).then_inc(weight_ready, 1)

                def take_out(p):
                    h, d = passes[p]
                    for n, (i, rows, _) in enumerate(order_of):
                        m = p * n_t + n
                        dve.wait_ge(mix_done, m + 1)
                        ps = mixed[:rows, m % 4, :]
                        c = den[:rows, 0:1]
                        out = y[:rows, i, h * P:(h + 1) * P]
                        order(dve.tensor_scalar(den[:rows, 1:2], ps[:, P:P + 1], -1.0, None, ALU.mult))
                        order(dve.tensor_tensor(c, ps[:, P:P + 1], den[:rows, 1:2], ALU.max))
                        order(dve.tensor_tensor(c, c, exp_col[:rows, i, d * HEADS + h:d * HEADS + h + 1], ALU.max))
                        order(dve.reciprocal(c, c))
                        if d == 0:
                            ins = dve.tensor_scalar(out, ps[:, 0:P], c, None, ALU.mult)
                        else:
                            ins = dve.scalar_tensor_tensor(out, ps[:, 0:P], c, out, ALU.mult, ALU.add)
                        ins.then_inc(mix_out, 1)
                        dve.wait_ge(mix_out, m + 1)

                for p in range(len(passes)):
                    exponents(p, 0)
                    exponents(p, 1)
                    for n in range(n_t):
                        if n + 2 < n_t:
                            exponents(p, n + 2)
                        weigh(p, n)
                    if p >= 1:
                        take_out(p - 1)
                take_out(len(passes) - 1)
                for i, rows, _ in ALL_TILES:
                    order(dve.tensor_tensor(y[:rows, i, :], y[:rows, i, :], mo[:rows, i, :], ALU.mult))
                head_norm(dve, order, root_ready, var_ready, y, ALL_TILES, stats, moments, inv)
                for i, rows, _ in ALL_TILES:
                    order(dve.tensor_tensor(y[:rows, i, :], y[:rows, i, :], gn[:rows, :], ALU.mult))

            @block.tensor
            def _(pe):
                def score(h):
                    for n, (_, rows, col) in enumerate(order_of):
                        m = h * n_t + n
                        if m >= 2:
                            pe.wait_ge(raw_ready, m - 1)
                        for a in range(2):
                            last = pe.matmul(scores[:rows, m % 2, a * 512:a * 512 + HALF],
                                             qk[:, HEADS + h, col:col + rows],
                                             qk[:, h, a * HALF:(a + 1) * HALF], start=True, stop=True)
                        last.then_inc(scored, 1)

                def mix(p):
                    h, d = passes[p]
                    pe.wait_ge(weight_ready, n_t * (p + 1))
                    for n, (_, rows, col) in enumerate(order_of):
                        m = p * n_t + n
                        if m >= 4:
                            pe.wait_ge(mix_out, m - 3)
                        keys = range(0, n + 1) if d == 0 else range(n, n_t)
                        for s in keys:
                            si, srows, _ = order_of[s]
                            last = pe.matmul(mixed[:rows, m % 4, 0:P + 1],
                                             weight[:srows, p % 2, s, col:col + rows], v1[:srows, si, h, :],
                                             start=(s == keys[0]), stop=(s == keys[-1]))
                        last.then_inc(mix_done, 1)

                score(0)
                for h in range(HEADS):
                    mix(2 * h)
                    if h + 1 < HEADS:
                        score(h + 1)
                    mix(2 * h + 1)


def turn_rows(nc, name, x, tiles, ident, xT, k_tiles=KD):
    split = isinstance(xT, tuple)
    with Stage(nc, name) as st:
        turned = st.ps("turned", [P, 2, D])
        turn_done, high_done, taken = st.sem("turn_done"), st.sem("high_done"), st.sem("taken")

        def turned_of(n):
            return turned[:, n % 2, 0:k_tiles * P].rearrange("p (k c) -> p k c", k=k_tiles)[:, :, 0:tiles[n][1]]

        def part(buf, n):
            _, rows, col = tiles[n]
            return buf[:, :, col:col + rows]

        with nc.Block() as block:

            @block.tensor
            def _(pe):
                for n, (i, rows, _) in enumerate(tiles):
                    if n >= 2:
                        pe.wait_ge(taken, n - 1)
                    for k in range(k_tiles):
                        last = pe.transpose(turned[:, n % 2, k * P:k * P + rows], x[:rows, i, k * P:(k + 1) * P],
                                            ident[:rows, :rows])
                    last.then_inc(turn_done, 1)

            @block.scalar
            def _(act):
                for n in range(len(tiles) if split else 0):
                    act.wait_ge(turn_done, n + 1)
                    act.copy(part(xT[0], n), turned_of(n)).then_inc(high_done, 1)

            @block.vector
            def _(dve):
                for n in range(len(tiles)):
                    if split:
                        dve.wait_ge(high_done, n + 1)
                        dve.tensor_tensor(part(xT[1], n), turned_of(n), part(xT[0], n).bitcast(F32),
                                          ALU.subtract).then_inc(taken, 1)
                    else:
                        dve.wait_ge(turn_done, n + 1)
                        dve.tensor_copy(part(xT, n), turned_of(n)).then_inc(taken, 1)


def route(nc, io, u, uT, ident, xs, slot_gate, scratch):
    n_t = len(ALL_TILES)
    parts = [(0, 6), (6, 5), (11, 5)]
    assert sum(n for _, n in parts) == EXPERTS
    with Stage(nc, "route") as st:
        w = st.sb("w", [P, KD, EXPERTS])
        logits = st.sb("logits", [P, n_t, EXPERTS])
        top1 = st.sb("top1", [P, n_t])
        total = st.sb("total", [P, n_t])
        affT = st.sb("affT", [EXPERTS, TOK])
        vals = st.sb("vals", [EXPERTS, TOP_ROUNDS * 8])
        idx = st.sb("idx", [EXPERTS, TOP_ROUNDS * 8], U32)
        idx_f = st.sb("idx_f", [EXPERTS, TOP_ROUNDS * 8])
        idx_all = st.sb("idx_all", [P, SLOTS])
        token_id = st.sb("token_id", [P, n_t])
        onehot = st.sb("onehot", [P, n_t, SLOTS], F32R)
        u_high = st.sb("u_high", [P, n_t, D], F32R)
        u_low = st.sb("u_low", [P, n_t, D], F32R)
        small = st.ps("small", [P, 512])
        turned = st.ps("turned", [P, 1024])
        gathered = st.ps("gathered", [P, 4, 512])
        landed, logits_done, shifted, exp_done, aff_done, turn_done, idx_done, stored, spread = (
            st.sem(s) for s in ("landed", "logits_done", "shifted", "exp_done", "aff_done", "turn_done", "idx_done",
                                "stored", "spread"))
        slot_turned, onehot_done, gather_done, act_taken, dve_taken, dve_order, act_order, u_high_done = (
            st.sem(s) for s in ("slot_turned", "onehot_done", "gather_done", "act_taken", "dve_taken", "dve_order",
                                "act_order", "u_high_done"))
        pieces = [(k, c) for k in range(KD) for c in parts]

        def part_of(m, k, c):
            first, n = c
            return (xs[:, first:first + n, k, :],
                    gathered[:, m % 4, 0:n * CAP].rearrange("p (e c) -> p e c", e=n))

        with nc.Block() as block:

            @block.sync
            def _(sp):
                sp.dma_start(w[:, :, :], io["w_router"][0].rearrange("(k p) e -> p k e", p=P)).then_inc(landed, 16)
                sp.dma_start(token_id[:, :], io["c_token_id"]).then_inc(landed, 16)
                sp.wait_ge(idx_done, 1)
                sp.dma_start(scratch, idx_f[:, 0:CAP]).then_inc(stored, 16)
                sp.wait_ge(stored, 16)
                sp.dma_start(idx_all[:, :], scratch.rearrange("e c -> (e c)").unsqueeze(0).partition_broadcast(P)
                             ).then_inc(spread, 16)
                sp.wait_ge(spread, 16)
                sp.wait_ge(landed, 32)

            @block.tensor
            def _(pe):
                pe.wait_ge(landed, 32)
                for n, (i, rows, col) in enumerate(ALL_TILES):
                    for k in range(KD):
                        last = pe.matmul(small[:rows, i * EXPERTS:(i + 1) * EXPERTS], uT[:, k, col:col + rows],
                                         w[:, k, :], start=(k == 0), stop=(k == KD - 1))
                last.then_inc(logits_done, 1)
                pe.wait_ge(aff_done, 1)
                for i, rows, col in ALL_TILES:
                    at = 512 if i == NT else i * P
                    last = pe.transpose(turned[:EXPERTS, at:at + rows], logits[:rows, i, :], ident[:rows, :rows])
                last.then_inc(turn_done, 1)
                pe.wait_ge(idx_done, 1)
                pe.transpose(small[:CAP, 160:160 + EXPERTS], vals[:, 0:CAP],
                             ident[:EXPERTS, :EXPERTS]).then_inc(slot_turned, 1)
                pe.wait_ge(onehot_done, 1)
                for m, (k, c) in enumerate(pieces):
                    if m >= 4:
                        pe.wait_ge(act_taken if m % 2 == 0 else dve_taken, m // 2 - 1)
                    first, n = c
                    for i, rows, _ in ALL_TILES:
                        for part in (u_high, u_low):
                            last = pe.matmul(gathered[:, m % 4, 0:n * CAP], part[:rows, i, k * P:(k + 1) * P],
                                             onehot[:rows, i, first * CAP:(first + n) * CAP],
                                             start=(i == 0 and part is u_high), stop=(i == NT and part is u_low))
                    last.then_inc(gather_done, 1)

            @block.vector
            def _(dve):
                order = InOrder(dve, dve_order)
                order(dve.memset(logits[:, :, :], 0.0))
                dve.wait_ge(logits_done, 1)
                for i, rows, _ in ALL_TILES:
                    order(dve.tensor_copy(logits[:rows, i, :], small[:rows, i * EXPERTS:(i + 1) * EXPERTS]))
                order(dve.tensor_reduce(top1[:, :], logits[:, :, :], AX_X, ALU.max))
                dve.tensor_tensor(logits[:, :, :], logits[:, :, :],
                                  top1[:, :].unsqueeze(2).broadcast_to([P, n_t, EXPERTS]),
                                  ALU.subtract).then_inc(shifted, 1)
                dve.wait_ge(exp_done, 1)
                order(dve.tensor_reduce(total[:, :], logits[:, :, :], AX_X, ALU.add))
                order(dve.reciprocal(total[:, :], total[:, :]))
                dve.tensor_tensor(logits[:, :, :], logits[:, :, :],
                                  total[:, :].unsqueeze(2).broadcast_to([P, n_t, EXPERTS]),
                                  ALU.mult).then_inc(aff_done, 1)
                dve.wait_ge(turn_done, 1)
                order(dve.tensor_copy(affT[:, META:TOK], turned[:EXPERTS, 0:SEQ]))
                order(dve.tensor_copy(affT[:, 0:META], turned[:EXPERTS, 512:512 + META]))
                for r in range(TOP_ROUNDS):
                    eight = slice(8 * r, 8 * r + 8)
                    order(dve.max(vals[:, eight], affT[:, :]))
                    order(dve.max_index(idx[:, eight], vals[:, eight], affT[:, :]))
                    if r + 1 < TOP_ROUNDS:
                        order(dve.match_replace(affT[:, :], vals[:, eight], affT[:, :], -1.0))
                dve.tensor_copy(idx_f[:, :], idx[:, :]).then_inc(idx_done, 1)
                dve.wait_ge(slot_turned, 1)
                order(dve.tensor_copy(slot_gate[:, :], small[:CAP, 160:160 + EXPERTS]))
                dve.wait_ge(spread, 16)
                for i, rows, _ in ALL_TILES:
                    order(dve.tensor_scalar(onehot[:rows, i, :], idx_all[:rows, :], token_id[:rows, i:i + 1], None,
                                            ALU.is_equal))
                for i, rows, _ in ALL_TILES:
                    dve.wait_ge(u_high_done, i + 1)
                    order(dve.tensor_tensor(u_low[:rows, i, :], u[:rows, i, :], u_high[:rows, i, :].bitcast(F32),
                                            ALU.subtract))
                dve.sem_inc(onehot_done, 1)
                for m, (k, c) in enumerate(pieces):
                    if m % 2:
                        dve.wait_ge(gather_done, m + 1)
                        dve.tensor_copy(*part_of(m, k, c)).then_inc(dve_taken, 1)

            @block.scalar
            def _(act):
                order = InOrder(act, act_order)
                act.wait_ge(shifted, 1)
                act.activation(logits[:, :, :], logits[:, :, :], ACT.Exp).then_inc(exp_done, 1)
                for i, rows, _ in ALL_TILES:
                    act.copy(u_high[:rows, i, :], u[:rows, i, :]).then_inc(u_high_done, 1)
                for m, (k, c) in enumerate(pieces):
                    if m % 2 == 0:
                        act.wait_ge(gather_done, m + 1)
                        act.copy(*part_of(m, k, c)).then_inc(act_taken, 1)


FF_CHUNK = 512
FF_CHUNKS = [(c, min(FF_CHUNK, D_FF - c)) for c in range(0, D_FF, FF_CHUNK)]
FF_N = len(FF_CHUNKS)
FF_BLOCKS = [b for c in range(FF_N) for b in [("gate", c), ("up", c)] + ([("down", c - 2)] if c >= 2 else [])]
FF_BLOCKS += [("down", FF_N - 2), ("down", FF_N - 1)]
FF_NB = len(FF_BLOCKS)
FF_RING = 3


def expert_ffn(nc, io, xs_dram, slot_gate, ident, y_dram):
    assert FF_NB % FF_RING == 0 and FF_N % 2 == 0
    per_slot = FF_NB // FF_RING
    at = {b: q for q, b in enumerate(FF_BLOCKS)}
    tensors = {
        "gate": io["w_gate"][0].rearrange("e (k p) f -> e p k f", p=P),
        "up": io["w_up"][0].rearrange("e (k p) f -> e p k f", p=P),
        "down": io["w_down"][0].rearrange("e (t p) d -> e p t d", p=P),
    }

    def shape_of(q):
        kind, c = FF_BLOCKS[q]
        width = FF_CHUNKS[c][1]
        return (KD, width) if kind != "down" else (width // P, D)

    def block_of(ring, q):
        a, b = shape_of(q)
        return ring[:, q % FF_RING, 0:a * b].rearrange("p (a b) -> p a b", a=a)

    def half_of(ring, q, h):
        a, b = shape_of(q)
        n = a * b // 2
        return ring[:, q % FF_RING, h * n:(h + 1) * n]

    with Stage(nc, "ffn") as st:
        raw = st.sb("raw", [P, FF_RING, KD * FF_CHUNK])
        high = st.sb("high", [P, FF_RING, KD * FF_CHUNK], F32R)
        low = st.sb("low", [P, FF_RING, KD * FF_CHUNK], F32R)
        x_raw = st.sb("x_raw", [P, KD, CAP])
        x_high = st.sb("x_high", [P, KD, CAP], F32R)
        x_low = st.sb("x_low", [P, KD, CAP], F32R)
        silu = st.sb("silu", [CAP, 2, FF_CHUNK])
        hidden = st.sb("hidden", [CAP, 2, FF_CHUNK])
        t_high = st.sb("t_high", [P, 2, FF_CHUNK // P * CAP], F32R)
        t_low = st.sb("t_low", [P, 2, FF_CHUNK // P * CAP], F32R)
        result = st.sb("result", [CAP, D])
        gate_p = st.ps("gate_p", [P, 2, 512])
        up_p = st.ps("up_p", [P, 2, 512])
        turn_p = st.ps("turn_p", [P, 2, 512])
        down_p = st.ps("down_p", [P, D])
        raw_in = [st.sem(f"raw_in{s}") for s in range(FF_RING)]
        high_done, low_done, block_used = (st.sem(s) for s in ("high_done", "low_done", "block_used"))
        x_in, x_high_done, x_low_done = (st.sem(s) for s in ("x_in", "x_high_done", "x_low_done"))
        silu_done, hidden_done, turn_done, t_high_done, t_low_done, result_out, y_stored, result_free = (
            st.sem(s) for s in ("silu_done", "hidden_done", "turn_done", "t_high_done", "t_low_done",
                                "result_out", "y_stored", "result_free"))

        def used(e, kind, c):
            return e * FF_NB + at[(kind, c)] + 1 + FF_RING

        def follow_ups(q):
            steps = []
            for c in range(FF_N):
                if q == at[("up", c)] + 2:
                    steps.append(("hidden", c))
                    if c >= 1:
                        steps.append(("turned", c - 1))
            if q == FF_NB - 1:
                steps.append(("turned", FF_N - 1))
            return steps

        with nc.Block() as block:

            @block.sync
            def _(sp):
                with sp.Fori(0, EXPERTS) as e:
                    for q, (kind, c) in enumerate(FF_BLOCKS):
                        first, width = FF_CHUNKS[c]
                        src = tensors[kind][bass.ds(e, 1)].squeeze(0)
                        if kind == "down":
                            src = src[:, first // P:(first + width) // P, :]
                        else:
                            src = src[:, :, first:first + width]
                        sp.wait_ge(low_done, (e * FF_NB + q) * 2 + 2)
                        sp.dma_start(block_of(raw, q), src).then_inc(raw_in[q % FF_RING], 16)

            @block.gpsimd
            def _(pool):
                pool.sem_inc(result_free, 1)

                def load_x(e):
                    pool.wait_ge(x_low_done, e + 1)
                    pool.dma_start(x_raw[:, :, :].rearrange("p k c -> p (k c)"),
                                   xs_dram[:, bass.ds(e * KD * CAP, KD * CAP)]).then_inc(x_in, 16)

                def store(e):
                    pool.wait_ge(result_out, 2 * e + 4)
                    pool.dma_start(y_dram[bass.ds(e, 1), :, :].squeeze(0), result[:, :]).then_inc(y_stored, 16)
                    pool.wait_ge(y_stored, e * 16 + 16)
                    pool.sem_inc(result_free, 1)

                load_x(0)
                with pool.Fori(1, EXPERTS) as e:
                    load_x(e)
                    store(e - 1)
                store(EXPERTS - 1)

            @block.tensor
            def _(pe):
                pe.sem_inc(block_used, FF_RING)
                pe.sem_inc(turn_done, 2)
                with pe.Fori(0, EXPERTS) as e:

                    def split_in(q):
                        pe.wait_ge(high_done, (e * FF_NB + q) * 2 + 2)
                        pe.wait_ge(low_done, (e * FF_NB + q + FF_RING) * 2 + 2)

                    def columns(kind, c, psum):
                        q, s, width = at[(kind, c)], c % 2, FF_CHUNKS[c][1]
                        split_in(q)
                        hi, lo = block_of(high, q), block_of(low, q)
                        for k in range(KD):
                            last = split_matmul(pe, psum[:CAP, s, 0:width], x_high[:, k, :], x_low[:, k, :],
                                                hi[:, k, :], lo[:, k, :], start=(k == 0), stop=(k == KD - 1))
                        last.then_inc(block_used, 1)

                    def turn(c):
                        s, width = c % 2, FF_CHUNKS[c][1]
                        pe.wait_ge(hidden_done, e * FF_N + c + 3)
                        pe.wait_ge(t_low_done, e * FF_N + c + 1)
                        for t in range(width // P):
                            last = pe.transpose(turn_p[:, s, t * CAP:(t + 1) * CAP],
                                                hidden[:, s, t * P:(t + 1) * P], ident[:CAP, :CAP])
                        last.then_inc(turn_done, 1)

                    def down(c):
                        q, s, width = at[("down", c)], c % 2, FF_CHUNKS[c][1]
                        if c == 0:
                            pe.wait_ge(result_out, 2 * e + 2)
                        split_in(q)
                        pe.wait_ge(t_high_done, e * FF_N + c + 1)
                        pe.wait_ge(t_low_done, e * FF_N + c + 3)
                        hi, lo = block_of(high, q), block_of(low, q)
                        for t in range(width // P):
                            mine = slice(t * CAP, (t + 1) * CAP)
                            for half in range(2):
                                cols = slice(half * 512, (half + 1) * 512)
                                last = split_matmul(pe, down_p[:CAP, cols], t_high[:, s, mine], t_low[:, s, mine],
                                                    hi[:, t, cols], lo[:, t, cols],
                                                    start=(c == 0 and t == 0),
                                                    stop=(c == FF_N - 1 and t == width // P - 1))
                        last.then_inc(block_used, 1)

                    pe.wait_ge(x_high_done, e + 1)
                    pe.wait_ge(x_low_done, e + 2)
                    for c in range(FF_N):
                        pe.wait_ge(hidden_done, e * FF_N + c + 1)
                        columns("gate", c, gate_p)
                        columns("up", c, up_p)
                        if c >= 1:
                            turn(c - 1)
                        if c >= 2:
                            down(c - 2)
                    turn(FF_N - 1)
                    down(FF_N - 2)
                    down(FF_N - 1)

            @block.scalar
            def _(act):
                act.sem_inc(result_out, 2)

                def take_result(e):
                    act.wait_ge(block_used, used(e, "down", FF_N - 1))
                    act.wait_ge(result_free, e + 1)
                    act.activation(result[:, 0:512], down_p[:CAP, 0:512], ACT.Copy,
                                   scale=slot_gate[:, bass.ds(e, 1)]).then_inc(result_out, 1)

                def expert(e, first=False):
                    for q in range(FF_NB):
                        act.wait_ge(block_used, e * FF_NB + q + 1)
                        act.wait_ge(raw_in[q % FF_RING], (e * per_slot + q // FF_RING) * 16 + 16)
                        for h in range(2):
                            act.copy(half_of(high, q, h), half_of(raw, q, h)).then_inc(high_done, 1)
                        if q == 0:
                            act.wait_ge(x_in, e * 16 + 16)
                            act.copy(x_high[:, :, :], x_raw[:, :, :]).then_inc(x_high_done, 1)
                        if q == FF_RING - 1 and not first:
                            take_result(e - 1)
                        for step, c in follow_ups(q):
                            s, width = c % 2, FF_CHUNKS[c][1]
                            if step == "hidden":
                                act.wait_ge(block_used, used(e, "gate", c))
                                act.wait_ge(hidden_done, e * FF_N + c + 1)
                                act.activation(silu[:, s, 0:width], gate_p[:CAP, s, 0:width], ACT.Silu
                                               ).then_inc(silu_done, 1)
                            else:
                                n = width // P * CAP
                                act.wait_ge(turn_done, e * FF_N + c + 3)
                                if c >= 2:
                                    act.wait_ge(block_used, used(e, "down", c - 2))
                                act.copy(t_high[:, s, 0:n], turn_p[:, s, 0:n]).then_inc(t_high_done, 1)

                expert(0, first=True)
                with act.Fori(1, EXPERTS) as e:
                    expert(e)
                take_result(EXPERTS - 1)

            @block.vector
            def _(dve):
                dve.sem_inc(hidden_done, 2)
                dve.sem_inc(t_low_done, 2)
                dve.sem_inc(low_done, 2 * FF_RING)
                dve.sem_inc(x_low_done, 1)

                def take_result(e):
                    dve.wait_ge(block_used, used(e, "down", FF_N - 1))
                    dve.wait_ge(result_free, e + 1)
                    dve.tensor_scalar(result[:, 512:D], down_p[:CAP, 512:D], slot_gate[:, bass.ds(e, 1)], None,
                                      ALU.mult).then_inc(result_out, 1)

                def expert(e, first=False):
                    for q in range(FF_NB):
                        for h in range(2):
                            dve.wait_ge(high_done, (e * FF_NB + q) * 2 + h + 1)
                            dve.tensor_tensor(half_of(low, q, h), half_of(raw, q, h),
                                              half_of(high, q, h).bitcast(F32), ALU.subtract).then_inc(low_done, 1)
                        if q == 0:
                            dve.wait_ge(x_high_done, e + 1)
                            dve.tensor_tensor(x_low[:, :, :], x_raw[:, :, :], x_high[:, :, :].bitcast(F32),
                                              ALU.subtract).then_inc(x_low_done, 1)
                        if q == FF_RING - 1 and not first:
                            take_result(e - 1)
                        for step, c in follow_ups(q):
                            s, width = c % 2, FF_CHUNKS[c][1]
                            if step == "hidden":
                                dve.wait_ge(block_used, used(e, "up", c))
                                dve.wait_ge(silu_done, e * FF_N + c + 1)
                                dve.wait_ge(turn_done, e * FF_N + c + 1)
                                dve.tensor_tensor(hidden[:, s, 0:width], silu[:, s, 0:width], up_p[:CAP, s, 0:width],
                                                  ALU.mult).then_inc(hidden_done, 1)
                            else:
                                n = width // P * CAP
                                dve.wait_ge(t_high_done, e * FF_N + c + 1)
                                dve.tensor_tensor(t_low[:, s, 0:n], turn_p[:, s, 0:n],
                                                  t_high[:, s, 0:n].bitcast(F32), ALU.subtract
                                                  ).then_inc(t_low_done, 1)

                expert(0, first=True)
                with dve.Fori(1, EXPERTS) as e:
                    expert(e)
                take_result(EXPERTS - 1)


SLOT_TILES = [(t, min(P, SLOTS - t * P)) for t in range((SLOTS + P - 1) // P)]


def combine(nc, io, h, idx_dram, y_dram):
    n_s = len(SLOT_TILES)
    with Stage(nc, "comb") as st:
        y = st.sb("y", [P, n_s, D])
        high = st.sb("high", [P, n_s, D], F32R)
        low = st.sb("low", [P, n_s, D], F32R)
        scatter = st.sb("scatter", [P, n_s, SEQ], F32R)
        ids = st.sb("ids", [P, SEQ])
        slot_tok = st.sb("slot_tok", [P, n_s])
        out = st.ps("out", [P, 2, D])
        ids_in = st.sem("ids_in")
        y_in = [st.sem(f"y_in{t}") for t in range(n_s)]
        high_done, low_done, scatter_done, sum_done, added = (
            st.sem(s) for s in ("high_done", "low_done", "scatter_done", "sum_done", "added"))
        slot_rows = idx_dram.rearrange("e c -> (e c)").unsqueeze(1)
        y_rows = y_dram.rearrange("e c d -> (e c) d")
        with nc.Block() as block:

            @block.sync
            def _(sp):
                sp.dma_start(ids[:, :], io["c_ids"].partition_broadcast(P)).then_inc(ids_in, 16)
                for t, rows in SLOT_TILES:
                    sp.dma_start(slot_tok[:rows, t:t + 1], slot_rows[t * P:t * P + rows, :]).then_inc(ids_in, 16)
                for t, rows in SLOT_TILES:
                    sp.dma_start(y[:rows, t, :], y_rows[t * P:t * P + rows, :]).then_inc(y_in[t], 16)

            @block.scalar
            def _(act):
                for t, rows in SLOT_TILES:
                    act.wait_ge(y_in[t], 16)
                    act.copy(high[:rows, t, :], y[:rows, t, :]).then_inc(high_done, 1)

            @block.vector
            def _(dve):
                dve.wait_ge(ids_in, 16 * (1 + n_s))
                for t, rows in SLOT_TILES:
                    dve.tensor_scalar(scatter[:rows, t, :], ids[:rows, :], slot_tok[:rows, t:t + 1], None,
                                      ALU.is_equal).then_inc(scatter_done, 1)
                    dve.wait_ge(high_done, t + 1)
                    dve.tensor_tensor(low[:rows, t, :], y[:rows, t, :], high[:rows, t, :].bitcast(F32),
                                      ALU.subtract).then_inc(low_done, 1)
                for i in range(NT):
                    dve.wait_ge(sum_done, i + 1)
                    dve.tensor_tensor(h[:, i, :], h[:, i, :], out[:, i % 2, :], ALU.add).then_inc(added, 1)

            @block.tensor
            def _(pe):
                pe.wait_ge(high_done, n_s)
                pe.wait_ge(low_done, n_s)
                pe.wait_ge(scatter_done, n_s)
                for i in range(NT):
                    if i >= 2:
                        pe.wait_ge(added, i - 1)
                    for half in range(2):
                        cols = slice(half * 512, (half + 1) * 512)
                        for t, rows in SLOT_TILES:
                            for part in (high, low):
                                last = pe.matmul(out[:, i % 2, cols], scatter[:rows, t, i * P:(i + 1) * P],
                                                 part[:rows, t, cols], start=(t == 0 and part is high),
                                                 stop=(t == n_s - 1 and part is low))
                    last.then_inc(sum_done, 1)


def first_block(nc, io, h, ident, dbg=None):
    w_in = io["w_in"][0].rearrange("(k p) c -> p k c", p=P)
    w_out = io["w_out"][0].rearrange("(k p) c -> p k c", p=P)
    max_dram = nc.dram_tensor("scratch_max", [HEADS, 2, TOK], F32).ap()
    idx_dram = nc.dram_tensor("scratch_idx", [EXPERTS, CAP], F32).ap()
    xs_dram = nc.dram_tensor("scratch_xs", [P, SLOTS * KD], F32).ap()
    y_dram = nc.dram_tensor("scratch_y", [EXPERTS, CAP, D], F32).ap()

    with Stage(nc, "b1") as st:
        cols = st.sb("cols", [P, COLS_1_N])
        load(nc, "load1", [(cols[:, :], io["p_cols_1"]), (ident[:, :], io["c_ident"]),
                           (h[:, 0:NT, :], io["x"][0].rearrange("(i p) d -> p i d", p=P)),
                           (h[0:META, NT, :], io["meta_tokens"])])

        def gain(name):
            a, n = COLS_1[name]
            return cols[:, a:a + n]

        with Stage(nc, "mix") as mx:
            y = mx.sb("y", [P, NT + 1, D])
            with Stage(nc, "mixin") as s1:
                uT = split_of(s1, "uT", [P, KD, TOK], side="right")
                normalise(nc, "norm1", h, ALL_TILES, gain("mix_g"), ident, uT)

                def chunks(index, jobs_of):
                    return [(w_in[:, :, index * 512 + n * 256:index * 512 + (n + 1) * 256], uT, jobs_of(n))
                            for n in range(2)]

                def channel_jobs(dst, base, pad=0):
                    return lambda n: [Job("channel", c * P, P, (lambda nc, ps, t=base + 2 * n + c, eng=eng: (
                        nc.scalar.copy if eng == "act" else nc.vector.tensor_copy)(
                            halves(dst[:, t, pad:pad + TOK]), ps)), eng, parts=2, tokens=TOK)
                        for c, eng in enumerate(("act", "dve"))]

                def copied(dst):
                    return lambda n: token_jobs(ALL_TILES, 256, lambda nc, i, r, ps: nc.vector.tensor_copy(
                        dst[:r, i, n * 256:(n + 1) * 256], ps), "dve")

                def activated(dst, function):
                    return lambda n: token_jobs(ALL_TILES, 256, lambda nc, i, r, ps: nc.scalar.activation(
                        dst[:r, i, n * 256:(n + 1) * 256], ps, function))

                with Stage(nc, "retbuf") as s2:
                    rqk = s2.sb("rqk", [P, 2 * HEADS, TOK])
                    rv = s2.sb("rv", [P, NT + 1, MIX])
                    rg = s2.sb("rg", [P, NT + 1, MIX])
                    project(nc, "proj_ret", chunks(0, channel_jobs(rqk, 0)) + chunks(1, channel_jobs(rqk, HEADS)) +
                            chunks(2, copied(rv)) + chunks(3, activated(rg, ACT.Silu)))
                    retention(nc, io, rqk, rv, rg, y)
                    if dbg: dbg("yret", y[:, :, 0:MIX])

                qk = mx.sb("qk", [P, 2 * HEADS, TOK])
                v1 = mx.sb("v1", [P, NT + 1, HEADS, P + 1])
                mo = mx.sb("mo", [P, NT + 1, MIX])
                gates = mx.sb("gates", [HEADS, 4, TOK])
                with Stage(nc, "convbuf") as s2:
                    padded = s2.sb("padded", [P, KD, TOK + CONV_K - 1])
                    gate_jobs = [Job("channel", g * HEADS, HEADS,
                                     (lambda nc, ps, g=g: nc.vector.tensor_copy(halves(gates[:, g, :]), ps)),
                                     "dve", parts=2, tokens=TOK) for g in range(4)]
                    def values(n):
                        return token_jobs(ALL_TILES, 256, lambda nc, i, r, ps: nc.vector.tensor_copy(
                            v1[:r, i, 2 * n:2 * n + 2, 0:P], ps.rearrange("p (h e) -> p h e", h=2)), "dve")

                    project(nc, "proj_ml", chunks(4, channel_jobs(padded, 0, 2)) +
                            chunks(5, channel_jobs(padded, HEADS, 2)) + chunks(6, values) +
                            chunks(7, activated(mo, ACT.Sigmoid)) +
                            [(w_in[:, :, 8 * 512:8 * 512 + N_GATES], uT, gate_jobs)])
                    clear(nc, "clear_ml", [padded[:, :, 0:2], padded[:, :, TOK + 2:TOK + 4]])
                    w0, b0 = COLS_1["conv_w"][0], COLS_1["conv_b"][0]
                    conv_silu(nc, "mlc", padded, KD, CONV_K, TOK,
                              lambda c, j: cols[:, w0 + c * CONV_K + j:w0 + c * CONV_K + j + 1],
                              lambda c: cols[:, b0 + c:b0 + c + 1], qk)
            with Stage(nc, "mlbuf") as s2:
                g_col = s2.sb("g_col", [P, NT + 1, 2 * HEADS])
                exp_col = s2.sb("exp_col", [P, NT + 1, 2 * HEADS])
                max_rows = s2.sb("max_rows", [P, 2 * HEADS, TOK])
                mlstm_gates(nc, io, cols, gates, ident, g_col, exp_col, max_rows, max_dram)
                clear(nc, "ones_ml", [v1[:, :, :, P:P + 1]], 1.0)
                mlstm(nc, io, qk, v1, mo, y[:, :, MIX:D], g_col, exp_col, max_rows)
            if dbg: dbg("y", y[:, :, :])
            with Stage(nc, "mixout") as s2:
                yT = split_of(s2, "yT", [P, KD, TOK])
                turn_rows(nc, "turn_y", y, ALL_TILES, ident, yT)
                project(nc, "proj_out", added_chunks(w_out, yT, h, ALL_TILES))
        if dbg: dbg("hmix", h[:, :, :])

        slot_gate = st.sb("slot_gate", [CAP, EXPERTS])
        with Stage(nc, "moe") as s1:
            with Stage(nc, "routebuf") as s2:
                xs = s2.sb("xs", [P, EXPERTS, KD, CAP])
                u = s2.sb("u", [P, NT + 1, D])
                uT = s2.sb("uT", [P, KD, TOK])
                gain_row = s2.sb("gain_row", [P, D])
                load(nc, "load_g", [(gain_row[:, :], io["ffn_g_row"].partition_broadcast(P))])
                normalise(nc, "norm2", h, ALL_TILES, None, ident, uT, gain_row=gain_row, kept=u)
                route(nc, io, u, uT, ident, xs, slot_gate, idx_dram)
                load(nc, "store_xs", [(xs_dram, xs[:, :, :, :].rearrange("p e k c -> p (e k c)"))])
            expert_ffn(nc, io, xs_dram, slot_gate, ident, y_dram)
        combine(nc, io, h, idx_dram, y_dram)


N_MEM = 256
SSD_HEADS = 16
SSD_HD = D // SSD_HEADS
SSD_GROUPS = 4
SSD_RATIO = SSD_HEADS // SSD_GROUPS
SSD_CONV = 4
XBC = D + 2 * SSD_GROUPS * P
XBC_TILES = XBC // P
DIL = ((128, 1), (512, 4), (2048, 16))
DIL_J = 4
DIL_HD = 64
DIL_HEADS = len(DIL) * DIL_J
DIL_W = DIL_HEADS * DIL_HD
MEM_HD = 192
MEM_W = HEADS * MEM_HD
ROT = DIL_HD // 4
ROT_HALF = ROT // 2
OFF_XBC = D
OFF_DT = OFF_XBC + XBC
OFF_DQ = OFF_DT + SSD_HEADS
OFF_MQ = OFF_DQ + 3 * DIL_W
OFF_GATE = OFF_MQ + MEM_W
BRANCHES = 3

PEER_HEADS = 8
PEER_KEYS = 128
PEER_TOP = 16
PEER_SLOTS = PEER_HEADS * PEER_TOP

SEQ_TILES = [(i, P, P * i) for i in range(NT)]

COLS_2 = {}
for _name, _count in (("mix_g", KD), ("mem_g", KD), ("conv_w", XBC_TILES * SSD_CONV), ("conv_b", XBC_TILES),
                      ("dt_bias", 1), ("a_log", 1)):
    COLS_2[_name] = (sum(c for _, c in COLS_2.values()), _count)
COLS_2_N = sum(c for _, c in COLS_2.values())


def rms_groups(nc, name, xs, groups, width, gain):
    n = len(xs)
    with Stage(nc, name) as st:
        squares = st.sb("squares", [P, 2, groups * width])
        ssq = st.sb("ssq", [P, n, groups])
        squared, summed, inverted, rooted, dve_order = (
            st.sem(s) for s in ("squared", "summed", "inverted", "rooted", "dve_order"))

        def grouped(ap):
            return ap.rearrange("p (g w) -> p g w", g=groups)

        with nc.Block() as block:

            @block.scalar
            def _(act):
                for i in range(n):
                    if i >= 2:
                        act.wait_ge(summed, i - 1)
                    act.activation(squares[:, i % 2, :], xs[i], ACT.Square).then_inc(squared, 1)
                act.wait_ge(inverted, 1)
                act.activation(ssq[:, :, :], ssq[:, :, :], ACT.Sqrt).then_inc(rooted, 1)

            @block.vector
            def _(dve):
                order = InOrder(dve, dve_order)
                for i in range(n):
                    dve.wait_ge(squared, i + 1)
                    dve.tensor_reduce(ssq[:, i, :], grouped(squares[:, i % 2, :]), AX_X, ALU.add
                                      ).then_inc(summed, 1)
                dve.wait_ge(summed, n)
                order(dve.tensor_scalar(ssq[:, :, :], ssq[:, :, :], 1.0 / width, EPS, ALU.mult, ALU.add))
                dve.reciprocal(ssq[:, :, :], ssq[:, :, :]).then_inc(inverted, 1)
                dve.wait_ge(rooted, 1)
                for i in range(n):
                    x = grouped(xs[i])
                    order(dve.tensor_tensor(x, x, ssq[:, i, :].unsqueeze(2).broadcast_to([P, groups, width]),
                                            ALU.mult))
                    g = (gain.unsqueeze(1).broadcast_to([P, groups, width]) if gain.shape[1] == width
                         else grouped(gain))
                    order(dve.tensor_tensor(x, x, g, ALU.mult))


def ssd_prepare(nc, io, cols, dt_raw, xbc, ident, acum_rows, acum_col, xs, x_dt, scratch):
    with Stage(nc, "ssp") as st:
        dt = st.sb("dt", [SSD_HEADS, SEQ])
        soft = st.sb("soft", [SSD_HEADS, SEQ])
        acum = st.sb("acum", [SSD_HEADS, SEQ])
        ones = st.sb("ones", [SSD_HEADS, SEQ])
        a = st.sb("a", [SSD_HEADS, 1])
        dt_col = st.sb("dt_col", [P, NT, SSD_HEADS])
        small = st.ps("small", [P, NT, 2, SSD_HEADS])
        turned = st.ps("turned", [P, 2, D])
        abs_done, soft_done, a_done, rows_done, cols_turned, x_turned, x_out, stored, landed, dve_order, act_order = (
            st.sem(s) for s in ("abs_done", "soft_done", "a_done", "rows_done", "cols_turned", "x_turned", "x_out",
                                "stored", "landed", "dve_order", "act_order"))
        bias, a_log = COLS_2["dt_bias"][0], COLS_2["a_log"][0]

        with nc.Block() as block:

            @block.vector
            def _(dve):
                order = InOrder(dve, dve_order)
                order(dve.memset(ones[:, :], 1.0))
                order(dve.tensor_scalar(dt_raw[:, :], dt_raw[:, :], cols[:SSD_HEADS, bias:bias + 1], None, ALU.add))
                dve.scalar_tensor_tensor(soft[:, :], dt_raw[:, :], -1.0, dt_raw[:, :], ALU.mult,
                                         ALU.max).then_inc(abs_done, 1)
                dve.wait_ge(soft_done, 1)
                order(dve.scalar_tensor_tensor(dt[:, :], dt_raw[:, :], 0.0, soft[:, :], ALU.max, ALU.add))
                dve.wait_ge(a_done, 1)
                order(dve.tensor_scalar(soft[:, :], dt[:, :], a[:, :], -1.0, ALU.mult, ALU.mult))
                dve.tensor_tensor_scan(acum[:, :], ones[:, :], soft[:, :], 0.0, ALU.mult, ALU.add
                                       ).then_inc(rows_done, 1)
                dve.wait_ge(cols_turned, 1)
                order(dve.tensor_copy(acum_col[:, :, :], small[:, :, 0, :]))
                order(dve.tensor_copy(dt_col[:, :, :], small[:, :, 1, :]))
                for i in range(NT):
                    dve.wait_ge(x_turned, i + 1)
                    order(dve.tensor_copy(xs[:, i, :], turned[:, i % 2, :]))
                    dve.sem_inc(x_out, 1)
                    order(dve.tensor_tensor(
                        x_dt[:, i, :].rearrange("p (h e) -> p h e", h=SSD_HEADS),
                        xs[:, i, :].rearrange("p (h e) -> p h e", h=SSD_HEADS),
                        dt_col[:, i, :].unsqueeze(2).broadcast_to([P, SSD_HEADS, SSD_HD]), ALU.mult))

            @block.scalar
            def _(act):
                order = InOrder(act, act_order)
                act.activation(a[:, :], cols[:SSD_HEADS, a_log:a_log + 1], ACT.Exp).then_inc(a_done, 1)
                act.wait_ge(abs_done, 1)
                order(act.activation(soft[:, :], soft[:, :], ACT.Exp, scale=-1.0))
                act.activation(soft[:, :], soft[:, :], ACT.Ln, bias=1.0).then_inc(soft_done, 1)

            @block.tensor
            def _(pe):
                def turn_x(i):
                    if i >= 2:
                        pe.wait_ge(x_out, i - 1)
                    for k in range(KD):
                        last = pe.transpose(turned[:, i % 2, k * P:(k + 1) * P], xbc[:, k, i * P:(i + 1) * P],
                                            ident[:, :])
                    last.then_inc(x_turned, 1)

                turn_x(0)
                turn_x(1)
                pe.wait_ge(rows_done, 1)
                for i in range(NT):
                    pe.transpose(small[:, i, 0, :], acum[:, i * P:(i + 1) * P], ident[:SSD_HEADS, :SSD_HEADS])
                    last = pe.transpose(small[:, i, 1, :], dt[:, i * P:(i + 1) * P], ident[:SSD_HEADS, :SSD_HEADS])
                last.then_inc(cols_turned, 1)
                turn_x(2)
                turn_x(3)

            @block.sync
            def _(sp):
                sp.wait_ge(rows_done, 1)
                sp.dma_start(scratch, acum[:, :]).then_inc(stored, 16)
                sp.wait_ge(stored, 16)
                for hd in range(SSD_HEADS):
                    sp.dma_start(acum_rows[:, hd, :], scratch[hd:hd + 1, :].partition_broadcast(P)
                                 ).then_inc(landed, 16)
                sp.wait_ge(landed, 16 * SSD_HEADS)


def ssd(nc, io, xbc, acum_rows, acum_col, x_dt, z, y):
    with Stage(nc, "ssd") as st:
        raw = st.sb("raw", [P, NT, SEQ])
        arg = st.sb("arg", [P, 3, SEQ])
        weight = st.sb("weight", [P, 2, NT, SEQ])
        keep = st.sb("keep", [P, 2, P])
        skip = st.sb("skip", [P, SSD_HEADS])
        scores = st.ps("scores", [P, 2, 512])
        mixed = st.ps("mixed", [P, 4, 512])
        landed, scored, raw_ready, arg_ready, exp_ready, weight_ready, mix_done, mix_out, dve_order = (
            st.sem(s) for s in ("landed", "scored", "raw_ready", "arg_ready", "exp_ready", "weight_ready",
                                "mix_done", "mix_out", "dve_order"))

        with nc.Block() as block:

            @block.sync
            def _(sp):
                sp.dma_start(keep[:, :, :], io["c_keep"]).then_inc(landed, 16)
                sp.dma_start(skip[:, :], io["ssd_d_row"].partition_broadcast(P)).then_inc(landed, 16)
                sp.wait_ge(landed, 32)

            @block.scalar
            def _(act):
                for p in range(SSD_HEADS):
                    g = p // SSD_RATIO
                    if p % SSD_RATIO == 0:
                        if p:
                            act.wait_ge(weight_ready, NT * p)
                        for n in range(NT):
                            act.wait_ge(scored, g * NT + n + 1)
                            act.copy(raw[:, n, n * P:], scores[:, (g * NT + n) % 2, n * P:]).then_inc(raw_ready, 1)
                    for n in range(NT):
                        m = p * NT + n
                        act.wait_ge(arg_ready, m + 1)
                        act.activation(arg[:, m % 3, n * P:], arg[:, m % 3, n * P:], ACT.Exp
                                       ).then_inc(exp_ready, 1)

            @block.vector
            def _(dve):
                order = InOrder(dve, dve_order)
                dve.wait_ge(landed, 32)

                def exponents(p, n):
                    m = p * NT + n
                    if m >= 3:
                        dve.wait_ge(weight_ready, m - 2)
                    dve.tensor_scalar(arg[:, m % 3, n * P:], acum_rows[:, p, n * P:], acum_col[:, n, p:p + 1], 0.0,
                                      ALU.subtract, ALU.min).then_inc(arg_ready, 1)

                def weigh(p, n):
                    m = p * NT + n
                    dve.wait_ge(exp_ready, m + 1)
                    if p >= 2:
                        dve.wait_ge(mix_done, NT * (p - 1))
                    dve.tensor_tensor(weight[:, p % 2, n, n * P:], arg[:, m % 3, n * P:], raw[:, n, n * P:],
                                      ALU.mult).then_inc(weight_ready, 1)

                def take_out(p):
                    part = slice(p * SSD_HD, (p + 1) * SSD_HD)
                    for i in range(NT):
                        m = p * NT + i
                        dve.wait_ge(mix_done, m + 1)
                        dve.scalar_tensor_tensor(y[:, i, part], y[:, i, part], skip[:, p:p + 1],
                                                 mixed[:, m % 4, 0:SSD_HD], ALU.mult, ALU.add).then_inc(mix_out, 1)

                for p in range(SSD_HEADS):
                    exponents(p, 0)
                    exponents(p, 1)
                    if p % SSD_RATIO == 0:
                        dve.wait_ge(raw_ready, NT * (p // SSD_RATIO + 1))
                        for n in range(NT):
                            order(dve.tensor_tensor(raw[:, n, n * P:(n + 1) * P], raw[:, n, n * P:(n + 1) * P],
                                                    keep[:, 0, :], ALU.mult))
                    for n in range(NT):
                        if n + 2 < NT:
                            exponents(p, n + 2)
                        weigh(p, n)
                    if p:
                        take_out(p - 1)
                take_out(SSD_HEADS - 1)
                dve.wait_ge(mix_out, NT * SSD_HEADS)
                for i in range(NT):
                    order(dve.tensor_tensor(y[:, i, :], y[:, i, :], z[:, i, :], ALU.mult))

            @block.tensor
            def _(pe):
                def score(g):
                    for n in range(NT):
                        m = g * NT + n
                        if m >= 2:
                            pe.wait_ge(raw_ready, m - 1)
                        pe.matmul(scores[:, m % 2, n * P:], xbc[:, KD + g, n * P:(n + 1) * P],
                                  xbc[:, KD + SSD_GROUPS + g, n * P:SEQ], start=True, stop=True
                                  ).then_inc(scored, 1)

                def mix(p):
                    pe.wait_ge(weight_ready, NT * (p + 1))
                    for i in range(NT):
                        m = p * NT + i
                        if m >= 4:
                            pe.wait_ge(mix_out, m - 3)
                        for n in range(i + 1):
                            last = pe.matmul(mixed[:, m % 4, 0:SSD_HD], weight[:, p % 2, n, i * P:(i + 1) * P],
                                             x_dt[:, n, p * SSD_HD:(p + 1) * SSD_HD], start=(n == 0), stop=(n == i))
                        last.then_inc(mix_done, 1)

                score(0)
                for p in range(SSD_HEADS):
                    if p % SSD_RATIO == SSD_RATIO - 1 and p + 1 < SSD_HEADS:
                        score(p // SSD_RATIO + 1)
                    mix(p)


def rope(nc, io, qk):
    heads = 2 * DIL_HEADS
    two_pi = (6.28125, 0.00193500518798828125, 3.0199159819567e-07)
    magic = 1.5 * 2.0 ** 23
    pi = 3.1415925
    with Stage(nc, "rope") as st:
        pos_i = st.sb("pos_i", [P, NT], I32)
        pos = st.sb("pos", [P, NT])
        inv = st.sb("inv", [P, ROT_HALF])
        ang = st.sb("ang", [P, NT, ROT_HALF])
        turns = st.sb("turns", [P, 2, NT, ROT_HALF])
        rest = st.sb("rest", [P, 2, NT, ROT_HALF])
        a, b, c, d = (st.sb(s, [P, heads, ROT_HALF]) for s in "abcd")
        landed, reduced, sines, dve_order = (st.sem(s) for s in ("landed", "reduced", "sines", "dve_order"))
        with nc.Block() as block:

            @block.sync
            def _(sp):
                sp.dma_start(pos_i[:, :], io["positions"]).then_inc(landed, 16)
                sp.dma_start(inv[:, :], io["c_inv"].partition_broadcast(P)).then_inc(landed, 16)
                sp.wait_ge(landed, 32)

            @block.vector
            def _(dve):
                order = InOrder(dve, dve_order)
                dve.wait_ge(landed, 32)
                order(dve.tensor_copy(pos[:, :], pos_i[:, :]))
                order(dve.tensor_tensor(ang[:, :, :], pos[:, :].unsqueeze(2).broadcast_to([P, NT, ROT_HALF]),
                                        inv[:, :].unsqueeze(1).broadcast_to([P, NT, ROT_HALF]), ALU.mult))
                for w in range(2):
                    t, r = turns[:, w, :, :], rest[:, w, :, :]
                    order(dve.tensor_scalar(t, ang[:, :, :], 0.15915494309189535, 0.25 * w, ALU.mult, ALU.add))
                    order(dve.tensor_scalar(t, t, magic, None, ALU.add))
                    order(dve.tensor_scalar(t, t, magic, None, ALU.subtract))
                    order(dve.scalar_tensor_tensor(r, t, -two_pi[0], ang[:, :, :], ALU.mult, ALU.add))
                    order(dve.scalar_tensor_tensor(r, t, -two_pi[1], r, ALU.mult, ALU.add))
                    order(dve.scalar_tensor_tensor(r, t, -two_pi[2], r, ALU.mult, ALU.add))
                    if w:
                        order(dve.tensor_scalar(r, r, 1.5707963267948966, None, ALU.add))
                    order(dve.tensor_scalar(r, r, pi, -pi, ALU.min, ALU.max))
                dve.sem_inc(reduced, 1)
                dve.wait_ge(sines, 1)
                for i in range(NT):
                    x1, x2 = qk[:, i, :, 0:ROT_HALF], qk[:, i, :, ROT_HALF:ROT]
                    sin = rest[:, 0, i, :].unsqueeze(1).broadcast_to([P, heads, ROT_HALF])
                    cos = rest[:, 1, i, :].unsqueeze(1).broadcast_to([P, heads, ROT_HALF])
                    order(dve.tensor_tensor(a[:, :, :], x1, cos, ALU.mult))
                    order(dve.tensor_tensor(b[:, :, :], x2, sin, ALU.mult))
                    order(dve.tensor_tensor(c[:, :, :], x2, cos, ALU.mult))
                    order(dve.tensor_tensor(d[:, :, :], x1, sin, ALU.mult))
                    order(dve.tensor_tensor(x1, a[:, :, :], b[:, :, :], ALU.subtract))
                    order(dve.tensor_tensor(x2, c[:, :, :], d[:, :, :], ALU.add))

            @block.scalar
            def _(act):
                act.wait_ge(reduced, 1)
                act.activation(rest[:, :, :, :], rest[:, :, :, :], ACT.Sin).then_inc(sines, 1)


def attend(nc, name, units, ident, groups, wide, scale):
    n_u = len(units)
    with Stage(nc, name) as st:
        s = st.sb("s", [P, 2, groups, wide])
        pT = st.sb("pT", [P, 2, groups, wide])
        peak = st.sb("peak", [P, 2])
        total = st.sb("total", [P, 2])
        scores = st.ps("scores", [P, groups, 512])
        turned = st.ps("turned", [P, groups, 512])
        mixed = st.ps("mixed", [P, 2, 512])
        scored, masked, peaked, exped, turn_done, turn_out, mix_done, mix_out, dve_order = (
            st.sem(x) for x in ("scored", "masked", "peaked", "exped", "turn_done", "turn_out", "mix_done",
                                "mix_out", "dve_order"))
        with nc.Block() as block:

            @block.tensor
            def _(pe):
                def score(u):
                    pieces, w, _, _, _ = units[u]
                    if u:
                        pe.wait_ge(masked, u)
                    for g in range(groups):
                        for n, (q, k) in enumerate(pieces[g]):
                            last = pe.matmul(scores[:, g, 0:w], q, k, start=(n == 0), stop=(n == len(pieces[g]) - 1))
                    last.then_inc(scored, 1)

                def turn(u):
                    _, w, _, _, _ = units[u]
                    pe.wait_ge(exped, u + 1)
                    if u:
                        pe.wait_ge(turn_out, u)
                    for g in range(groups):
                        for n in range(w // P):
                            last = pe.transpose(turned[:, g, n * P:(n + 1) * P], s[:, u % 2, g, n * P:(n + 1) * P],
                                                ident[:, :])
                    last.then_inc(turn_done, 1)

                def mix(u):
                    _, w, _, values, out = units[u]
                    pe.wait_ge(turn_out, u + 1)
                    if u >= 2:
                        pe.wait_ge(mix_out, u - 1)
                    blocks = [(g, n) for g in range(groups) for n in range(w // P)]
                    for g, n in blocks:
                        last = pe.matmul(mixed[:, u % 2, 0:out.shape[1]], pT[:, u % 2, g, n * P:(n + 1) * P],
                                         values(g, n), start=((g, n) == blocks[0]), stop=((g, n) == blocks[-1]))
                    last.then_inc(mix_done, 1)

                for u in range(n_u + 2):
                    if u < n_u:
                        score(u)
                    if u >= 2:
                        mix(u - 2)
                    if 1 <= u <= n_u:
                        turn(u - 1)

            @block.vector
            def _(dve):
                order = InOrder(dve, dve_order)
                for u in range(n_u + 2):
                    if u < n_u:
                        _, w, mask, _, _ = units[u]
                        dve.wait_ge(scored, u + 1)
                        if u >= 2:
                            dve.wait_ge(turn_done, u - 1)
                        now = s[:, u % 2, :, 0:w]
                        if mask is None:
                            order(dve.tensor_scalar(now, scores[:, :, 0:w], scale, None, ALU.mult))
                        else:
                            order(dve.scalar_tensor_tensor(now, scores[:, :, 0:w], scale, mask, ALU.mult, ALU.add))
                        dve.sem_inc(masked, 1)
                        order(dve.tensor_reduce(peak[:, u % 2:u % 2 + 1], now, mybir.AxisListType.XY, ALU.max))
                        dve.tensor_scalar(peak[:, u % 2:u % 2 + 1], peak[:, u % 2:u % 2 + 1], -1.0, None,
                                          ALU.mult).then_inc(peaked, 1)
                    if u >= 2:
                        v, out = u - 2, units[u - 2][4]
                        dve.wait_ge(mix_done, v + 1)
                        order(dve.reciprocal(total[:, v % 2:v % 2 + 1], total[:, v % 2:v % 2 + 1]))
                        order(dve.tensor_scalar(out, mixed[:, v % 2, 0:out.shape[1]], total[:, v % 2:v % 2 + 1],
                                                None, ALU.mult))
                        dve.sem_inc(mix_out, 1)

            @block.scalar
            def _(act):
                for u in range(n_u + 1):
                    if u < n_u:
                        w = units[u][1]
                        act.wait_ge(peaked, u + 1)
                        if u >= 2:
                            act.wait_ge(mix_out, u - 1)
                        now = s[:, u % 2, :, 0:w]
                        act.activation(now, now, ACT.Exp, bias=peak[:, u % 2:u % 2 + 1],
                                       accum_out=total[:, u % 2:u % 2 + 1]).then_inc(exped, 1)
                    if u >= 1:
                        v, w = u - 1, units[u - 1][1]
                        act.wait_ge(turn_done, v + 1)
                        if v >= 2:
                            act.wait_ge(mix_done, v - 1)
                        act.copy(pT[:, v % 2, :, 0:w], turned[:, :, 0:w]).then_inc(turn_out, 1)


def peer_scores(nc, io, qT, score_dram):
    hc = 2 * PEER_HEADS
    with Stage(nc, "score") as st:
        keys = st.sb("keys", [P, hc, PEER_KEYS])
        sc = st.sb("sc", [P, 2, hc, PEER_KEYS])
        scores = st.ps("scores", [P, 2, hc, PEER_KEYS])
        landed, scored, sc_ready = (st.sem(x) for x in ("landed", "scored", "sc_ready"))
        stored = [st.sem("stored0"), st.sem("stored1")]
        with nc.Block() as block:

            @block.sync
            def _(sp):
                sp.dma_start(keys[:, :, :], io["sub_keys"]).then_inc(landed, 16)
                for i in range(NT):
                    sp.wait_ge(sc_ready, i + 1)
                    sp.dma_start(score_dram[i], sc[:, i % 2, :, :].rearrange("p c k -> p (c k)")
                                 ).then_inc(stored[i % 2], 16)
                for half in range(2):
                    sp.wait_ge(stored[half], 16 * (NT // 2))

            @block.tensor
            def _(pe):
                pe.wait_ge(landed, 16)
                for i in range(NT):
                    if i >= 2:
                        pe.wait_ge(sc_ready, i - 1)
                    for c in range(hc):
                        last = pe.matmul(scores[:, i % 2, c, :], qT[:, c, i * P:(i + 1) * P], keys[:, c, :],
                                         start=True, stop=True)
                    last.then_inc(scored, 1)

            @block.scalar
            def _(act):
                for i in range(NT):
                    act.wait_ge(scored, i + 1)
                    if i >= 2:
                        act.wait_ge(stored[i % 2], 16 * (i // 2))
                    act.copy(sc[:, i % 2, :, :], scores[:, i % 2, :, :]).then_inc(sc_ready, 1)


class Selection:

    def __init__(self, nc, io, st, chosen, gates):
        self.dve, self.chosen, self.gates = nc.vector, chosen, gates
        hc, H, T = 2 * PEER_HEADS, PEER_HEADS, PEER_TOP
        self.sc = st.sb("sc", [P, hc * PEER_KEYS])
        self.v = st.sb("v", [P, hc, T])
        self.ix = st.sb("ix", [P, hc, T], U32)
        self.ixf = st.sb("ixf", [P, hc, T])
        self.cand = st.sb("cand", [P, H, T, T])
        self.top = st.sb("top", [P, 2, H, T])
        self.pos = st.sb("pos", [P, H, T], U32)
        self.part = st.sb("part", [P, 2, H, T], U32)
        self.partf = st.sb("partf", [P, 2, H, T])
        self.picked = st.sb("picked", [P, 2, H, T])
        self.iota = st.sb("iota", [P, T])
        self.total = st.sb("total", [P, H])
        self.sc_in, self.iota_in = st.sem("sc_in"), st.sem("iota_in")
        self.selected, self.top_ready, self.exp_ready = (st.sem(x) for x in ("selected", "top_ready", "exp_ready"))
        self.order = InOrder(self.dve, st.sem("sel_order"))

    def best16(self, rows):
        dve, order = self.dve, self.order
        steps = (lambda vals, where, x: dve.max(vals[:, 0:8], x),
                 lambda vals, where, x: dve.max_index(where[:, 0:8], vals[:, 0:8], x),
                 lambda vals, where, x: dve.match_replace(x, vals[:, 0:8], x, -3.0e38),
                 lambda vals, where, x: dve.max(vals[:, 8:16], x),
                 lambda vals, where, x: dve.max_index(where[:, 8:16], vals[:, 8:16], x))
        for n, step in enumerate(steps):
            for row in rows:
                if n:
                    dve.wait_ge(order.sem, order.n - len(rows) + 1)
                order.issue(step(*row))
        order.settle()

    def keys(self, i, half):
        if half == 0:
            self.dve.wait_ge(self.sc_in, 16 * (i + 1))
        sc = self.sc[:, :].rearrange("p (c k) -> p c k", k=PEER_KEYS)
        self.best16([(self.v[:, c, :], self.ix[:, c, :], sc[:, c, :])
                     for c in range(half * PEER_HEADS, (half + 1) * PEER_HEADS)])

    def sums(self, i):
        H, T, order, dve = PEER_HEADS, PEER_TOP, self.order, self.dve
        cand = self.cand
        order(dve.tensor_copy(self.ixf[:, :, :], self.ix[:, :, :]))
        v4 = self.v[:, :, :].rearrange("p (h c) t -> p h c t", c=2)
        order(dve.tensor_tensor(cand[:, :, :, :], v4[:, :, 0, :].unsqueeze(3).broadcast_to([P, H, T, T]),
                                v4[:, :, 1, :].unsqueeze(2).broadcast_to([P, H, T, T]), ALU.add))
        self.best16([(self.top[:, i % 2, h, :], self.pos[:, h, :], cand[:, h, :, :].rearrange("p a b -> p (a b)"))
                     for h in range(H)])

    def numbers(self, i):
        H, T, order, dve = PEER_HEADS, PEER_TOP, self.order, self.dve
        part, partf, picked, top = self.part, self.partf, self.picked, self.top
        i4 = self.ixf[:, :, :].rearrange("p (h c) t -> p h c t", c=2)
        flat = self.sc[:, :].rearrange("p (n a) -> p n a", a=T)
        match = self.sc[:, :].rearrange("p (h t a) -> p h t a", h=H, t=T)
        order(dve.tensor_scalar(part[:, 0, :, :], self.pos[:, :, :], 4, None, ALU.logical_shift_right))
        order(dve.tensor_scalar(part[:, 1, :, :], self.pos[:, :, :], T - 1, None, ALU.bitwise_and))
        order(dve.tensor_copy(partf[:, :, :, :], part[:, :, :, :]))
        if i == 0:
            dve.wait_ge(self.iota_in, 16)
        for c in range(2):
            order(dve.tensor_tensor(
                flat, partf[:, c, :, :].rearrange("p h t -> p (h t)").unsqueeze(2).broadcast_to([P, H * T, T]),
                self.iota[:, :].unsqueeze(1).broadcast_to([P, H * T, T]), ALU.is_equal))
            order(dve.tensor_tensor(match, match, i4[:, :, c, :].unsqueeze(2).broadcast_to([P, H, T, T]), ALU.mult))
            order(dve.tensor_reduce(picked[:, c, :, :], match, AX_X, ALU.add))
        order(dve.scalar_tensor_tensor(
            self.chosen[:, i, :].rearrange("p (h t) -> p h t", h=H), picked[:, 0, :, :], float(PEER_KEYS),
            picked[:, 1, :, :], ALU.mult, ALU.add))
        dve.sem_inc(self.selected, 1)
        order(dve.tensor_tensor(picked[:, 0, :, :], top[:, i % 2, :, :],
                                top[:, i % 2, :, 0:1].broadcast_to([P, H, T]), ALU.subtract))
        order(dve.tensor_copy(top[:, i % 2, :, :], picked[:, 0, :, :]))
        dve.sem_inc(self.top_ready, 1)

    def parts(self, i):
        return [lambda: self.keys(i, 0), lambda: self.keys(i, 1), lambda: self.sums(i), lambda: self.numbers(i)]

    def finish(self, i):
        H, T, order, dve = PEER_HEADS, PEER_TOP, self.order, self.dve
        dve.wait_ge(self.exp_ready, i + 1)
        t = self.top[:, i % 2, :, :]
        order(dve.tensor_reduce(self.total[:, :], t, AX_X, ALU.add))
        order(dve.reciprocal(self.total[:, :], self.total[:, :]))
        order(dve.tensor_tensor(self.gates[:, i, :].rearrange("p (h t) -> p h t", h=H), t,
                                self.total[:, :].unsqueeze(2).broadcast_to([P, H, T]), ALU.mult))


GROUP = 8
RING = 2 * GROUP
ROUNDS = PEER_SLOTS // RING


def peer_experts(nc, io, hn, h, score_dram, out):
    down = io["peer_down_2"][0]
    up = io["peer_up_2"][0]
    with Stage(nc, "peer") as st:
        down_rows = [st.sb(f"down{u}", [P, D]) for u in range(RING)]
        up_rows = [st.sb(f"up{u}", [P, D]) for u in range(RING)]
        chosen = st.sb("chosen", [P, NT, PEER_SLOTS])
        gates = st.sb("gates", [P, NT, PEER_SLOTS])
        select = Selection(nc, io, st, chosen, gates)
        junk = st.ps("junk", [P, 2, D])
        idx_d = st.sb("idx_d", [P, 2, GROUP], U32)
        idx_u = st.sb("idx_u", [P, 2, GROUP], U32)
        dots = st.sb("dots", [P, NT, PEER_SLOTS])
        coef = st.sb("coef", [P, NT, PEER_SLOTS])
        diag = st.sb("diag", [P, 4, P])
        ident = st.sb("ident", [P, P])
        zeros = st.sb("zeros", [P, 512])
        acc = st.ps("acc", [P, 2, D])
        down_in = [st.sem(f"down_in{u}") for u in range(RING)]
        up_in = [st.sem(f"up_in{u}") for u in range(RING)]
        landed, down_used, up_used, gelu_done, coef_done, diag_done, diag_used, sum_done, added, stored = (
            st.sem(x) for x in ("landed", "down_used", "up_used", "gelu_done", "coef_done", "diag_done",
                                "diag_used", "sum_done", "added", "stored"))
        dve_order, ready, idx_ready, idx_seen = (st.sem(x) for x in ("dve_order", "ready", "idx_ready", "idx_seen"))

        steps = [(j < NT, j >= 1) for j in range(NT + 1)]

        with nc.Block() as block:

            @block.sync
            def _(sp):
                sp.dma_start(ident[:, :], io["c_ident"]).then_inc(landed, 16)
                sp.dma_start(select.iota[:, :], io["c_iota16"].partition_broadcast(P)).then_inc(select.iota_in, 16)
                for i in range(NT):
                    if i:
                        sp.wait_ge(select.selected, i)
                    sp.dma_start(select.sc[:, :], score_dram[i]).then_inc(select.sc_in, 16)
                for i in range(NT):
                    sp.wait_ge(added, i + 1)
                    sp.dma_start(out[i * P:(i + 1) * P, :], h[:, i, :]).then_inc(stored, 16)
                sp.wait_ge(stored, 16 * NT)

            @block.gpsimd
            def _(pool):
                pool.sem_inc(down_used, RING)
                pool.sem_inc(up_used, RING)
                copies = 0
                for j, (has_down, has_up) in enumerate(steps):
                    if has_down:
                        pool.wait_ge(select.selected, j + 1)
                    kinds = ([("down", j)] if has_down else []) + ([("up", j - 1)] if has_up else [])
                    with pool.Fori(0, ROUNDS) as r:
                        for b in range(2):
                            for n, (kind, i) in enumerate(kinds):
                                used = down_used if kind == "down" else up_used
                                idx = idx_d if kind == "down" else idx_u
                                first = r * RING + b * GROUP
                                pool.wait_ge(used, first + (i * PEER_SLOTS + GROUP))
                                pool.tensor_copy(idx[:, b, :], chosen[:, i, bass.ds(first, GROUP)]
                                                 ).then_inc(idx_ready, 1)
                                pool.wait_ge(idx_ready, r * (2 * len(kinds)) + (copies + b * len(kinds) + n + 1))
                                pool.sem_inc(idx_seen, 1)
                            for u in range(GROUP):
                                for kind, i in kinds:
                                    rows, table, sems, idx = ((down_rows, down, down_in, idx_d) if kind == "down"
                                                              else (up_rows, up, up_in, idx_u))
                                    pool.indirect_dma_start(
                                        rows[b * GROUP + u][:, :], None, table,
                                        bass.IndirectOffsetOnAxis(ap=idx[:, b, u:u + 1], axis=0)
                                    ).then_inc(sems[b * GROUP + u], 16)
                    copies += ROUNDS * 2 * len(kinds)

            @block.vector
            def _(dve):
                order = InOrder(dve, dve_order)
                dve.memset(zeros[:, :], 0.0).then_inc(ready, 1)
                for part in select.parts(0):
                    part()

                def dot_rounds(j, first, end):
                    with dve.Fori(first, end) as r:
                        for u in range(RING):
                            slot = r * RING + u
                            dve.wait_ge(down_in[u], (r + (j * ROUNDS + 1)) * 16)
                            dve.wait_ge(down_used, slot + (j * PEER_SLOTS + RING - 1))
                            dve.scalar_tensor_tensor(junk[:, u % 2, :], down_rows[u][:, :], 1.0, hn[:, j, :],
                                                     ALU.mult, ALU.mult,
                                                     accum_out=dots[:, j, bass.ds(slot, 1)]
                                                     ).then_inc(down_used, 1)

                for j, (has_down, has_up) in enumerate(steps):
                    if has_down and j + 1 < NT:
                        for part, (first, end) in zip(select.parts(j + 1), ((0, 1), (1, 3), (3, 5), (5, 7))):
                            dot_rounds(j, first, end)
                            part()
                        dot_rounds(j, 7, ROUNDS)
                    elif has_down:
                        dot_rounds(j, 0, ROUNDS)
                    if has_down:
                        select.finish(j)
                        dve.wait_ge(gelu_done, j + 1)
                        dve.tensor_tensor(coef[:, j, :], dots[:, j, :], gates[:, j, :], ALU.mult
                                          ).then_inc(coef_done, 1)
                    if has_up:
                        i = j - 1
                        dve.wait_ge(sum_done, i + 1)
                        dve.tensor_tensor(h[:, i, :], h[:, i, :], acc[:, i % 2, :], ALU.add).then_inc(added, 1)

            @block.scalar
            def _(act):
                act.sem_inc(diag_used, 4)
                act.wait_ge(landed, 16)

                def exponential(i):
                    act.wait_ge(select.top_ready, i + 1)
                    act.activation(select.top[:, i % 2, :, :], select.top[:, i % 2, :, :], ACT.Exp
                                   ).then_inc(select.exp_ready, 1)

                exponential(0)
                for j, (has_down, has_up) in enumerate(steps):
                    if has_up:
                        i = j - 1
                        act.wait_ge(coef_done, i + 1)
                        with act.Fori(0, ROUNDS) as r:
                            for u in range(RING):
                                slot = r * RING + u
                                act.wait_ge(diag_used, slot + (i * PEER_SLOTS + 1))
                                act.activation(diag[:, u % 4, :], ident[:, :], ACT.Copy,
                                               scale=coef[:, i, bass.ds(slot, 1)]).then_inc(diag_done, 1)
                    if has_down:
                        act.wait_ge(down_used, (j + 1) * PEER_SLOTS + RING)
                        act.activation(dots[:, j, :], dots[:, j, :], ACT.Gelu).then_inc(gelu_done, 1)
                    if j + 1 < NT:
                        exponential(j + 1)

            @block.tensor
            def _(pe):
                pe.wait_ge(ready, 1)
                for i in range(NT):
                    if i >= 2:
                        pe.wait_ge(added, i - 1)
                    for half in range(2):
                        pe.matmul(acc[:, i % 2, half * 512:(half + 1) * 512], zeros[:, 0:P], zeros[:, :],
                                  start=True, stop=False, skip_group_check=True)
                    with pe.Fori(0, ROUNDS) as r:
                        for u in range(RING):
                            slot = r * RING + u
                            pe.wait_ge(diag_done, slot + (i * PEER_SLOTS + 1))
                            pe.wait_ge(up_in[u], (r + (i * ROUNDS + 1)) * 16)
                            for half in range(2):
                                last = pe.matmul(acc[:, i % 2, half * 512:(half + 1) * 512], diag[:, u % 4, :],
                                                 up_rows[u][:, half * 512:(half + 1) * 512],
                                                 start=False, stop=False, skip_group_check=True)
                            last.then_inc(up_used, 1)
                            pe.wait_ge(up_used, slot + (i * PEER_SLOTS + RING + 1))
                            pe.sem_inc(diag_used, 1)
                    for half in range(2):
                        last = pe.matmul(acc[:, i % 2, half * 512:(half + 1) * 512], zeros[:, 0:P], zeros[:, :],
                                         start=False, stop=True, skip_group_check=True)
                    last.then_inc(sum_done, 1)


def second_block(nc, io, x, ident, out, dbg=None):
    w_in = io["w_in_2"][0].rearrange("(k p) c -> p k c", p=P)
    score_dram = nc.dram_tensor("scratch_score", [NT, P, 2 * PEER_HEADS * PEER_KEYS], F32).ap()
    acum_dram = nc.dram_tensor("scratch_acum", [SSD_HEADS, SEQ], F32).ap()

    def copy_jobs(tiles, width, dst):
        return [Job("token", 0, width, (lambda nc, ps, i=i: (nc.scalar.copy if i % 2 else nc.vector.tensor_copy)(
            dst(i), ps)), "act" if i % 2 else "dve", col=col, rows=rows) for i, rows, col in tiles]

    with Stage(nc, "b2") as st:
        cols = st.sb("cols", [P, COLS_2_N])
        load(nc, "load2", [(cols[:, :], io["p_cols_2"])])

        def gain(name):
            a, n = COLS_2[name]
            return cols[:, a:a + n]

        with Stage(nc, "branches") as br:
            uT = split_of(br, "uT", [P, KD, SEQ])
            normalise(nc, "norm3", x, SEQ_TILES, gain("mix_g"), ident, uT)

            def w_cols(first, width):
                return w_in[:, :, first:first + width]

            with own_semaphores(nc), Stage(nc, "ssdbuf") as s1:
                y = s1.sb("y", [P, NT, D])
                z = s1.sb("z", [P, NT, D])
                xbc = s1.sb("xbc", [P, XBC_TILES, SEQ + SSD_CONV - 1])
                dt_raw = s1.sb("dt_raw", [SSD_HEADS, SEQ])
                chunks = [(w_cols(OFF_XBC + n * 256, 256), uT, [
                    Job("channel", c * P, P, (lambda nc, ps, t=2 * n + c, eng=eng: (
                        nc.scalar.copy if eng == "act" else nc.vector.tensor_copy)(
                            xbc[:, t, SSD_CONV - 1:SSD_CONV - 1 + SEQ], ps)), eng)
                    for c, eng in enumerate(("act", "dve"))]) for n in range(XBC // 256)]
                chunks.append((w_cols(OFF_DT, SSD_HEADS), uT, [
                    Job("channel", 0, SSD_HEADS, lambda nc, ps: nc.vector.tensor_copy(dt_raw[:, :], ps), "dve")]))
                chunks += [(w_cols(n * 256, 256), uT, token_jobs(
                    SEQ_TILES, 256, lambda nc, i, r, ps, n=n: nc.scalar.activation(
                        z[:, i, n * 256:(n + 1) * 256], ps, ACT.Silu))) for n in range(D // 256)]
                project(nc, "proj_ssd", chunks)
                clear(nc, "clear_ssd", [xbc[:, :, 0:SSD_CONV - 1]])
                w0, b0 = COLS_2["conv_w"][0], COLS_2["conv_b"][0]
                conv_silu(nc, "ssc", xbc, XBC_TILES, SSD_CONV, SEQ,
                          lambda c, j: cols[:, w0 + c * SSD_CONV + j:w0 + c * SSD_CONV + j + 1],
                          lambda c: cols[:, b0 + c:b0 + c + 1], xbc)
                with Stage(nc, "ssdbuf2") as s2:
                    acum_rows = s2.sb("acum_rows", [P, SSD_HEADS, SEQ])
                    acum_col = s2.sb("acum_col", [P, NT, SSD_HEADS])
                    x_dt = s2.sb("x_dt", [P, NT, D])
                    ssd_prepare(nc, io, cols, dt_raw, xbc, ident, acum_rows, acum_col, y, x_dt, acum_dram)
                    ssd(nc, io, xbc, acum_rows, acum_col, x_dt, z, y)
                gain_row = s1.sb("gain_row", [P, D])
                load(nc, "load_ssd_g", [(gain_row[:, :], io["ssd_g_row"].partition_broadcast(P))])
                rms_groups(nc, "ssd_norm", [y[:, i, :] for i in range(NT)], SSD_GROUPS, D // SSD_GROUPS,
                           gain_row[:, :])
                if dbg: dbg("y_ssd", y[:, :, :])
                ssdT = br.sb("ssdT", [P, KD, SEQ], side="right")
                turn_rows(nc, "turn_ssd", y, SEQ_TILES, ident, ssdT)

            dilT = br.sb("dilT", [P, DIL_J * DIL_HD // P, SEQ])
            with own_semaphores(nc), Stage(nc, "dilbuf") as s1:
                qkv = s1.sb("qkv", [P, NT, 3 * DIL_W])
                project(nc, "proj_dil", [
                    (w_cols(OFF_DQ + n * 256, 256), uT,
                     copy_jobs(SEQ_TILES, 256, lambda i, n=n: qkv[:, i, n * 256:(n + 1) * 256]))
                    for n in range(3 * DIL_W // 256)])
                y = s1.sb("y", [P, NT, DIL_J * DIL_HD])
                qkT = s1.sb("qkT", [P, 2 * DIL_W // P, SEQ])
                q_gain = s1.sb("q_gain", [P, DIL_HD])
                k_gain = s1.sb("k_gain", [P, DIL_HD])
                mask = s1.sb("mask", [P, len(DIL), SEQ])
                load(nc, "load_dil", [(q_gain[:, :], io["dil_q_row"].partition_broadcast(P)),
                                      (k_gain[:, :], io["dil_k_row"].partition_broadcast(P)),
                                      (mask[:, :, :], io["c_dilated"])])
                rms_groups(nc, "norm_dq", [qkv[:, i, 0:DIL_W] for i in range(NT)], DIL_HEADS, DIL_HD, q_gain[:, :])
                rms_groups(nc, "norm_dk", [qkv[:, i, DIL_W:2 * DIL_W] for i in range(NT)], DIL_HEADS, DIL_HD,
                           k_gain[:, :])
                rope(nc, io, qkv[:, :, 0:2 * DIL_W].rearrange("p i (h e) -> p i h e", e=DIL_HD))
                turn_rows(nc, "turn_dil_q", qkv, SEQ_TILES, ident, qkT[:, 0:6, :], DIL_W // P)
                turn_rows(nc, "turn_dil_k", qkv[:, :, DIL_W:2 * DIL_W], SEQ_TILES, ident, qkT[:, 6:12, :],
                          DIL_W // P)
                units = []
                for i in range(NT):
                    w = (i + 1) * P
                    for j in range(DIL_J):
                        pieces = []
                        for g in range(len(DIL)):
                            head = g * DIL_J + j
                            a = (head % 2) * DIL_HD
                            pieces.append([(qkT[a:a + DIL_HD, head // 2, i * P:(i + 1) * P],
                                            qkT[a:a + DIL_HD, 6 + head // 2, 0:w])])
                        units.append((pieces, w, mask[:, :, SEQ - w:SEQ],
                                      (lambda g, n, j=j: qkv[:, n, 2 * DIL_W + (g * DIL_J + j) * DIL_HD:
                                                             2 * DIL_W + (g * DIL_J + j + 1) * DIL_HD]),
                                      y[:, i, j * DIL_HD:(j + 1) * DIL_HD]))
                attend(nc, "dil", units, ident, len(DIL), SEQ, float(DIL_HD) ** -0.5)
                if dbg: dbg("y_dil", y[:, :, :])
                turn_rows(nc, "turn_dil", y, SEQ_TILES, ident, dilT, DIL_J * DIL_HD // P)

            memT = br.sb("memT", [P, MEM_W // P, SEQ])
            with own_semaphores(nc), Stage(nc, "membuf") as s1:
                mem = s1.sb("mem", [P, N_MEM // P, D])
                mem_uT = split_of(s1, "mem_uT", [P, KD, N_MEM])
                mkv = s1.sb("mkv", [P, N_MEM // P, 2 * MEM_W])
                mq = s1.sb("mq", [P, NT, MEM_W])
                q_gain = s1.sb("q_gain", [P, MEM_HD])
                k_gain = s1.sb("k_gain", [P, MEM_HD])
                mem_tiles = [(i, P, P * i) for i in range(N_MEM // P)]
                load(nc, "load_mem", [(mem[:, :, :], io["mem_2"][0].rearrange("(i p) d -> p i d", p=P)),
                                      (q_gain[:, :], io["mem_q_row"].partition_broadcast(P)),
                                      (k_gain[:, :], io["mem_k_row"].partition_broadcast(P))])
                normalise(nc, "norm_mem", mem, mem_tiles, gain("mem_g"), ident, mem_uT)
                w_kv = io["w_mem_kv_2"][0].rearrange("(k p) c -> p k c", p=P)
                project(nc, "proj_mem", [
                    (w_kv[:, :, n * 256:(n + 1) * 256], mem_uT,
                     copy_jobs(mem_tiles, 256, lambda i, n=n: mkv[:, i, n * 256:(n + 1) * 256]))
                    for n in range(2 * MEM_W // 256)] + [
                    (w_cols(OFF_MQ + n * 256, 256), uT,
                     copy_jobs(SEQ_TILES, 256, lambda i, n=n: mq[:, i, n * 256:(n + 1) * 256]))
                    for n in range(MEM_W // 256)])
                y = s1.sb("y", [P, NT, MEM_W])
                mqT = s1.sb("mqT", [P, MEM_W // P, SEQ])
                mkT = s1.sb("mkT", [P, MEM_W // P, N_MEM])
                rms_groups(nc, "norm_mq", [mq[:, i, :] for i in range(NT)], HEADS, MEM_HD, q_gain[:, :])
                rms_groups(nc, "norm_mk", [mkv[:, i, 0:MEM_W] for i in range(N_MEM // P)], HEADS, MEM_HD,
                           k_gain[:, :])
                turn_rows(nc, "turn_mq", mq, SEQ_TILES, ident, mqT, MEM_W // P)
                turn_rows(nc, "turn_mk", mkv, mem_tiles, ident, mkT, MEM_W // P)

                def pieces_of(hd):
                    a, end = hd * MEM_HD, (hd + 1) * MEM_HD
                    while a < end:
                        b = min(end, (a // P + 1) * P)
                        yield a // P, a % P, b - a
                        a = b

                units = [([[(mqT[a:a + n, t, i * P:(i + 1) * P], mkT[a:a + n, t, :]) for t, a, n in pieces_of(hd)]],
                          N_MEM, None,
                          (lambda g, n, hd=hd: mkv[:, n, MEM_W + hd * MEM_HD:MEM_W + (hd + 1) * MEM_HD]),
                          y[:, i, hd * MEM_HD:(hd + 1) * MEM_HD]) for i in range(NT) for hd in range(HEADS)]
                attend(nc, "mem", units, ident, 1, N_MEM, float(MEM_HD) ** -0.5)
                if dbg: dbg("y_mem", y[:, :, :])
                turn_rows(nc, "turn_mem", y, SEQ_TILES, ident, memT, MEM_W // P)

            with own_semaphores(nc), Stage(nc, "mergebuf") as s1:
                merged = s1.sb("merged", [P, NT, D])
                gate = s1.sb("gate", [P, NT, 256])
                halfway = split_of(s1, "halfway", [P, KD, SEQ])
                gated = s1.sem("gated")
                n_gated = [0]

                def gated_product(nc, i, ps, cols, first):
                    if first:
                        return nc.vector.tensor_tensor(merged[:, i, cols], gate[:, i, :], ps, ALU.mult)
                    n_gated[0] += 1
                    nc.vector.tensor_tensor(gate[:, i, :], gate[:, i, :], ps, ALU.mult).then_inc(gated, 1)
                    nc.vector.wait_ge(gated, n_gated[0])
                    return nc.vector.tensor_tensor(merged[:, i, cols], merged[:, i, cols], gate[:, i, :], ALU.add)

                def branch(name, branches):
                    chunks = []
                    for b, wt, k0, nk in branches:
                        wb = io[wt][0].rearrange("(k p) c -> p k c", p=P)
                        rows = tuple(buf[:, k0:k0 + nk, :] for buf in halfway)
                        for n in range(D // 256):
                            cols = slice(n * 256, (n + 1) * 256)
                            chunks.append((w_cols(OFF_GATE + b * D + n * 256, 256), uT, token_jobs(
                                SEQ_TILES, 256, lambda nc, i, r, ps: nc.scalar.activation(
                                    gate[:, i, :], ps, ACT.Sigmoid))))
                            jobs = token_jobs(SEQ_TILES, 256, lambda nc, i, r, ps, b=b, cols=cols: gated_product(
                                nc, i, ps, cols, b == 0), "dve")
                            for i, job in enumerate(jobs):
                                job.after = (len(chunks) - 1) * NT + i
                            chunks.append((wb[:, :, cols], rows, jobs))
                    project(nc, name, chunks)

                mem_k, dil_k = MEM_W // P, DIL_J * DIL_HD // P
                split_buffers(nc, "split_ssd", [(ssdT[:, :, :], tuple(buf[:, :, :] for buf in halfway))])
                branch("merge_ssd", [(0, "w_ssd_br_2", 0, KD)])
                split_buffers(nc, "split_att", [
                    (dilT[:, :, :], tuple(buf[:, 0:dil_k, :] for buf in halfway)),
                    (memT[:, :, :], tuple(buf[:, dil_k:dil_k + mem_k, :] for buf in halfway))])
                branch("merge_att", [(1, "w_dil_br_2", 0, dil_k), (2, "w_mem_br_2", dil_k, mem_k)])
                turn_rows(nc, "turn_merged", merged, SEQ_TILES, ident, uT)
                project(nc, "proj_out2", added_chunks(io["w_out_2"][0].rearrange("(k p) c -> p k c", p=P), uT, x,
                                                      SEQ_TILES))
        if dbg: dbg("hmix2", x[:, 0:NT, :])

        with Stage(nc, "peerbuf") as s1:
            hn = s1.sb("hn", [P, NT, D])
            with Stage(nc, "selbuf") as s2:
                hnT = split_of(s2, "hnT", [P, KD, SEQ])
                gain_row = s2.sb("gain_row", [P, D])
                qT = s2.sb("qT", [P, 2 * PEER_HEADS, SEQ])
                load(nc, "load_peer_g", [(gain_row[:, :], io["ffn_g_row_2"].partition_broadcast(P))])
                normalise(nc, "norm4", x, SEQ_TILES, None, ident, hnT, gain_row=gain_row, kept=hn)
                w_q = io["peer_w_query_2"][0].rearrange("(k p) c -> p k c", p=P)
                project(nc, "proj_query", [(w_q[:, :, n * 256:(n + 1) * 256], hnT, [
                    Job("channel", c * P, P, (lambda nc, ps, t=2 * n + c, eng=eng: (
                        nc.scalar.copy if eng == "act" else nc.vector.tensor_copy)(qT[:, t, :], ps)), eng)
                    for c, eng in enumerate(("act", "dve"))]) for n in range(8)])
                peer_scores(nc, io, qT, score_dram)
            peer_experts(nc, io, hn, x, score_dram, out)


def two_blocks(nc, io, out):
    with Stage(nc, "top") as st:
        h = st.sb("h", [P, NT + 1, D])
        ident = st.sb("ident", [P, P])
        with own_semaphores(nc):
            first_block(nc, io, h, ident)
        with Stage(nc, "between") as s1:
            gain_row = s1.sb("gain_row", [P, D])
            load(nc, "load_final_g", [(gain_row[:, :], io["final_g_row"].partition_broadcast(P))])
            normalise(nc, "norm_final", h, SEQ_TILES, None, ident, None, gain_row=gain_row, kept=h)
        second_block(nc, io, h, ident, out)


def constants():
    import numpy as np

    f = np.float32
    half = P // 2
    inv = (f(10000.0) ** (-np.arange(half, dtype=f) / f(half))).astype(f)
    ang = np.arange(TOK, dtype=f)[None, :] * inv[:, None]
    x = np.arange(REL_W)[None, :] - REL_BASE - np.arange(P)[:, None]
    p, c = np.arange(P)[:, None], np.arange(P)[None, :]
    back = p + SEQ - P - np.arange(SEQ)[None, :]
    dilated = np.stack([np.where((back >= 0) & (back <= window) & (back % step == 0), 0.0, NEG)
                        for window, step in DIL], 1)
    inv2 = np.exp(f(-np.log(500000.0) * (2.0 / ROT)) * np.arange(ROT_HALF, dtype=f)).astype(f)
    token_id = np.zeros((P, NT + 1), f)
    for i, rows, col in ALL_TILES:
        token_id[:, i] = col + np.arange(P)
    return {
        "c_ident": np.eye(P, dtype=f),
        "c_cos": np.concatenate([np.cos(ang)] * 2).astype(f),
        "c_sin": np.concatenate([-np.sin(ang), np.sin(ang)]).astype(f),
        "c_ahead": np.maximum(x, 0).astype(f),
        "c_behind": np.maximum(-x, 0).astype(f),
        "c_diag": (1.0 + (x == 0)).astype(f),
        "c_keep": np.stack([c >= p, c <= p], 1).astype(f),
        "c_token_id": token_id,
        "c_dilated": dilated.astype(f),
        "c_inv": inv2[None, :],
        "c_iota16": np.arange(PEER_TOP, dtype=f)[None, :],
        "c_ids": (META + np.arange(SEQ, dtype=f))[None, :],
    }


def channel_columns(v):
    return v.reshape((-1, P) + v.shape[1:]).swapaxes(0, 1)


def layouts(inputs):
    import numpy as np

    cat = np.concatenate
    conv = channel_columns(inputs["conv_w"][0].T)
    gate_b = np.zeros((P, 4), np.float32)
    gate_b[:HEADS] = inputs["b_gates"][0].reshape(4, HEADS).T
    heads = np.zeros((P, 2), np.float32)
    heads[:SSD_HEADS, 0] = inputs["ssd_dt_bias_2"][0]
    heads[:SSD_HEADS, 1] = inputs["ssd_a_log_2"][0]
    return {
        "p_cols_2": np.ascontiguousarray(cat([
            channel_columns(inputs["norm_mix_w_2"][0]), channel_columns(inputs["mem_norm_w_2"][0]),
            channel_columns(inputs["ssd_conv_w_2"][0].T).reshape(P, -1), channel_columns(inputs["ssd_conv_b_2"][0]),
            heads], axis=1)),
        "positions": np.ascontiguousarray(inputs["positions_2"][0].reshape(NT, P).T),
        "sub_keys": np.ascontiguousarray(inputs["peer_sub_keys_2"][0].reshape(-1, PEER_KEYS, P).transpose(2, 0, 1)),
        "ssd_d_row": inputs["ssd_d_2"], "ssd_g_row": inputs["ssd_norm_w_2"], "dil_q_row": inputs["dil_q_norm_w_2"],
        "dil_k_row": inputs["dil_k_norm_w_2"], "mem_q_row": inputs["mem_q_norm_w_2"],
        "mem_k_row": inputs["mem_k_norm_w_2"], "ffn_g_row_2": inputs["norm_ffn_w_2"],
        "final_g_row": inputs["final_norm_g"].reshape(1, D),
        **{k: inputs[k] for k in ("mem_2", "w_in_2", "w_mem_kv_2", "w_ssd_br_2", "w_dil_br_2", "w_mem_br_2",
                                  "w_out_2", "peer_w_query_2", "peer_down_2", "peer_up_2")},
        "p_cols_1": np.ascontiguousarray(cat([
            channel_columns(inputs["mix_norm_g"][0]), channel_columns(inputs["ffn_norm_g"][0]),
            conv.reshape(P, -1), channel_columns(inputs["conv_b"][0]), gate_b], axis=1)),
        "decay_logit": inputs["ret_decay_logit"][0].reshape(1, 8),
        "ret_gn_row": inputs["ret_gn_g"], "mlstm_gn_row": inputs["mlstm_gn_g"], "ffn_g_row": inputs["ffn_norm_g"],
        **{k: inputs[k] for k in ("x", "meta_tokens", "w_in", "w_out", "w_router", "w_gate", "w_up", "w_down")},
    }


def kernel(**inputs):
    import concourse.bacc as bacc
    import numpy as np
    from concourse.bass_utils import run_bass_kernel_spmd

    nc = bacc.Bacc("TRN2", target_bir_lowering=False, num_devices=1)
    arrays, io = {}, {}
    for name, a in {**constants(), **layouts({k: np.asarray(v) for k, v in inputs.items()})}.items():
        arrays[f"in_{name}"] = np.ascontiguousarray(a)
        io[name] = nc.dram_tensor(f"in_{name}", a.shape, mybir.dt.from_np(a.dtype), kind="ExternalInput").ap()
    out = nc.dram_tensor("result", (1, SEQ, D), F32, kind="ExternalOutput").ap()
    two_blocks(nc, io, out[0])
    done = run_bass_kernel_spmd(nc, [arrays], core_ids=[0])
    return done.results[0]["result"]
```
